# Optimizing a Trainium2 kernel written in Bass

```python
import jax, jax.numpy as jnp
from jax import lax
import numpy as np

D_MODEL = 1024
BATCH = 1
SEQ = 512
DEPTH = 2
DEC_BATCH = 8
DEC_SEQ = 1
PAST_LEN = 4096
PAGE_SIZE = 128

N_MIXERS = 4
W_GROUP = D_MODEL // N_MIXERS
CONV_A = 3
CHUNK = 128
N_HEADS_B = 4
HEAD_B = W_GROUP // N_HEADS_B
CONV_C = 31
POOL_WINDOWS = (2, 4, 8, 16)
POOL_MAX = 16
N_POOL_GROUPS = 4
GROUP_D = W_GROUP // N_POOL_GROUPS
IN_COLS = 3 * W_GROUP + 2 * W_GROUP + 2 * W_GROUP + W_GROUP
D_FF = 2816
N_EXPERTS = 8
TOP_K = 2
D_FF_E = 1408
N_DENSE = (DEPTH + 1) // 2
N_MOE = DEPTH // 2
EPS = 1e-6

kernel_name = 'hybrid_conv_gmlp_conformer_pool_decoder_step'

def rmsnorm(x, g):
    xf = x.astype(jnp.float32)
    y = xf * lax.rsqrt(jnp.mean(xf * xf, axis=-1, keepdims=True) + EPS)
    return (y * g.astype(jnp.float32)).astype(x.dtype)

def layernorm(x, g, b):
    xf = x.astype(jnp.float32)
    xc = xf - jnp.mean(xf, axis=-1, keepdims=True)
    var = jnp.mean(xc * xc, axis=-1, keepdims=True)
    y = xc * lax.rsqrt(var + EPS) * g.astype(jnp.float32) + b.astype(jnp.float32)
    return y.astype(x.dtype)

def causal_dwconv(x, buf, w):
    width = w.shape[0]
    xp = jnp.concatenate([buf.astype(x.dtype), x], axis=1)
    y = lax.conv_general_dilated(xp, w[:, None, :].astype(x.dtype), window_strides=(1,),
                                 padding='VALID', dimension_numbers=('NWC', 'WIO', 'NWC'),
                                 feature_group_count=x.shape[-1])
    return y, xp[:, xp.shape[1] - (width - 1):]

def chunk_spatial_mix(v, w_s, b_s):
    n_b, length, _ = v.shape
    n_chunks = -(-length // CHUNK)
    pad = n_chunks * CHUNK - length
    vp = jnp.pad(v, ((0, 0), (0, pad), (0, 0))).reshape(n_b, n_chunks, CHUNK, N_HEADS_B, HEAD_B)
    causal = jnp.tril(jnp.ones((CHUNK, CHUNK), dtype=bool))
    w_masked = jnp.where(causal[None], w_s, jnp.zeros_like(w_s)).astype(v.dtype)
    mixed = jnp.einsum('hts,bnshd->bnthd', w_masked, vp)
    mixed = mixed + jnp.swapaxes(b_s, 0, 1).astype(v.dtype)[None, None, :, :, None]
    return mixed.reshape(n_b, n_chunks * CHUNK, W_GROUP)[:, :length]

def causal_multiscale_pool(p_in, buf, start_pos):
    length = p_in.shape[1]
    pcat = jnp.concatenate([buf.astype(p_in.dtype), p_in], axis=1)
    cs = jnp.cumsum(pcat.astype(jnp.float32), axis=1)
    cs = jnp.pad(cs, ((0, 0), (1, 0), (0, 0)))
    pos = start_pos + jnp.arange(length)
    means = []
    for gi, win in enumerate(POOL_WINDOWS):
        sl = slice(gi * GROUP_D, (gi + 1) * GROUP_D)
        s = cs[:, POOL_MAX:POOL_MAX + length, sl] - cs[:, POOL_MAX - win:POOL_MAX - win + length, sl]
        cnt = jnp.minimum(pos + 1, win).astype(jnp.float32)[None, :, None]
        means.append(s / cnt)
    mean = jnp.concatenate(means, axis=-1)
    pooled = (mean - p_in.astype(jnp.float32)).astype(p_in.dtype)
    return pooled, pcat[:, pcat.shape[1] - (POOL_MAX - 1):]

def swiglu(h, w1, w3, w2):
    return (jax.nn.silu(h @ w1) * (h @ w3)) @ w2

def moe_swiglu(h, w_router, b_router, w1, w3, w2):
    logits = h.astype(jnp.float32) @ w_router.astype(jnp.float32) + b_router.astype(jnp.float32)
    top_v, top_i = lax.top_k(logits, TOP_K)
    gates = jax.nn.softmax(top_v, axis=-1)
    comb = jnp.sum(jax.nn.one_hot(top_i, N_EXPERTS, dtype=jnp.float32) * gates[..., None], axis=-2)
    comb = comb.astype(h.dtype)
    y = jnp.zeros_like(h)
    for e in range(N_EXPERTS):
        y = y + comb[..., e:e + 1] * swiglu(h, w1[e], w3[e], w2[e])
    return y

def token_mixers(h, buf_a, buf_c, buf_d, start_pos, l, p):
    n_b, length, _ = h.shape
    proj = h @ p['w_in'][l]
    a_b, a_c, a_h, b_u, b_v, c_a, c_g, d_p = jnp.split(proj, 8, axis=-1)
    y_a, nb_a = causal_dwconv(a_c * a_h, buf_a, p['conv_a_w'][l])
    out_a = a_b * y_a
    v_n = layernorm(b_v, p['ln_v_g'][l], p['ln_v_b'][l])
    out_b = b_u * chunk_spatial_mix(v_n, p['w_s'][l], p['b_s'][l])
    glu = c_a * jax.nn.sigmoid(c_g)
    y_c, nb_c = causal_dwconv(glu, buf_c, p['conv_c_w'][l])
    out_c = jax.nn.silu(layernorm(y_c + p['conv_c_b'][l], p['ln_c_g'][l], p['ln_c_b'][l]))
    pooled, nb_d = causal_multiscale_pool(d_p, buf_d, start_pos)
    out_d = jnp.einsum('blgc,gcd->blgd', pooled.reshape(n_b, length, N_POOL_GROUPS, GROUP_D),
                       p['pool_w'][l]).reshape(n_b, length, W_GROUP) * p['pool_scale'][l]
    groups = jnp.stack([out_a, out_b, out_c, out_d], axis=2)
    merged = rmsnorm(groups, p['g_out'][l]).reshape(n_b, length, D_MODEL)
    return merged @ p['w_out'][l], nb_a, nb_c, nb_d, v_n

def trunk(x, c, buf_a, buf_c, buf_d, start_pos, p):
    length = x.shape[1]
    keep_from = CHUNK * ((length - 1) // CHUNK)
    new_a, new_c, new_d, new_v = [], [], [], []
    for l in range(DEPTH):
        mod = (jax.nn.silu(c) @ p['w_ada'][l] + p['b_ada'][l])[:, None, :]
        shift1, scale1, gate1, shift2, scale2, gate2 = jnp.split(mod, 6, axis=-1)
        h = rmsnorm(x, p['g_mix'][l]) * (1 + scale1) + shift1
        mix, nb_a, nb_c, nb_d, v_n = token_mixers(h, buf_a[l], buf_c[l], buf_d[l], start_pos, l, p)
        x = x + gate1 * mix
        h = rmsnorm(x, p['g_ffn'][l]) * (1 + scale2) + shift2
        i = l // 2
        if l % 2 == 0:
            f = swiglu(h, p['w1_dense'][i], p['w3_dense'][i], p['w2_dense'][i])
        else:
            f = moe_swiglu(h, p['w_router'][i], p['b_router'][i],
                           p['w1_moe'][i], p['w3_moe'][i], p['w2_moe'][i])
        x = x + gate2 * f
        new_a.append(nb_a)
        new_c.append(nb_c)
        new_d.append(nb_d)
        new_v.append(v_n[:, keep_from:])
    y = rmsnorm(x, p['g_final'])
    return y, jnp.stack(new_a), jnp.stack(new_c), jnp.stack(new_d), jnp.stack(new_v)

def setup_inputs(seed: int = 0) -> dict:
    key = jax.random.key(seed)
    ks = iter(jax.random.split(key, 64))

    def nrm(shape, s):
        return jax.random.normal(next(ks), shape, jnp.float32) * s

    def gain(shape):
        return 1.0 + 0.1 * jax.random.normal(next(ks), shape, jnp.float32)

    d = D_MODEL
    return {
        'x_prompt': nrm((BATCH, SEQ, d), 1.0),
        'x_sample': nrm((DEC_BATCH, DEC_SEQ, d), 1.0),
        'state_conv_a': nrm((DEPTH, DEC_BATCH, CONV_A - 1, W_GROUP), 1.0),
        'state_conv_c': nrm((DEPTH, DEC_BATCH, CONV_C - 1, W_GROUP), 0.5),
        'state_pool_d': nrm((DEPTH, DEC_BATCH, POOL_MAX - 1, W_GROUP), 1.0),
        'c_prompt': nrm((BATCH, d), 1.0),
        'c_sample': nrm((DEC_BATCH, d), 1.0),
        'w_ada': nrm((DEPTH, d, 6 * d), 0.5 * d ** -0.5),
        'b_ada': nrm((DEPTH, 6 * d), 0.02),
        'g_mix': gain((DEPTH, d)),
        'w_in': nrm((DEPTH, d, IN_COLS), d ** -0.5),
        'conv_a_w': nrm((DEPTH, CONV_A, W_GROUP), CONV_A ** -0.5),
        'ln_v_g': gain((DEPTH, W_GROUP)),
        'ln_v_b': nrm((DEPTH, W_GROUP), 0.02),
        'w_s': nrm((DEPTH, N_HEADS_B, CHUNK, CHUNK), CHUNK ** -0.5),
        'b_s': gain((DEPTH, N_HEADS_B, CHUNK)),
        'conv_c_w': nrm((DEPTH, CONV_C, W_GROUP), CONV_C ** -0.5),
        'conv_c_b': nrm((DEPTH, W_GROUP), 0.02),
        'ln_c_g': gain((DEPTH, W_GROUP)),
        'ln_c_b': nrm((DEPTH, W_GROUP), 0.02),
        'pool_w': nrm((DEPTH, N_POOL_GROUPS, GROUP_D, GROUP_D), GROUP_D ** -0.5),
        'pool_scale': gain((DEPTH, W_GROUP)),
        'g_out': gain((DEPTH, N_MIXERS, W_GROUP)),
        'w_out': nrm((DEPTH, d, d), d ** -0.5),
        'g_ffn': gain((DEPTH, d)),
        'w1_dense': nrm((N_DENSE, d, D_FF), d ** -0.5),
        'w3_dense': nrm((N_DENSE, d, D_FF), d ** -0.5),
        'w2_dense': nrm((N_DENSE, D_FF, d), D_FF ** -0.5),
        'w_router': nrm((N_MOE, d, N_EXPERTS), d ** -0.5),
        'b_router': nrm((N_MOE, N_EXPERTS), 0.01),
        'w1_moe': nrm((N_MOE, N_EXPERTS, d, D_FF_E), d ** -0.5),
        'w3_moe': nrm((N_MOE, N_EXPERTS, d, D_FF_E), d ** -0.5),
        'w2_moe': nrm((N_MOE, N_EXPERTS, D_FF_E, d), D_FF_E ** -0.5),
        'g_final': gain((d,)),
    }

def reference(x_prompt, x_sample, state_conv_a, state_conv_c, state_pool_d, c_prompt, c_sample,
              w_ada, b_ada, g_mix, w_in, conv_a_w, ln_v_g, ln_v_b, w_s, b_s, conv_c_w, conv_c_b,
              ln_c_g, ln_c_b, pool_w, pool_scale, g_out, w_out, g_ffn, w1_dense, w3_dense, w2_dense,
              w_router, b_router, w1_moe, w3_moe, w2_moe, g_final):
    p = dict(w_ada=w_ada, b_ada=b_ada, g_mix=g_mix, w_in=w_in, conv_a_w=conv_a_w,
             ln_v_g=ln_v_g, ln_v_b=ln_v_b, w_s=w_s, b_s=b_s, conv_c_w=conv_c_w, conv_c_b=conv_c_b,
             ln_c_g=ln_c_g, ln_c_b=ln_c_b, pool_w=pool_w, pool_scale=pool_scale, g_out=g_out,
             w_out=w_out, g_ffn=g_ffn, w1_dense=w1_dense, w3_dense=w3_dense, w2_dense=w2_dense,
             w_router=w_router, b_router=b_router, w1_moe=w1_moe, w3_moe=w3_moe, w2_moe=w2_moe,
             g_final=g_final)
    n_p = x_prompt.shape[0]
    zeros_a = jnp.zeros((DEPTH, n_p, CONV_A - 1, W_GROUP), x_prompt.dtype)
    zeros_c = jnp.zeros((DEPTH, n_p, CONV_C - 1, W_GROUP), x_prompt.dtype)
    zeros_d = jnp.zeros((DEPTH, n_p, POOL_MAX - 1, W_GROUP), x_prompt.dtype)
    y_prompt, a_p, c_p, d_p, v_p = trunk(x_prompt, c_prompt, zeros_a, zeros_c, zeros_d, 0, p)
    y_sample, a_s, c_s, d_s, v_s = trunk(x_sample, c_sample, state_conv_a, state_conv_c,
                                         state_pool_d, PAST_LEN, p)
    return (y_prompt, y_sample, a_p, c_p, d_p, v_p, a_s, c_s, d_s, v_s)


_drawn_inputs = setup_inputs


def setup_inputs(seed=0):
    import zlib

    import numpy as np

    out = dict(_drawn_inputs(seed))
    spreads = {}
    factors = {'ln_v_b': 2.89, 'b_s': 2.788, 'conv_c_b': 5.183, 'ln_c_b': 7.118, 'b_router': 6.547}
    for name, (base, spread) in spreads.items():
        noise = np.random.default_rng([zlib.crc32(name.encode()), seed]).standard_normal(out[name].shape)
        drawn = base * np.exp(spread * noise) if base else spread * noise
        out[name] = __import__('jax').numpy.asarray(drawn.astype(out[name].dtype))
    for name, factor in factors.items():
        out[name] = (out[name] * factor).astype(out[name].dtype)
    return out
```

```python
from contextlib import ExitStack

import concourse.bass as bass
from concourse import mybir

F32 = mybir.dt.float32
I32 = mybir.dt.int32
U32 = mybir.dt.uint32
ALU = mybir.AluOpType
ACT = mybir.ActivationFunctionType
AX = mybir.AxisListType

P = 128
D = 1024
KD = D // P
SEQ = 512
NS = 8
T = SEQ + NS
HT = T // 2
NQ = 1 + NS
DEPTH = 2
W = 256
TAPS_A, TAPS_C, POOL = 3, 31, 16
FF = 2816
FE = 1408
NE = 8
EPS = 1e-6
RING = 6
SLOT = KD * 384
NT = (T + P - 1) // P
AT = [0, 128, 256, 384, T - P]
PICKS = 2 * T
ROOM = PICKS + T
NW = 2 * P
WIDTHS = [128, 144, 160, 192, 224, NW]

A_B, A_C, A_H, B_U, B_V, C_A, C_G, D_P = range(8)
ORDER = [C_G, C_A, B_V, D_P, A_H, A_C, B_U, A_B]
HOME = {C_G: 0, B_V: 2, A_H: 4, B_U: 6, A_B: 8}

ROWS, _at = {}, 0
for _name, _n in [("g_mix", 8), ("ln_v_g", 2), ("ln_v_b", 2), ("conv_c_b", 2), ("ln_c_g", 2), ("ln_c_b", 2),
                  ("pool_scale", 2), ("g_out", 8), ("g_ffn", 8), ("conv_a_w", 2 * TAPS_A), ("conv_c_w", 2 * TAPS_C),
                  ("g_final", 8)]:
    ROWS[_name] = (_at, _n)
    _at += _n
NROWS = _at

TAIL = [TAPS_A - 1, TAPS_C - 1, POOL - 1, NS, NS, NS, NS]

SHIFT1, SCALE1, GATE1, SHIFT2, SCALE2, GATE2 = range(6)

ADA0 = 0
WIN0 = ADA0 + 24 * DEPTH
WOUT0 = WIN0 + 8
DENSE = WOUT0 + 4
DENSE2 = DENSE + 16
WIN1 = DENSE2 + 8
WOUT1 = WIN1 + 8
MOE = WOUT1 + 4
PER_E = 12
FT = FF // P
ET = FE // P


def trunk_program(nc, A, O):
    ctx = ExitStack()
    with ctx:
        def sb(name, shape, dt=F32):
            return ctx.enter_context(nc.sbuf_tensor(name, shape, dt))

        def sem(name):
            return ctx.enter_context(nc.semaphore(name))

        ring = sb("ring", [P, RING, SLOT])
        xT = sb("xT", [P, KD, T])
        hT = sb("hT", [P, KD, T])
        work = sb("work", [P, KD, T])
        big = sb("big", [P, 11440])
        stage = sb("stage", [P, 3, D])
        vec = sb("vec", [P, DEPTH, NROWS])
        bada = sb("bada", [P, DEPTH * 48])
        mod = sb("mod", [P, DEPTH, 48, NQ])
        cT = sb("cT", [P, KD, NQ])
        ident = sb("ident", [P, P])
        ones = sb("ones", [P, P])
        eps = sb("eps", [P, 1])
        wrt = sb("wrt", [P, KD, NE])
        brt = sb("brt", [NE, 1])
        win = sb("win", [P, 2])
        winv = sb("winv", [P, 2])
        cinv = sb("cinv", [P, 2, POOL])
        flat = stage[:, :, :].rearrange("p a n -> p (a n)")

        def cut(src, at, *shape):
            n = 1
            for s in shape:
                n *= s
            v = src[:, at:at + n]
            if len(shape) == 2:
                v = v.rearrange("p (a b) -> p a b", a=shape[0])
            if len(shape) == 3:
                v = v.rearrange("p (a b c) -> p a b c", a=shape[0], b=shape[1])
            return v

        ws_raw = cut(flat, 0, 4, P)
        bsb = cut(flat, 512, 2, P)
        bd = cut(flat, 768, 2, P)
        stA = cut(flat, 1024, W)
        stC = cut(flat, 1280, 2, W)
        stD = cut(flat, 1792, W)
        wsT = cut(flat, 2048, 4, P)
        ws00 = sb("ws00", [P, 2])
        hisA = sb("hisA", [P, 2, NS, TAPS_A])
        hisC = sb("hisC", [P, 2, NS, TAPS_C])
        hisD = sb("hisD", [P, 2, NS, POOL])
        head16 = sb("head16", [P, 2, POOL])
        tapC = sb("tapC", [P, NS, TAPS_C])
        small = sb("small", [P, 2, NS])
        stat = sb("stat", [P, T])
        stat2 = sb("stat2", [P, T])
        lg = sb("lg", [P, NT, NE])
        vmax = sb("vmax", [P, NT, 8])
        imax = sb("imax", [P, NT, 8], U32)
        imf = sb("imf", [P, NT, 8])
        pick = sb("pick", [P, 2, NT, NE])
        mask = sb("mask", [P, NT, NE])
        before = sb("before", [P, NT, NE])
        totals = sb("totals", [P, NT, NE])
        tri = sb("tri", [P, P])
        eidx = sb("eidx", [P, NE])
        ebase = sb("ebase", [P, NE])
        valid = sb("valid", [P, NT])
        placef = sb("placef", [P, 2, NT])
        place = sb("place", [P, 2, NT], U32)
        gate = sb("gate", [P, 2, NT])
        countf = sb("countf", [P, NE])
        count = sb("count", [P, NE], I32)
        first = sb("first", [P, NE], I32)
        modrow = sb("modrow", [NQ, 2, 256])

        xin = cut(big, 0, NT, D)
        rows = cut(big, 5 * D, 4, P)
        crow = cut(big, 5 * D + 4 * P, D)
        proj = cut(big, 0, 10, T)
        zin = cut(big, 10 * T, 2, TAPS_A - 1 + T)
        gin = cut(big, 10 * T + 2 * (2 + T), 2, TAPS_C - 1 + T)
        pin = cut(big, 10 * T + 2 * (32 + 2 * T), 2, POOL - 1 + T)
        DAT = 10 * T + 2 * (47 + 3 * T)
        pa = cut(big, DAT, 2, POOL - 1 + T)
        pb = cut(big, DAT + 2 * (15 + T), 2, POOL - 1 + T)
        outrow = cut(big, DAT, 7, W)
        vtok = cut(big, HOME[A_H] * T, 4, W)
        G = cut(big, 0, 22, T)
        hexp = cut(big, 11 * T, KD, T)
        hact = cut(big, 19 * T, 2, T)
        Gn = cut(big, 0, ET, NW)
        hn = cut(big, 11 * T, KD, NW)
        hactn = cut(big, 19 * T, 2, NW)
        wflat = work[:, :, :].rearrange("p k n -> p (k n)")
        yn = cut(wflat, 0, KD, NW)
        yrow = cut(wflat, KD * NW, 2, D)
        outs = work
        lgT = stat2[0:NE]

        PP = [ctx.enter_context(nc.psum_tensor(f"PP{q}", [P, 2, 512], F32)) for q in range(4)]

        Hd = nc.dram_tensor("h_by_expert", (ROOM, D), F32).ap()
        Yd = nc.dram_tensor("y_by_expert", (ROOM, D), F32).ap()

        def v_(name, l, j):
            return vec[:, l, ROWS[name][0] + j:ROWS[name][0] + j + 1]

        def tail_bank(n):
            return PP[3 - n // 4][:, n % 4 // 2, (n % 2) * W:(n % 2) * W + W]

        def pp(q, n=HT):
            return PP[q][:, :, 0:n]

        def two(ap):
            return ap.rearrange("p (h n) -> p h n", h=2)

        full = [sem(f"slot_full{s}") for s in range(RING)]
        const_ready = sem("const_ready")
        const_dve = sem("const_dve")
        x_in = sem("x_in")
        vec_in = sem("vec_in")
        c_in = sem("c_in")
        wr_in = sem("wr_in")
        silu_c = sem("silu_c")
        pro_tr = sem("pro_tr")
        pro_act = sem("pro_act")
        pro_dve = sem("pro_dve")
        ada_mm = sem("ada_mm")
        ada_row = sem("ada_row")
        ada_tr = sem("ada_tr")
        ada_out = sem("ada_out")
        mod_ready = sem("mod_ready")
        dchain = sem("dve_order")
        achain = sem("act_order")
        gchain = sem("pool_order")
        stored = sem("stored")
        STEPS = {"mx_in": 256, "ws_tr": 1, "ws_copy": 1, "ws_masked": 1, "st_tr": 1, "st_copy": 3, "hist_zero": 1,
                 "pj_done": 16, "pj_free0": 8, "pj_free1": 8, "conv_tap": 2 * TAPS_C, "lnc_in": 1, "vxc": 2, "lnc_xc": 2,
                 "lnb_sum": 1, "lnb_sq": 2, "lnb_var": 1, "lnb_root": 1, "lnc_sum": 1, "lnc_sq": 2, "lnc_var": 1,
                 "lnc_root": 1, "lnc_hat": 2, "pool_out": 1, "pooled": 1, "pool_mm": 2, "pool_free": 1, "vn_ready": 2,
                 "vt_tr": 1, "vt_copy": 1, "mix_done": 1, "mix_read": 1, "gA": 2, "gB": 2, "gC": 2, "gD": 2,
                 "g_sq": 8, "g_sum": 4, "g_root": 4, "merged": 8, "po_done": 8, "po_free": 8, "x1_ready": 1,
                 "x2_ready": 1, "tail_tr": 7, "tail_copy": 7, "tail_out": 128}
        s = {name: sem(name) for name in STEPS}

        def step(l, name, n):
            return s[name], STEPS[name] * l + n

        NORM_STEPS = {"sq": KD, "sum": 1, "root": 1, "xhat": KD, "h": 1}
        ns = {k: sem(f"norm_{k}") for k in NORM_STEPS}

        def norm_step(tag, k, n):
            return ns[k], NORM_STEPS[k] * tag + n

        ff_done, ff_act, ff_free = sem("ff_done"), sem("ff_act"), sem("ff_free")
        fy_done, fy_free = sem("fy_done"), sem("fy_free")
        R = {k: sem(f"moe_{k}") for k in ["lg", "lg_ev", "lg_tr", "idx", "mask", "pre", "route", "gate",
                                          "zero", "h_tr", "h_row", "h_in", "in_tr", "in_ev",
                                          "f_done", "f_act", "f_free", "y_done", "y_free", "yt_tr", "yt_ev",
                                          "y_out", "f_row", "count", "fo_tr", "fo_ev", "exp_d", "const", "x_ready"]}
        Rout = [sem(f"moe_rows_out{s}") for s in range(3)]
        Rwide = [sem(f"moe_wide_in{t}") for t in range(2, NT)]
        Rin = [sem(f"moe_in{s}") for s in range(2)]
        Rback = [sem(f"moe_back{r}") for r in range(2)]
        fin_tr, fin_ev, fin_out = sem("fin_tr"), sem("fin_ev"), sem("fin_out")

        def slot(n, k, cols):
            return ring[:, n % RING, 0:k * cols].rearrange("p (k n) -> p k n", k=k)

        def tokens_of(eng, e):
            return eng.value_load(count[0:1, bass.ds(e, 1)], min_val=0, max_val=T)

        def first_of(eng, e):
            return eng.value_load(first[0:1, bass.ds(e, 1)], min_val=0, max_val=PICKS)

        w_in_v = [A["w_in"][l].rearrange("(k p) (b n) -> b p k n", p=P, n=256) for l in range(DEPTH)]
        w_out_v = [A["w_out"][l].rearrange("(k p) (b n) -> b p k n", p=P, n=256) for l in range(DEPTH)]
        w_ada_v = [A["w_ada"][l].rearrange("(k p) (b n) -> b p k n", p=P, n=256) for l in range(DEPTH)]
        w1_v = A["w1_dense"][0].rearrange("(k p) n -> p k n", p=P)
        w3_v = A["w3_dense"][0].rearrange("(k p) n -> p k n", p=P)
        w2_v = A["w2_dense"][0].rearrange("(g k p) (b n) -> b g p k n", g=2, p=P, n=256)

        def expert_chunk(e, j):
            if j < 8:
                w = A["w1_moe" if j % 2 == 0 else "w3_moe"][0]
                n = P * min(3, ET - 3 * (j // 2))
                return w[e].rearrange("(k p) n -> p k n", p=P)[:, :, (j // 2) * 384:(j // 2) * 384 + n], KD, n
            return A["w2_moe"][0][e].rearrange("(k p) n -> p k n", p=P)[:, :, (j - 8) * 256:(j - 7) * 256], ET, 256

        def chunk(n):
            if n < WIN0:
                return w_ada_v[n // 24][n % 24], KD, 256
            for base, v in ((WIN0, w_in_v[0]), (WIN1, w_in_v[1])):
                if base <= n < base + 8:
                    return v[ORDER[n - base]], KD, 256
            for base, v in ((WOUT0, w_out_v[0]), (WOUT1, w_out_v[1])):
                if base <= n < base + 4:
                    return v[n - base], KD, 256
            if n < DENSE2:
                c = (n - DENSE) // 2
                m = P * min(3, FT - 3 * c)
                return (w1_v, w3_v)[(n - DENSE) % 2][:, :, 384 * c:384 * c + m], KD, m
            return w2_v[(n - DENSE2) // 2][(n - DENSE2) % 2], 11, 256

        def released(n):
            if n < WIN0:
                return ada_mm, n + 1
            for l, base in ((0, WIN0), (1, WIN1)):
                if base <= n < base + 8:
                    return step(l, "pj_done", 2 * (n - base) + 2)
            for l, base in ((0, WOUT0), (1, WOUT1)):
                if base <= n < base + 4:
                    return step(l, "po_done", 2 * (n - base) + 2)
            if n < DENSE2:
                return ff_done, min(3 * ((n - DENSE) // 2) + 3, FT)
            return fy_done, 2 * ((n - DENSE2) // 2) + 2

        block = ctx.enter_context(nc.Block())

        @block.sync
        def _(sp):
            def load(n, src):
                ap, k, cols = src
                sp.dma_start(slot(n, k, cols), ap).then_inc(full[n % RING], 16)

            for n in range(RING):
                load(n, chunk(n))
            for l in range(DEPTH):
                with sp.Fori(0, 24 // RING - 1) as i:
                    for j in range(RING):
                        used = sp.snap(sp.to_reg(24 * l + RING * i + j + 1))
                        sp.wait_ge(const_ready, 1)
                        sp.wait_ge(ada_mm, used)
                        load(j, (w_ada_v[l][RING * i + RING + j], KD, 256))
                for j in range(RING):
                    sp.wait_ge(ada_mm, 24 * l + 24 - RING + j + 1)
                    load(j, chunk(24 * (l + 1) + j))
            for n in range(WIN0, MOE):
                sp.wait_ge(*released(n))
                load(n + RING, chunk(n + RING) if n + RING < MOE else expert_chunk(0, n + RING - MOE))

            def used(e, j):
                if j < 8:
                    return R["f_done"], ET * e + min(3 * (j // 2) + 3, ET)
                return R["y_done"], KD * e + 2 * (j - 8) + 2

            def first_rows(e):
                row = first_of(sp, e)
                for t in range(2):
                    sp.dma_start(stage[:, t, :], Hd[bass.ds(row + P * t, P), :]).then_inc(Rin[t], 16)

            def rest_of_rows(e):
                c, row = tokens_of(sp, e), first_of(sp, e)
                with sp.If(c <= NW):
                    for t in range(2, NT):
                        sp.sem_inc(Rwide[t - 2], 16)
                with sp.Else():
                    for t in range(2, NT):
                        free = sp.snap(sp.to_reg(NT * e + t - 1))
                        sp.wait_ge(const_ready, 1)
                        sp.wait_ge(R["in_tr"], free)
                        sp.dma_start(stage[:, t % 2, :], Hd[bass.ds(row + AT[t], P), :]).then_inc(Rwide[t - 2], 16)

            def rows_out(e):
                c, row = tokens_of(sp, e), first_of(sp, e)
                with sp.If(c <= NW):
                    sp.sem_inc(R["y_out"], 16 * (NT - 2))
                    for t in range(2):
                        there = sp.snap(sp.to_reg(NT * e + NT + t))
                        sp.wait_ge(const_ready, 1)
                        sp.wait_ge(R["yt_ev"], there)
                        sp.dma_start(Yd[bass.ds(row + P * t, P), :], yrow[:, t, :]).then_inc(R["y_out"], 16)
                with sp.Else():
                    for t in range(NT):
                        there = sp.snap(sp.to_reg(NT * e + t + 2))
                        sp.wait_ge(const_ready, 1)
                        sp.wait_ge(R["yt_ev"], there)
                        sp.dma_start(Yd[bass.ds(row + AT[t], P), :], stage[:, 2, :]).then_inc(R["y_out"], 16)

            for b in range(3):
                sp.wait_ge(Rout[b], 32 * len(range(b, NT, 3)))
            sp.wait_ge(R["count"], 2)
            first_rows(0)
            with sp.Fori(0, NE - 1) as e:
                rest_of_rows(e)
                free = sp.snap(sp.to_reg(NT * e + NT))
                sp.wait_ge(const_ready, 1)
                sp.wait_ge(R["in_tr"], free)
                first_rows(e + 1)
                for j in range(PER_E):
                    which, n = used(e, j)
                    n = sp.snap(sp.to_reg(n))
                    sp.wait_ge(const_ready, 1)
                    sp.wait_ge(which, n)
                    load(MOE + j + RING, expert_chunk(e, j + RING) if j < PER_E - RING else expert_chunk(e + 1, j + RING - PER_E))
                rows_out(e)
            last = sp.snap(sp.to_reg(NE - 1))
            rest_of_rows(last)
            for j in range(PER_E - RING):
                sp.wait_ge(*used(NE - 1, j))
                load(MOE + j + RING, expert_chunk(NE - 1, j + RING))
            rows_out(last)
            for t in range(NT):
                n = min(P, T - P * t)
                sp.wait_ge(fin_ev, t + 1)
                dst = O["y_prompt"][0, P * t:P * t + n, :] if t < 4 else O["y_sample"].rearrange("b s d -> (b s) d")
                sp.dma_start(dst, xin[0:n, t, :]).then_inc(fin_out, 16)
            sp.wait_ge(fin_out, 16 * NT)
            sp.wait_ge(stored, 16 * 3 * DEPTH)
            for l in range(DEPTH):
                sp.wait_ge(*step(l, "tail_out", 16 * 8))

        @block.gpsimd
        def _(pool):
            order = [0]

            def link(ins):
                order[0] += 1
                ins.then_inc(gchain, 1)
                pool.wait_ge(gchain, order[0])

            link(pool.memset(ident[:], 0.0))
            pool.affine_select(out=ident[:], in_=ident[:], compare_op=ALU.not_equal, fill=1.0, base=0,
                               pattern=[[-1, P]], channel_multiplier=1).then_inc(const_ready, 1)
            pool.iota(cinv[:], pattern=[[0, 2], [1, POOL]], base=1, channel_multiplier=0,
                      allow_small_or_imprecise_dtypes=True).then_inc(const_ready, 1)
            link(pool.memset(tri[:], 1.0))
            link(pool.memset(valid[:], 1.0))
            link(pool.memset(valid[:, NT - 1:NT], 0.0))
            pool.memset(valid[0:NS, NT - 1:NT], 1.0)
            pool.affine_select(out=tri[:], in_=tri[:], compare_op=ALU.is_gt, fill=0.0, base=0,
                               pattern=[[1, P]], channel_multiplier=-1).then_inc(R["const"], 1)
            pool.iota(eidx[:], pattern=[[1, NE]], base=0, channel_multiplier=0,
                      allow_small_or_imprecise_dtypes=True).then_inc(R["const"], 1)
            pool.memset(ebase[:], 0.0).then_inc(R["const"], 1)

            for l in range(DEPTH):
                if l:
                    pool.wait_ge(*step(l - 1, "x1_ready", 1))
                    link(pool.memset(stage[0:T // 5, 0, :], 0.0))
                    pool.dma_start(Hd[PICKS:ROOM].rearrange("(a p) n -> p a n", a=5),
                                   stage[0:T // 5, 0:1, :].to_broadcast([T // 5, 5, D])).then_inc(R["zero"], 16)
                    pool.wait_ge(R["zero"], 16)
                pool.dma_start(ws_raw, A["w_s"][l].rearrange("h t s -> t h s")).then_inc(s["mx_in"], 16)
                for h in range(4):
                    r = slice(64 * (h % 2), 64 * (h % 2) + 64)
                    pool.dma_start(bsb[r, h // 2, :], A["b_s"][l, h:h + 1, :].to_broadcast([64, P])).then_inc(s["mx_in"], 16)
                    pool.dma_start(ws00[r, h // 2:h // 2 + 1], A["w_s"][l, h, 0:1, 0:1].to_broadcast([64, 1])).then_inc(s["mx_in"], 16)
                link(pool.memset(bd, 0.0))
                for g in range(4):
                    r = slice(64 * (g % 2), 64 * (g % 2) + 64)
                    pool.dma_start(bd[r, g // 2, r], A["pool_w"][l, g]).then_inc(s["mx_in"], 16)
                pool.dma_start(stA[0:2 * NS], A["state_conv_a"][l].rearrange("b r c -> (b r) c")).then_inc(s["mx_in"], 16)
                pool.dma_start(stC[0:120], A["state_conv_c"][l].rearrange("(g b) r c -> (b r) g c", g=2)).then_inc(s["mx_in"], 16)
                pool.dma_start(stD[0:120], A["state_pool_d"][l].rearrange("b r c -> (b r) c")).then_inc(s["mx_in"], 16)
                pool.dma_start(O["a_s"][l, :, 0:1, :], A["state_conv_a"][l, :, 1:2, :]).then_inc(stored, 16)
                pool.dma_start(O["c_s"][l, :, 0:29, :], A["state_conv_c"][l, :, 1:30, :]).then_inc(stored, 16)
                pool.dma_start(O["d_s"][l, :, 0:14, :], A["state_pool_d"][l, :, 1:15, :]).then_inc(stored, 16)
                if l == 0:
                    pool.wait_ge(pro_tr, 11)
                else:
                    pool.wait_ge(fy_done, KD)
                pool.memset(zin[:, :, 0:TAPS_A - 1], 0.0)
                pool.memset(gin[:, :, 0:TAPS_C - 1], 0.0)
                pool.memset(pin[:, :, 0:POOL - 1], 0.0).then_inc(s["hist_zero"], 1)
                pool.wait_ge(*step(l, "ws_copy", 1))
                pool.affine_select(out=wsT, in_=wsT, compare_op=ALU.is_ge, fill=0.0, base=0,
                                   pattern=[[0, 4], [1, P]], channel_multiplier=-1).then_inc(s["ws_masked"], 1)
                pool.wait_ge(*step(l, "pj_free0", 4))
                pool.wait_ge(*step(l, "pj_free1", 4))
                lo, hi, n = slice(0, 64), slice(64, P), SEQ + 15

                def doubled(dst, src, back, a):
                    return pool.tensor_tensor(dst[..., a:n], src[..., a:n], src[..., a - back:n - back], ALU.add)

                def last(dst_rows, ct, src, back):
                    return pool.tensor_tensor(outs[dst_rows, 6 + ct, 0:SEQ], src[dst_rows, ct, 15:n],
                                              src[dst_rows, ct, 15 - back:n - back], ALU.add)
                link(doubled(pa, pin, 1, 1))
                link(last(lo, 0, pin, 1))
                link(last(hi, 0, pa, 2))
                link(doubled(pb[:, 1], pa[:, 1], 2, 3))
                link(last(lo, 1, pb, 4))
                link(doubled(pa[:, 1], pb[:, 1], 4, 7))
                last(hi, 1, pa, 8).then_inc(s["pool_out"], 1)
                pool.wait_ge(*step(l, "vt_copy", 1))
                pool.dma_start(O["v_p"][l, 0], vtok[:, 3, :]).then_inc(s["tail_out"], 16)
                for n, dst in enumerate([O["a_p"][l, 0], O["c_p"][l, 0], O["d_p"][l, 0], O["a_s"][l, :, 1, :],
                                         O["c_s"][l, :, 29, :], O["d_s"][l, :, 14, :], O["v_s"][l, :, 0, :]]):
                    pool.wait_ge(*step(l, "tail_copy", n + 1))
                    pool.dma_start(dst, outrow[0:TAIL[n], n, :]).then_inc(s["tail_out"], 16)
            pool.wait_ge(R["zero"], 16)
            for t in range(NT):
                n = min(P, T - P * t)
                pool.wait_ge(R["h_row"], t + 1)
                pool.wait_ge(R["route"], 1)
                for r in range(2):
                    pool.indirect_dma_start(Hd, bass.IndirectOffsetOnAxis(ap=place[0:n, r, t:t + 1], axis=0),
                                            stage[0:n, t % 3, :], None).then_inc(Rout[t % 3], 16)
            for b in range(3):
                pool.wait_ge(Rout[b], 32 * len(range(b, NT, 3)))
            pool.wait_ge(R["y_out"], 16 * NE * NT + 16)
            pool.wait_ge(R["in_tr"], NE * NT)
            for t in range(NT):
                n = min(P, T - P * t)
                for r in range(2):
                    if t >= 1:
                        pool.wait_ge(R["f_row"], t)
                    pool.indirect_dma_start(stage[0:n, r, :], None, Yd[0:PICKS],
                                            bass.IndirectOffsetOnAxis(ap=place[0:n, r, t:t + 1], axis=0)).then_inc(Rback[r], 16)

        NVEC = 12 * DEPTH + 1
        GO = [0, 2, 3, 1]
        READY = {0: "gA", 1: "gB", 2: "gC", 3: "gD"}

        @block.tensor
        def _(pe):
            def gemm(q, lhs, rhs, kn):
                for k in range(kn):
                    for h in range(2):
                        mm = pe.matmul(PP[q][:, h, 0:HT], lhs(k), rhs(k)[:, HT * h:HT * h + HT],
                                       start=(k == 0), stop=(k == kn - 1))
                return mm

            def channel_sum(q, tiles):
                return gemm(q, lambda k: ones[:], lambda k: tiles[k], len(tiles))

            def norm_sum(tag):
                for j in range(KD):
                    pe.wait_ge(*norm_step(tag, "sq", j + 1))
                    for h in range(2):
                        mm = pe.matmul(PP[2][:, h, 0:HT], ones[:], work[:, j, HT * h:HT * h + HT],
                                       start=(j == 0), stop=(j == KD - 1))
                mm.then_inc(ns["sum"], 1)

            def arrived(n):
                pe.wait_ge(full[n % RING], 16 * (n // RING + 1))

            pe.wait_ge(const_ready, 1)
            pe.wait_ge(vec_in, 16 * NVEC)
            for l in range(DEPTH):
                pe.transpose(PP[2][:, 0, l * NROWS:(l + 1) * NROWS], rows[0:NROWS, l, :], ident[0:NROWS, 0:NROWS])
            pe.transpose(PP[2][:, 1, 0:96], rows[0:96, 2, :], ident[0:96, 0:96]).then_inc(pro_tr, 1)
            pe.wait_ge(silu_c, 1)
            for j in range(KD):
                tr = pe.transpose(PP[3][:, 0, j * NQ:(j + 1) * NQ], crow[0:NQ, j * P:(j + 1) * P], ident[0:NQ, 0:NQ])
            tr.then_inc(pro_tr, 1)
            pe.wait_ge(x_in, 16 * NT)
            for j in range(KD):
                if j >= 4:
                    if j % 2 == 0:
                        pe.wait_ge(pro_dve, 3 + (j - 4) // 2 + 1)
                    else:
                        pe.wait_ge(pro_act, (j - 4) // 2 + 1)
                for t in range(4):
                    tr = pe.transpose(PP[j % 4 // 2][:, j % 2, t * P:(t + 1) * P], xin[:, t, j * P:(j + 1) * P], ident[:])
                tr.then_inc(pro_tr, 1)
            for j in range(KD):
                tr = pe.transpose(PP[3][:, 1, j * NS:(j + 1) * NS], xin[0:NS, 4, j * P:(j + 1) * P], ident[0:NS, 0:NS])
            tr.then_inc(pro_tr, 1)

            pe.wait_ge(pro_dve, 8)
            pe.wait_ge(pro_act, 4)
            pe.sem_inc(ada_tr, 2)
            for l in range(DEPTH):
                with pe.Fori(0, 24 // RING) as i:
                    def turned(j):
                        n = 24 * l + RING * i + j
                        there, free = pe.snap(pe.to_reg(n + 3)), pe.snap(pe.to_reg(n + 1))
                        pe.wait_ge(pro_dve, 8)
                        pe.wait_ge(ada_row, there)
                        pe.wait_ge(ada_out, free)
                        for m in range(2):
                            tr = pe.transpose(PP[1][:, j % 2, m * NQ:(m + 1) * NQ], modrow[0:NQ, j % 2, m * P:(m + 1) * P],
                                              ident[0:NQ, 0:NQ])
                        tr.then_inc(ada_tr, 1)
                    for j in range(RING):
                        pe.wait_ge(full[j], 16 * (24 // RING * l + i + 1))
                        pe.wait_ge(ada_row, 24 * l + RING * i + j + 1)
                        for k in range(KD):
                            mm = pe.matmul(PP[0][0:NQ, j % 2, 0:256], cT[:, k, :], slot(j, KD, 256)[:, k, :],
                                           start=(k == 0), stop=(k == KD - 1))
                        mm.then_inc(ada_mm, 1)
                        if j:
                            turned(j - 1)
                    turned(RING - 1)

            for l in range(DEPTH):
                norm_sum(2 * l)
                pe.wait_ge(*norm_step(2 * l, "h", 1))
                pe.wait_ge(*step(l, "mx_in", 16 * 16))
                for h in range(4):
                    tr = pe.transpose(PP[3][:, 0, h * P:(h + 1) * P], ws_raw[:, h, :], ident[:])
                tr.then_inc(s["ws_tr"], 1)
                for ct in range(2):
                    c = slice(ct * P, ct * P + P)
                    pe.transpose(PP[3][:, 1, 16 * ct:16 * ct + 16], stA[0:16, c], ident[0:16, 0:16])
                    for g in range(2):
                        at = 32 + 240 * ct + 120 * g
                        pe.transpose(PP[3][:, 1, at:at + 120], stC[0:120, g, c], ident[0:120, 0:120])
                    tr = pe.transpose(PP[2][:, 0, 260 + 120 * ct:380 + 120 * ct], stD[0:120, c], ident[0:120, 0:120])
                tr.then_inc(s["st_tr"], 1)
                for q in range(16):
                    n = (WIN0, WIN1)[l] + q // 2
                    if q % 2 == 0:
                        arrived(n)
                    if q >= 2:
                        pe.wait_ge(*step(l, f"pj_free{q % 2}", q // 2))
                    gemm(q % 2, lambda k: slot(n, KD, 256)[:, k, P * (q % 2):P * (q % 2) + P],
                         lambda k: hT[:, k, :], KD).then_inc(s["pj_done"], 1)
                    if q == 11:
                        pe.wait_ge(*step(l, "pj_free0", 3))
                        pe.wait_ge(*step(l, "pj_free1", 3))
                        pe.wait_ge(*step(l, "st_copy", 3))
                        channel_sum(2, [proj[:, HOME[B_V] + ct, :] for ct in range(2)]).then_inc(s["lnb_sum"], 1)
                        pe.wait_ge(*step(l, "lnc_in", 1))
                        channel_sum(3, [outs[:, 4 + ct, :] for ct in range(2)]).then_inc(s["lnc_sum"], 1)
                    if q == 13:
                        pe.wait_ge(*step(l, "lnb_sq", 2))
                        channel_sum(2, [proj[:, HOME[C_G] + ct, :] for ct in range(2)]).then_inc(s["lnb_var"], 1)
                        pe.wait_ge(*step(l, "lnc_sq", 2))
                        channel_sum(3, [proj[:, HOME[A_H] + ct, :] for ct in range(2)]).then_inc(s["lnc_var"], 1)
                pe.wait_ge(*step(l, "vn_ready", 2))
                pe.wait_ge(*step(l, "lnc_root", 1))
                for n in range(4):
                    for ct in range(2):
                        tr = pe.transpose(PP[3][:, n // 2, (n % 2) * W + ct * P:(n % 2) * W + ct * P + P],
                                          proj[:, HOME[B_V] + ct, n * P:(n + 1) * P], ident[:])
                tr.then_inc(s["vt_tr"], 1)
                pe.wait_ge(*step(l, "vt_copy", 1))
                pe.wait_ge(*step(l, "ws_masked", 1))
                pe.wait_ge(*step(l, "pj_free0", 8))
                pe.wait_ge(*step(l, "pj_free1", 8))
                for n in range(4):
                    for ct in range(2):
                        mm = pe.matmul(PP[n // 2][:, n % 2, ct * 256:ct * 256 + 256], vtok[:, n, ct * P:(ct + 1) * P],
                                       wsT[:, 2 * ct:2 * ct + 2, :].rearrange("p h t -> p (h t)"), start=True, stop=True)
                mm.then_inc(s["mix_done"], 1)
                pe.wait_ge(*step(l, "pooled", 1))
                for ct in range(2):
                    gemm(2 + ct, lambda k: bd[:, ct, :], lambda k: outs[:, 6 + ct, :], 1).then_inc(s["pool_mm"], 1)
                pe.wait_ge(*step(l, "gD", 2))
                for i, g in enumerate(GO):
                    pe.wait_ge(*step(l, "g_sq", 2 * i + 2))
                    if i == 2:
                        pe.wait_ge(*step(l, "mix_read", 1))
                    channel_sum((i + 2) % 4, [hT[:, 2 * g + ct, :] for ct in range(2)]).then_inc(s["g_sum"], 1)
                pe.wait_ge(*step(l, "merged", KD))
                for q in range(KD):
                    n = (WOUT0, WOUT1)[l] + q // 2
                    if q % 2 == 0:
                        arrived(n)
                    if q >= 2:
                        pe.wait_ge(*step(l, "po_free", q - 1))
                    gemm(q % 2, lambda k: slot(n, KD, 256)[:, k, P * (q % 2):P * (q % 2) + P],
                         lambda k: hT[:, k, :], KD).then_inc(s["po_done"], 1)
                src = [zin[:, :, SEQ:SEQ + 2], gin[:, :, SEQ:SEQ + 30], pin[:, :, SEQ:SEQ + 15], zin[:, :, SEQ + 2:SEQ + 10],
                       gin[:, :, SEQ + 30:SEQ + 38], pin[:, :, SEQ + 15:SEQ + 23],
                       proj[:, HOME[B_V]:HOME[B_V] + 2, SEQ:T]]
                for n, (a, m) in enumerate(zip(src, TAIL)):
                    for ct in range(2):
                        tr = pe.transpose(tail_bank(n)[0:m, ct * P:(ct + 1) * P], a[:, ct, :], ident[:])
                    tr.then_inc(s["tail_tr"], 1)
                pe.wait_ge(*step(l, "tail_copy", 7))
                norm_sum(2 * l + 1)
                pe.wait_ge(*norm_step(2 * l + 1, "h", 1))
                if l == 0:
                    for f in range(FT):
                        n = DENSE + 2 * (f // 3)
                        if f % 3 == 0:
                            arrived(n)
                            arrived(n + 1)
                        if f >= 2:
                            pe.wait_ge(ff_free, f - 1)
                        m = P * min(3, FT - 3 * (f // 3))
                        for w in range(2):
                            mm = gemm(2 * (f % 2) + w, lambda k: slot(n + w, KD, m)[:, k, P * (f % 3):P * (f % 3) + P],
                                      lambda k: hT[:, k, :], KD)
                        mm.then_inc(ff_done, 1)
                    pe.wait_ge(ff_free, FT)
                    for q in range(KD):
                        n = DENSE2 + 2 * (q // 2)
                        if q % 2 == 0:
                            arrived(n)
                            arrived(n + 1)
                        if q >= 4:
                            pe.wait_ge(fy_free, q - 3)
                        gemm(q % 4, lambda k: slot(n + k // 11, 11, 256)[:, k % 11, P * (q % 2):P * (q % 2) + P],
                             lambda k: G[:, k, :], FT).then_inc(fy_done, 1)

            pe.wait_ge(wr_in, 32)
            for k in range(KD):
                for h in range(2):
                    gemm_r = pe.matmul(PP[0][0:NE, h, 0:HT], wrt[:, k, :], hT[:, k, HT * h:HT * h + HT],
                                       start=(k == 0), stop=(k == KD - 1))
            gemm_r.then_inc(R["lg"], 1)
            pe.wait_ge(R["lg_ev"], 1)
            for t in range(NT):
                n = min(P, T - P * t)
                tr = pe.transpose(PP[1][0:n, 0, t * NE:(t + 1) * NE], lgT[0:NE, P * t:P * t + n], ident[0:NE, 0:NE])
            tr.then_inc(R["lg_tr"], 1)
            def h_rows(t):
                n = min(P, T - P * t)
                if t:
                    pe.wait_ge(R["h_row"], t)
                for j in range(KD):
                    tr = pe.transpose(PP[2][0:n, j // 4, (j % 4) * P:(j % 4) * P + P], hT[:, j, P * t:P * t + n], ident[:])
                tr.then_inc(R["h_tr"], 1)
            h_rows(0)
            pe.wait_ge(R["mask"], 1)
            mflat = mask[:].rearrange("p t e -> p (t e)")
            pe.matmul(PP[0][:, 0, 0:NT * NE], tri[:], mflat, start=True, stop=True)
            pe.matmul(PP[0][:, 1, 0:NT * NE], ones[:], mflat, start=True, stop=True).then_inc(R["pre"], 1)
            for t in range(1, NT):
                h_rows(t)
            pe.wait_ge(R["route"], 1)


            def chunk_here(e, n):
                pe.wait_ge(full[n % RING], 16 * (n // RING + 1) + 32 * e)

            def narrow_rows(e):
                pe.sem_inc(R["in_tr"], 1)
                pe.sem_inc(R["yt_tr"], 3)
                for t in range(2):
                    pe.wait_ge(Rin[t], 16 * e + 16)
                    for h in range(2):
                        if t:
                            pe.wait_ge(R["in_ev"], NT * e + h + 2)
                        for j in range(4 * h, 4 * h + 4):
                            tr = pe.transpose(PP[3][:, h, (j % 4) * P:(j % 4) * P + P], stage[:, t, j * P:(j + 1) * P], ident[:])
                        tr.then_inc(R["in_tr"], 1)
                pe.wait_ge(R["in_ev"], NT * e + NT)

            def narrow_products(e, n):
                for f in range(ET):
                    c = f // 3
                    if f % 3 == 0:
                        chunk_here(e, MOE + 2 * c)
                        chunk_here(e, MOE + 2 * c + 1)
                    pe.wait_ge(R["f_free"], ET * e + f + 1)
                    m = P * min(3, ET - 3 * c)
                    for w in range(2):
                        for k in range(KD):
                            mm = pe.matmul(PP[w][:, f % 2, 0:n], slot(MOE + 2 * c + w, KD, m)[:, k, P * (f % 3):P * (f % 3) + P],
                                           hn[:, k, 0:n], start=(k == 0), stop=(k == KD - 1))
                    mm.then_inc(R["f_done"], 1)
                pe.wait_ge(R["f_free"], ET * e + ET + 2)
                for q in range(KD + 1):
                    if q < KD:
                        if q % 2 == 0:
                            chunk_here(e, MOE + 8 + q // 2)
                        pe.wait_ge(R["y_free"], KD * e + q + 1)
                        for k in range(ET):
                            mm = pe.matmul(PP[2][:, q % 2, 0:n], slot(MOE + 8 + q // 2, ET, 256)[:, k, P * (q % 2):P * (q % 2) + P],
                                           Gn[:, k, 0:n], start=(k == 0), stop=(k == ET - 1))
                        mm.then_inc(R["y_done"], 1)
                    if q:
                        j = q - 1
                        pe.wait_ge(R["y_free"], KD * e + j + 3)
                        if j == 4:
                            pe.wait_ge(R["yt_ev"], NT * e + 4)
                        for t in range(2):
                            tr = pe.transpose(PP[3][:, t, (j % 4) * P:(j % 4) * P + P], yn[:, j, P * t:P * t + P], ident[:])
                        if j % 4 == 3:
                            tr.then_inc(R["yt_tr"], 1)

            def wide(e):
                for t in range(NT):
                    if t < 2:
                        pe.wait_ge(Rin[t], 16 * e + 16)
                    else:
                        pe.wait_ge(Rwide[t - 2], 16 * e + 16)
                    if t:
                        pe.wait_ge(R["in_ev"], NT * e + t)
                    for j in range(KD):
                        tr = pe.transpose(PP[3][:, j // 4, (j % 4) * P:(j % 4) * P + P], stage[:, t % 2, j * P:(j + 1) * P], ident[:])
                    tr.then_inc(R["in_tr"], 1)
                pe.wait_ge(R["in_ev"], NT * e + NT)
                for f in range(ET):
                    c = f // 3
                    if f % 3 == 0:
                        chunk_here(e, MOE + 2 * c)
                        chunk_here(e, MOE + 2 * c + 1)
                    pe.wait_ge(R["f_free"], ET * e + f + 2)
                    m = P * min(3, ET - 3 * c)
                    for w in range(2):
                        mm = gemm(w, lambda k: slot(MOE + 2 * c + w, KD, m)[:, k, P * (f % 3):P * (f % 3) + P],
                                  lambda k: hexp[:, k, :], KD)
                    mm.then_inc(R["f_done"], 1)
                pe.wait_ge(R["f_free"], ET * e + ET + 2)
                for q in range(KD):
                    if q % 2 == 0:
                        chunk_here(e, MOE + 8 + q // 2)
                    pe.wait_ge(R["y_free"], KD * e + q + 2)
                    gemm(2, lambda k: slot(MOE + 8 + q // 2, ET, 256)[:, k, P * (q % 2):P * (q % 2) + P],
                         lambda k: G[:, k, :], ET).then_inc(R["y_done"], 1)
                pe.wait_ge(R["y_free"], KD * e + KD + 2)
                for t in range(NT):
                    if t:
                        pe.wait_ge(R["yt_ev"], NT * e + t + 1)
                    for j in range(KD):
                        tr = pe.transpose(PP[3][:, j // 4, (j % 4) * P:(j % 4) * P + P], work[:, j, AT[t]:AT[t] + P], ident[:])
                    tr.then_inc(R["yt_tr"], 1)

            def narrow_by_width(e, c, widths):
                if len(widths) == 1:
                    narrow_products(e, widths[0])
                    return
                with pe.If(c <= widths[0]):
                    narrow_products(e, widths[0])
                with pe.Else():
                    narrow_by_width(e, c, widths[1:])

            pe.wait_ge(R["count"], 2)
            with pe.Fori(0, NE) as e:
                c = tokens_of(pe, e)
                pe.wait_ge(R["yt_ev"], NT * e + 1)
                with pe.If(c <= NW):
                    narrow_rows(e)
                    narrow_by_width(e, c, WIDTHS)
                with pe.Else():
                    wide(e)
            for t in range(NT):
                n = min(P, T - P * t)
                pe.wait_ge(R["f_row"], t + 1)
                if t:
                    pe.wait_ge(R["fo_ev"], t)
                for j in range(KD):
                    tr = pe.transpose(PP[0][:, j // 4, (j % 4) * P:(j % 4) * P + n], stage[0:n, 2, j * P:(j + 1) * P],
                                      ident[0:n, 0:n])
                tr.then_inc(R["fo_tr"], 1)
            norm_sum(4)
            pe.wait_ge(*norm_step(4, "h", 1))
            for t in range(NT):
                n = min(P, T - P * t)
                if t >= 2:
                    pe.wait_ge(fin_ev, t - 1)
                for j in range(KD):
                    tr = pe.transpose(PP[t % 2][0:n, j // 4, (j % 4) * P:(j % 4) * P + P], hT[:, j, P * t:P * t + n], ident[:])
                tr.then_inc(fin_tr, 1)

        @block.scalar
        def _(act):
            act.dma_start(crow[0:1], A["c_prompt"]).then_inc(c_in, 16)
            act.dma_start(crow[1:NQ], A["c_sample"]).then_inc(c_in, 16)
            for l in range(DEPTH):
                for name, (at, n) in ROWS.items():
                    src = A[name] if name == "g_final" else A[name][l]
                    if name in ("g_out", "conv_a_w", "conv_c_w"):
                        src = src.rearrange("a (r p) -> (a r) p", p=P)
                    else:
                        src = src.rearrange("(r p) -> r p", p=P)
                    act.dma_start(rows[at:at + n, l, :], src).then_inc(vec_in, 16)
            act.dma_start(rows[0:96, 2, :], A["b_ada"].rearrange("l (r p) -> (l r) p", p=P)).then_inc(vec_in, 16)
            for t in range(4):
                act.dma_start(xin[:, t, :], A["x_prompt"][0, P * t:P * t + P, :]).then_inc(x_in, 16)
            act.dma_start(xin[0:NS, 4, :], A["x_sample"].rearrange("b s d -> (b s) d")).then_inc(x_in, 16)
            act.dma_start(wrt[:], A["w_router"][0].rearrange("(k p) e -> p k e", p=P)).then_inc(wr_in, 16)
            act.dma_start(brt[:], A["b_router"][0].rearrange("(e a) -> e a", a=1)).then_inc(wr_in, 16)

            act.wait_ge(c_in, 32)
            act.activation(crow[0:NQ], crow[0:NQ], ACT.Silu).then_inc(silu_c, 1)
            for j in range(1, KD, 2):
                act.wait_ge(pro_tr, 3 + j)
                act.activation(xT[:, j, 0:SEQ], PP[j % 4 // 2][:, j % 2, :], ACT.Copy).then_inc(pro_act, 1)
            act.sem_inc(ada_row, 2)
            for l in range(DEPTH):
                with act.Fori(0, 24 // RING) as i:
                    for j in range(RING):
                        n = 24 * l + RING * i + j
                        act.wait_ge(ada_mm, n + 1)
                        act.wait_ge(ada_tr, n + 1)
                        act.activation(modrow[:, j % 2, :], PP[0][0:NQ, j % 2, 0:256], ACT.Copy).then_inc(ada_row, 1)

            def root(q, dst, n, done):
                act.activation(two(dst), pp(q), ACT.Sqrt, bias=eps[:], scale=1.0 / n).then_inc(done, 1)

            def norm_act(tag):
                for j in range(KD):
                    act.activation(work[:, j, :], xT[:, j, :], ACT.Square).then_inc(ns["sq"], 1)
                act.wait_ge(*norm_step(tag, "sum", 1))
                root(2, stat[:], D, ns["root"])

            for l in range(DEPTH):
                if l == 0:
                    act.wait_ge(pro_dve, 8)
                    act.wait_ge(pro_act, 4)
                    act.wait_ge(const_dve, 1)
                else:
                    act.wait_ge(*step(0, "x2_ready", 1))
                norm_act(2 * l)

                def evac(q, dst, func=ACT.Copy):
                    act.wait_ge(*step(l, "pj_done", q + 1))
                    act.activation(two(dst), pp(q % 2), func).then_inc(s[f"pj_free{q % 2}"], 1)

                for q in (0, 1):
                    evac(q, proj[:, HOME[C_G] + q, :], ACT.Sigmoid)
                for q in (4, 5):
                    evac(q, proj[:, HOME[B_V] + q - 4, :])
                act.wait_ge(*step(l, "hist_zero", 1))
                for q in (6, 7):
                    evac(q, pin[:, q - 6, 15:15 + T])
                for q in (8, 9):
                    evac(q, proj[:, HOME[A_H] + q - 8, :])
                for ct in range(2):
                    act.wait_ge(*step(l, "vxc", ct + 1))
                    act.activation(proj[:, HOME[C_G] + ct, :], proj[:, HOME[B_V] + ct, :], ACT.Square).then_inc(s["lnb_sq"], 1)
                for ct in range(2):
                    act.wait_ge(*step(l, "lnc_xc", ct + 1))
                    act.activation(proj[:, HOME[A_H] + ct, :], outs[:, 4 + ct, :], ACT.Square).then_inc(s["lnc_sq"], 1)
                for q in (12, 13):
                    evac(q, proj[:, HOME[B_U] + q - 12, :])
                act.wait_ge(*step(l, "lnb_var", 1))
                root(2, stat[:], W, s["lnb_root"])
                act.wait_ge(*step(l, "lnc_var", 1))
                root(3, stat2[:], W, s["lnc_root"])
                for q in (14, 15):
                    evac(q, proj[:, HOME[A_B] + q - 14, :])
                for ct in range(2):
                    act.wait_ge(*step(l, "lnc_hat", ct + 1))
                    act.activation(outs[:, 4 + ct, :], outs[:, 4 + ct, :], ACT.Silu, bias=v_("ln_c_b", l, ct),
                                   scale=v_("ln_c_g", l, ct)).then_inc(s["gC"], 1)
                act.wait_ge(*step(l, "pj_done", 16))
                for i in range(5):
                    if i < 4:
                        g = GO[i]
                        for ct in range(2):
                            act.wait_ge(*step(l, READY[g], ct + 1))
                            act.activation(hT[:, 2 * g + ct, :], outs[:, 2 * g + ct, :], ACT.Square).then_inc(s["g_sq"], 1)
                    if i:
                        act.wait_ge(*step(l, "g_sum", i))
                        if i >= 3:
                            act.wait_ge(*step(l, "merged", 2 * (i - 2)))
                        root((i + 1) % 4, (stat, stat2)[(i - 1) % 2][:], W, s["g_root"])
                act.wait_ge(*step(l, "pool_free", 1))
                for n in range(7):
                    act.wait_ge(*step(l, "tail_tr", min(n // 2 * 2 + 2, 7)))
                    act.activation(outrow[0:TAIL[n], n, :], tail_bank(n)[0:TAIL[n]], ACT.Copy).then_inc(s["tail_copy"], 1)
                act.wait_ge(*step(l, "x1_ready", 1))
                norm_act(2 * l + 1)
                if l == 0:
                    act.wait_ge(*step(l, "tail_out", 16 * 8))
                    for f in range(FT):
                        act.wait_ge(ff_done, f + 1)
                        if f >= 2:
                            act.wait_ge(ff_free, f - 1)
                        act.activation(two(work[:, f % 2, :]), pp(2 * (f % 2)), ACT.Silu).then_inc(ff_act, 1)

            act.wait_ge(R["lg"], 1)
            act.wait_ge(wr_in, 32)
            act.activation(two(lgT), PP[0][0:NE, :, 0:HT], ACT.Identity, bias=brt[:]).then_inc(R["lg_ev"], 1)
            act.wait_ge(R["exp_d"], 1)
            act.activation(gate[:, 1, :], gate[:, 0, :], ACT.Exp).then_inc(R["gate"], 1)
            act.sem_inc(R["y_free"], 2)
            act.wait_ge(R["count"], 2)
            with act.Fori(0, NE) as e:
                c = tokens_of(act, e)
                with act.If(c <= NW):
                    for f in range(ET):
                        act.wait_ge(R["f_done"], ET * e + f + 1)
                        act.wait_ge(R["f_free"], ET * e + f + 1)
                        act.activation(hactn[:, f % 2, :], PP[0][:, f % 2, 0:NW], ACT.Silu).then_inc(R["f_act"], 1)
                    for q in range(KD):
                        act.wait_ge(R["y_done"], KD * e + q + 1)
                        act.activation(yn[:, q, :], PP[2][:, q % 2, 0:NW], ACT.Copy).then_inc(R["y_free"], 1)
                with act.Else():
                    for f in range(ET):
                        act.wait_ge(R["f_done"], ET * e + f + 1)
                        act.wait_ge(R["f_free"], ET * e + f + 1)
                        act.activation(two(hact[:, f % 2, :]), pp(0), ACT.Silu).then_inc(R["f_act"], 1)
                    act.wait_ge(R["y_out"], 16 * NT * e + 16)
                    for q in range(KD):
                        act.wait_ge(R["y_done"], KD * e + q + 1)
                        act.activation(two(work[:, q, :]), pp(2), ACT.Copy).then_inc(R["y_free"], 1)
            act.wait_ge(R["x_ready"], 1)
            norm_act(4)

        @block.vector
        def _(dve):
            order = [0]

            def done(ins):
                order[0] += 1
                ins.then_inc(dchain, 1)
                return order[0]

            def link(ins):
                dve.wait_ge(dchain, done(ins))

            dve.memset(eps[:], EPS)
            dve.memset(ones[:], 1.0).then_inc(const_dve, 1)
            for ct in range(2):
                dve.memset(win[0:64, ct:ct + 1], float((2, 8)[ct]))
                last = dve.memset(win[64:P, ct:ct + 1], float((4, 16)[ct]))
            link(last)
            dve.wait_ge(const_ready, 2)
            dve.reciprocal(winv[:], win[:])
            for ct in range(2):
                last = dve.tensor_scalar(cinv[:, ct, :], cinv[:, ct, :], win[:, ct:ct + 1], None, ALU.min)
            link(last)
            link(dve.reciprocal(cinv[:], cinv[:]))
            dve.wait_ge(pro_tr, 1)
            dve.tensor_copy(vec[:], PP[2][:, 0, 0:DEPTH * NROWS].rearrange("p (l n) -> p l n", l=DEPTH)).then_inc(pro_dve, 1)
            dve.tensor_copy(bada[:], PP[2][:, 1, 0:96]).then_inc(pro_dve, 1)
            dve.wait_ge(pro_tr, 2)
            dve.tensor_copy(cT[:], PP[3][:, 0, 0:KD * NQ].rearrange("p (k q) -> p k q", k=KD)).then_inc(pro_dve, 1)
            for j in range(0, KD, 2):
                dve.wait_ge(pro_tr, 3 + j)
                dve.tensor_copy(xT[:, j, 0:SEQ], PP[j % 4 // 2][:, j % 2, :]).then_inc(pro_dve, 1)
            dve.wait_ge(pro_tr, 11)
            dve.tensor_copy(xT[:, :, SEQ:T], PP[3][:, 1, 0:KD * NS].rearrange("p (k q) -> p k q", k=KD)).then_inc(pro_dve, 1)

            dve.wait_ge(pro_dve, 2)
            dve.sem_inc(ada_out, 2)
            for l in range(DEPTH):
                bad = bada[:, 48 * l:48 * l + 48].rearrange("p (b m) -> p b m", m=2)
                mv = mod[:, l].rearrange("p (b m) q -> p b m q", m=2)
                with dve.Fori(0, 24 // RING) as i:
                    for j in range(RING):
                        n = 24 * l + RING * i + j
                        dve.wait_ge(ada_tr, n + 3)
                        dve.tensor_tensor(mv[:, RING * i + j], PP[1][:, j % 2, 0:2 * NQ].rearrange("p (m q) -> p m q", m=2),
                                          bad[:, RING * i + j].unsqueeze(2).to_broadcast([P, 2, NQ]), ALU.add).then_inc(ada_out, 1)
            dve.wait_ge(ada_out, 2 + 24 * DEPTH)
            for l in range(DEPTH):
                for sec, g in ((SCALE1, "g_mix"), (SCALE2, "g_ffn")):
                    a = mod[:, l, 8 * sec:8 * sec + 8, :]
                    gv = vec[:, l, ROWS[g][0]:ROWS[g][0] + 8]
                    last = dve.scalar_tensor_tensor(a, a, 1.0, gv.unsqueeze(2).to_broadcast([P, 8, NQ]), ALU.add, ALU.mult)
            link(last)

            def norm_dve(tag, l, scale, shift):
                dve.wait_ge(*norm_step(tag, "root", 1))
                link(dve.reciprocal(stat[:], stat[:]))
                for j in range(KD):
                    dve.tensor_tensor(hT[:, j, :], xT[:, j, :], stat[:], ALU.mult).then_inc(ns["xhat"], 1)
                    if j:
                        affine(tag, l, scale, shift, j - 1)
                last = affine(tag, l, scale, shift, KD - 1)
                if scale is None:
                    last.then_inc(ns["h"], 1)
                    return
                link(last)
                hs = hT[:, :, SEQ:T]
                link(dve.tensor_tensor(hs, hs, mod[:, l, 8 * scale:8 * scale + 8, 1:NQ], ALU.mult))
                dve.tensor_tensor(hs, hs, mod[:, l, 8 * shift:8 * shift + 8, 1:NQ], ALU.add).then_inc(ns["h"], 1)

            def affine(tag, l, scale, shift, j):
                dve.wait_ge(*norm_step(tag, "xhat", j + 1))
                if scale is None:
                    return dve.tensor_scalar(hT[:, j, :], hT[:, j, :], v_("g_final", 0, j), None, ALU.mult)
                return dve.tensor_scalar(hT[:, j, 0:SEQ], hT[:, j, 0:SEQ], mod[:, l, 8 * scale + j, 0:1],
                                         mod[:, l, 8 * shift + j, 0:1], ALU.mult, ALU.add)

            def add_gated(l, sec, q, pair, free):
                g = mod[:, l, 8 * sec + q, :]
                c = done(dve.tensor_tensor(small[:, q % 2, :], PP[pair][:, 1, HT - NS:HT], g[:, 1:NQ], ALU.mult))
                dve.scalar_tensor_tensor(xT[:, q, 0:HT], PP[pair][:, 0, 0:HT], g[:, 0:1], xT[:, q, 0:HT], ALU.mult, ALU.add)
                dve.scalar_tensor_tensor(xT[:, q, HT:SEQ], PP[pair][:, 1, 0:HT - NS], g[:, 0:1], xT[:, q, HT:SEQ],
                                         ALU.mult, ALU.add).then_inc(free, 1)
                dve.wait_ge(dchain, c)
                return dve.tensor_tensor(xT[:, q, SEQ:T], xT[:, q, SEQ:T], small[:, q % 2, :], ALU.add)

            for l in range(DEPTH):
                norm_dve(2 * l, l, SCALE1, SHIFT1)
                dve.wait_ge(*step(l, "ws_tr", 1))
                dve.tensor_copy(wsT, PP[3][:, 0, :].rearrange("p (h t) -> p h t", h=4)).then_inc(s["ws_copy"], 1)
                dve.wait_ge(*step(l, "st_tr", 1))
                for dst, src, r in ((hisA, PP[3][:, 1, 0:32], 2), (hisC, PP[3][:, 1, 32:512], 30),
                                    (hisD, PP[2][:, 0, 260:500], 15)):
                    for ct in range(2):
                        m = NS * r
                        last = dve.tensor_copy(dst[:, ct, :, 0:r], src[:, ct * m:ct * m + m].rearrange("p (b r) -> p b r", r=r))
                    last.then_inc(s["st_copy"], 1)
                dve.wait_ge(*step(l, "hist_zero", 1))
                for q in (2, 3):
                    dve.wait_ge(*step(l, "pj_done", q + 1))
                    dve.wait_ge(*step(l, f"pj_free{q % 2}", 1))
                    dve.tensor_tensor(two(gin[:, q - 2, 30:30 + T]), pp(q % 2), two(proj[:, HOME[C_G] + q - 2, :]),
                                      ALU.mult).then_inc(s[f"pj_free{q % 2}"], 1)
                dve.wait_ge(*step(l, "pj_free0", 2))
                dve.wait_ge(*step(l, "pj_free1", 2))
                for ct in range(2):
                    last = dve.tensor_copy(hisC[:, ct, :, 30], gin[:, ct, SEQ + 30:SEQ + 38])
                link(last)

                def tap(name, k, ct):
                    return v_(name, l, 2 * k + ct)

                def taps(name, n, ct):
                    r0 = ROWS[name][0]
                    w = vec[:, l, r0:r0 + 2 * n].rearrange("p (k c) -> p c k", c=2)[:, ct]
                    return w.unsqueeze(1).to_broadcast([P, NS, n])

                for k in range(TAPS_C):
                    for ct in range(2):
                        acc = outs[:, 4 + ct, 0:SEQ]
                        if k == 0:
                            dve.tensor_scalar(acc, gin[:, ct, 0:SEQ], tap("conv_c_w", 0, ct), v_("conv_c_b", l, ct),
                                              ALU.mult, ALU.add).then_inc(s["conv_tap"], 1)
                        else:
                            dve.wait_ge(*step(l, "conv_tap", 2 * k + ct - 1))
                            dve.scalar_tensor_tensor(acc, gin[:, ct, k:k + SEQ], tap("conv_c_w", k, ct), acc,
                                                     ALU.mult, ALU.add).then_inc(s["conv_tap"], 1)
                for ct in range(2):
                    o = outs[:, 4 + ct, SEQ:T]
                    link(dve.tensor_tensor(tapC[:], hisC[:, ct], taps("conv_c_w", TAPS_C, ct), ALU.mult))
                    link(dve.tensor_reduce(o, tapC[:], AX.X, ALU.add))
                    last = dve.tensor_scalar(o, o, v_("conv_c_b", l, ct), None, ALU.add)
                last.then_inc(s["lnc_in"], 1)
                for q in (10, 11):
                    dve.wait_ge(*step(l, "pj_done", q + 1))
                    dve.wait_ge(*step(l, f"pj_free{q % 2}", 5))
                    dve.tensor_tensor(two(zin[:, q - 10, 2:2 + T]), pp(q % 2), two(proj[:, HOME[A_H] + q - 10, :]),
                                      ALU.mult).then_inc(s[f"pj_free{q % 2}"], 1)
                for q, tiles, sums, xc in ((2, [proj[:, HOME[B_V] + ct, :] for ct in range(2)], "lnb_sum", "vxc"),
                                           (3, [outs[:, 4 + ct, :] for ct in range(2)], "lnc_sum", "lnc_xc")):
                    dve.wait_ge(*step(l, sums, 1))
                    for ct in range(2):
                        dve.scalar_tensor_tensor(two(tiles[ct]), pp(q), -1.0 / W, two(tiles[ct]), ALU.mult,
                                                 ALU.add).then_inc(s[xc], 1)
                dve.wait_ge(*step(l, "pj_free0", 6))
                dve.wait_ge(*step(l, "pj_free1", 6))
                for ct in range(2):
                    last = dve.tensor_copy(hisA[:, ct, :, 2], zin[:, ct, SEQ + 2:SEQ + 10])
                link(last)
                for ct in range(2):
                    acc = outs[:, ct, 0:SEQ]
                    link(dve.tensor_scalar(acc, zin[:, ct, 0:SEQ], tap("conv_a_w", 0, ct), None, ALU.mult))
                    for k in (1, 2):
                        link(dve.scalar_tensor_tensor(acc, zin[:, ct, k:k + SEQ], tap("conv_a_w", k, ct), acc, ALU.mult, ALU.add))
                    link(dve.tensor_tensor(tapC[:, :, 0:TAPS_A], hisA[:, ct], taps("conv_a_w", TAPS_A, ct), ALU.mult))
                    link(dve.tensor_reduce(outs[:, ct, SEQ:T], tapC[:, :, 0:TAPS_A], AX.X, ALU.add))
                for ct in range(2):
                    last = dve.tensor_copy(hisD[:, ct, :, 15], pin[:, ct, SEQ + 15:SEQ + 23])
                link(last)
                for ct in range(2):
                    for r, w in ((slice(0, 64), (2, 8)[ct]), (slice(64, P), (4, 16)[ct])):
                        last = dve.tensor_reduce(outs[r, 6 + ct, SEQ:T], hisD[r, ct, :, POOL - w:POOL], AX.X, ALU.add)
                dve.wait_ge(*step(l, "pool_out", 1))
                link(last)
                link(dve.tensor_tensor(head16[:], outs[:, 6:8, 0:POOL], cinv[:], ALU.mult))
                for ct in range(2):
                    last = dve.scalar_tensor_tensor(outs[:, 6 + ct, :], outs[:, 6 + ct, :], winv[:, ct:ct + 1],
                                                    pin[:, ct, 15:15 + T], ALU.mult, ALU.subtract)
                link(last)
                dve.tensor_tensor(outs[:, 6:8, 0:POOL], head16[:], pin[:, :, 15:15 + POOL], ALU.subtract).then_inc(s["pooled"], 1)
                dve.wait_ge(*step(l, "lnb_root", 1))
                link(dve.reciprocal(stat[:], stat[:]))
                for ct in range(2):
                    v = proj[:, HOME[B_V] + ct, :]
                    link(dve.tensor_tensor(v, v, stat[:], ALU.mult))
                    dve.tensor_scalar(v, v, v_("ln_v_g", l, ct), v_("ln_v_b", l, ct), ALU.mult, ALU.add).then_inc(s["vn_ready"], 1)
                dve.wait_ge(*step(l, "lnc_root", 1))
                link(dve.reciprocal(stat2[:], stat2[:]))
                for ct in range(2):
                    o = outs[:, 4 + ct, :]
                    dve.tensor_tensor(o, o, stat2[:], ALU.mult).then_inc(s["lnc_hat"], 1)
                dve.wait_ge(*step(l, "pj_free0", 8))
                dve.wait_ge(*step(l, "pj_free1", 8))
                for ct in range(2):
                    dve.tensor_tensor(outs[:, ct, :], outs[:, ct, :], proj[:, HOME[A_B] + ct, :], ALU.mult).then_inc(s["gA"], 1)
                dve.wait_ge(*step(l, "vt_tr", 1))
                dve.wait_ge(*step(l, "lnc_sq", 2))
                dve.tensor_copy(vtok.rearrange("p (h a) w -> p h (a w)", h=2), PP[3][:]).then_inc(s["vt_copy"], 1)
                dve.wait_ge(*step(l, "vn_ready", 2))
                for ct in range(2):
                    last = dve.tensor_scalar(outs[:, 2 + ct, SEQ:T], proj[:, HOME[B_V] + ct, SEQ:T], ws00[:, ct:ct + 1],
                                             bsb[:, ct, 0:1], ALU.mult, ALU.add)
                dve.wait_ge(*step(l, "mix_done", 1))
                for r in range(2):
                    rr = slice(64 * r, 64 * r + 64)
                    for ct in range(2):
                        for h in range(2):
                            last = dve.tensor_tensor(outs[rr, 2 + ct, 256 * h:256 * h + 256].rearrange("p (n t) -> p n t", n=2),
                                                     PP[h][rr, :, ct * 256 + r * P:ct * 256 + r * P + P],
                                                     bsb[rr, ct:ct + 1, :].to_broadcast([64, 2, P]), ALU.add)
                last.then_inc(s["mix_read"], 1)
                dve.wait_ge(*step(l, "mix_read", 1))
                for ct in range(2):
                    dve.tensor_tensor(outs[:, 2 + ct, :], outs[:, 2 + ct, :], proj[:, HOME[B_U] + ct, :], ALU.mult).then_inc(s["gB"], 1)
                for ct in range(2):
                    dve.wait_ge(*step(l, "pool_mm", ct + 1))
                    dve.tensor_scalar(two(outs[:, 6 + ct, :]), pp(2 + ct), v_("pool_scale", l, ct), None, ALU.mult).then_inc(s["gD"], 1)
                dve.sem_inc(s["pool_free"], 1)
                for i, g in enumerate(GO):
                    st = (stat, stat2)[i % 2]
                    dve.wait_ge(*step(l, "g_root", i + 1))
                    link(dve.reciprocal(st[:], st[:]))
                    for ct in range(2):
                        j = 2 * g + ct
                        dve.scalar_tensor_tensor(hT[:, j, :], outs[:, j, :], v_("g_out", l, j), st[:], ALU.mult,
                                                 ALU.mult).then_inc(s["merged"], 1)
                for q in range(KD):
                    dve.wait_ge(*step(l, "po_done", q + 1))
                    last = add_gated(l, GATE1, q, q % 2, s["po_free"])
                last.then_inc(s["x1_ready"], 1)
                dve.wait_ge(*step(l, "x1_ready", 1))
                norm_dve(2 * l + 1, l, SCALE2, SHIFT2)
                if l == 0:
                    dve.wait_ge(*step(l, "tail_out", 16 * 8))
                    for f in range(FT):
                        dve.wait_ge(ff_act, f + 1)
                        dve.tensor_tensor(two(G[:, f, :]), pp(2 * (f % 2) + 1), two(work[:, f % 2, :]), ALU.mult).then_inc(ff_free, 1)
                    for q in range(KD):
                        dve.wait_ge(fy_done, q + 1)
                        last = add_gated(l, GATE2, q, q % 4, fy_free)
                    last.then_inc(s["x2_ready"], 1)
                    dve.wait_ge(*step(l, "x2_ready", 1))

            link(dve.memset(lg[:], 0.0))
            dve.wait_ge(R["lg_tr"], 1)
            dve.tensor_copy(lg[:, 0:4, :], PP[1][:, 0, 0:4 * NE].rearrange("p (t e) -> p t e", t=4))
            link(dve.tensor_copy(lg[0:NS, 4, :], PP[1][0:NS, 0, 4 * NE:5 * NE]))
            for t in range(NT):
                last = dve.max(vmax[:, t, :], lg[:, t, :])
            link(last)
            for t in range(NT):
                last = dve.max_index(imax[:, t, :], vmax[:, t, :], lg[:, t, :])
            dve.tensor_tensor(gate[:, 0, :], vmax[:, :, 1], vmax[:, :, 0], ALU.subtract).then_inc(R["exp_d"], 1)
            link(last)
            link(dve.tensor_copy(imf[:], imax[:]))
            dve.wait_ge(R["const"], 3)
            for r in range(2):
                for t in range(NT):
                    last = dve.tensor_scalar(pick[:, r, t, :], eidx[:], imf[:, t, r:r + 1], valid[:, t:t + 1],
                                             ALU.is_equal, ALU.mult)
            link(last)
            dve.tensor_tensor(mask[:], pick[:, 0], pick[:, 1], ALU.add).then_inc(R["mask"], 1)
            dve.wait_ge(R["h_tr"], 1)
            dve.tensor_copy(stage[:, 0, :].rearrange("p (h n) -> p h n", h=2), PP[2][:]).then_inc(R["h_row"], 1)
            dve.wait_ge(R["pre"], 1)
            dve.tensor_copy(before[:], PP[0][:, 0, 0:NT * NE].rearrange("p (t e) -> p t e", t=NT))
            dve.tensor_copy(totals[:, 1:NT, :], PP[0][:, 1, 0:(NT - 1) * NE].rearrange("p (t e) -> p t e", t=NT - 1))
            link(dve.tensor_reduce(countf[:], PP[0][:, 1, 0:NT * NE].rearrange("p (t e) -> p e t", t=NT), AX.X, ALU.add))
            dve.tensor_copy(count[:], countf[:]).then_inc(R["count"], 1)
            for e in range(1, NE):
                link(dve.tensor_tensor(ebase[:, e:e + 1], ebase[:, e - 1:e], countf[:, e - 1:e], ALU.add))
            dve.tensor_copy(first[:], ebase[:]).then_inc(R["count"], 1)
            link(dve.tensor_copy(totals[:, 0, :], ebase[:]))
            for t in range(1, NT):
                link(dve.tensor_tensor(totals[:, t, :], totals[:, t, :], totals[:, t - 1, :], ALU.add))
            link(dve.tensor_tensor(before[:], before[:], totals[:], ALU.add))
            for r in range(2):
                last = dve.tensor_tensor(pick[:, r], pick[:, r], before[:], ALU.mult)
            link(last)
            link(dve.tensor_reduce(placef[:], pick[:], AX.X, ALU.add))
            dve.tensor_copy(place[:], placef[:]).then_inc(R["route"], 1)
            dve.wait_ge(R["gate"], 1)
            link(dve.tensor_scalar(gate[:, 0, :], gate[:, 1, :], 1.0, None, ALU.add))
            link(dve.reciprocal(gate[:, 0, :], gate[:, 0, :]))
            link(dve.tensor_tensor(gate[:, 1, :], gate[:, 1, :], gate[:, 0, :], ALU.mult))
            for t in range(1, NT):
                n = min(P, T - P * t)
                dve.wait_ge(R["h_tr"], t + 1)
                if t >= 3:
                    dve.wait_ge(Rout[t % 3], 32 * (t // 3))
                dve.tensor_copy(stage[0:n, t % 3, :].rearrange("p (h n) -> p h n", h=2), PP[2][0:n]).then_inc(R["h_row"], 1)

            dve.wait_ge(*step(1, "tail_out", 16 * 8))
            for b in range(3):
                dve.wait_ge(Rout[b], 32 * len(range(b, NT, 3)))
            dve.sem_inc(R["yt_ev"], 1)
            dve.sem_inc(R["f_free"], 2)
            dve.sem_inc(R["y_out"], 16)
            dve.wait_ge(R["count"], 2)
            with dve.Fori(0, NE) as e:
                c = tokens_of(dve, e)
                with dve.If(c <= NW):
                    dve.sem_inc(R["in_ev"], 1)
                    for t in range(2):
                        for h in range(2):
                            dve.wait_ge(R["in_tr"], NT * e + 2 * t + h + 2)
                            dve.tensor_copy(hn[:, 4 * h:4 * h + 4, P * t:P * t + P],
                                            PP[3][:, h, :].rearrange("p (a n) -> p a n", a=4)).then_inc(R["in_ev"], 1)
                    dve.sem_inc(R["yt_ev"], 1)
                    for f in range(ET):
                        dve.wait_ge(R["f_act"], ET * e + f + 1)
                        dve.tensor_tensor(Gn[:, f, :], PP[1][:, f % 2, 0:NW], hactn[:, f % 2, :], ALU.mult).then_inc(R["f_free"], 1)
                    dve.wait_ge(R["y_out"], 16 * NT * e + 16)
                    for h in range(2):
                        dve.wait_ge(R["yt_tr"], NT * e + h + 4)
                        for t in range(2):
                            dve.tensor_copy(yrow[:, t, 4 * P * h:4 * P * h + 4 * P], PP[3][:, t, :]).then_inc(R["yt_ev"], 1)
                with dve.Else():
                    for t in range(NT):
                        dve.wait_ge(R["in_tr"], NT * e + t + 1)
                        dve.tensor_copy(hexp[:, :, AT[t]:AT[t] + P].rearrange("p (h a) n -> p h a n", h=2),
                                        PP[3][:].rearrange("p h (a n) -> p h a n", a=4)).then_inc(R["in_ev"], 1)
                    for f in range(ET):
                        dve.wait_ge(R["f_act"], ET * e + f + 1)
                        dve.tensor_tensor(two(G[:, f, :]), pp(1), two(hact[:, f % 2, :]), ALU.mult).then_inc(R["f_free"], 1)
                    for t in range(NT):
                        dve.wait_ge(R["yt_tr"], NT * e + t + 1)
                        dve.wait_ge(R["y_out"], 16 * (NT * e + t) + 16)
                        dve.tensor_copy(stage[:, 2, :].rearrange("p (h n) -> p h n", h=2), PP[3][:]).then_inc(R["yt_ev"], 1)
            for t in range(NT):
                n = min(P, T - P * t)
                dve.wait_ge(Rback[0], 16 * (t + 1))
                dve.wait_ge(Rback[1], 16 * (t + 1))
                if t:
                    dve.wait_ge(R["fo_tr"], t)
                link(dve.tensor_scalar(stage[0:n, 2, :], stage[0:n, 0, :], gate[0:n, 0, t:t + 1], None, ALU.mult))
                dve.scalar_tensor_tensor(stage[0:n, 2, :], stage[0:n, 1, :], gate[0:n, 1, t:t + 1], stage[0:n, 2, :],
                                         ALU.mult, ALU.add).then_inc(R["f_row"], 1)
                if t < 4:
                    dve.wait_ge(R["fo_tr"], t + 1)
                    for j in range(KD):
                        c = slice(P * t, P * t + P)
                        last = dve.scalar_tensor_tensor(xT[:, j, c], PP[0][:, j // 4, (j % 4) * P:(j % 4) * P + P],
                                                        mod[:, 1, 8 * GATE2 + j, 0:1], xT[:, j, c], ALU.mult, ALU.add)
                    last.then_inc(R["fo_ev"], 1)
            dve.wait_ge(R["fo_tr"], NT)
            f4 = hT[:, :, SEQ:T]
            link(dve.tensor_tensor(f4.rearrange("p (h a) n -> p h a n", h=2),
                                   PP[0][:].rearrange("p h (a n) -> p h a n", a=4)[:, :, :, 0:NS],
                                   mod[:, 1, 8 * GATE2:8 * GATE2 + 8, 1:NQ].rearrange("p (h a) n -> p h a n", h=2), ALU.mult))
            dve.tensor_tensor(xT[:, :, SEQ:T], xT[:, :, SEQ:T], f4, ALU.add).then_inc(R["x_ready"], 1)
            dve.wait_ge(R["x_ready"], 1)
            norm_dve(4, 1, None, None)
            for t in range(NT):
                n = min(P, T - P * t)
                dve.wait_ge(fin_tr, t + 1)
                dve.tensor_copy(xin[0:n, t, :].rearrange("p (h n) -> p h n", h=2), PP[t % 2][0:n]).then_inc(fin_ev, 1)


_INS = ["x_prompt", "x_sample", "state_conv_a", "state_conv_c", "state_pool_d", "c_prompt", "c_sample", "w_ada", "b_ada",
        "g_mix", "w_in", "conv_a_w", "ln_v_g", "ln_v_b", "w_s", "b_s", "conv_c_w", "conv_c_b", "ln_c_g", "ln_c_b",
        "pool_w", "pool_scale", "g_out", "w_out", "g_ffn", "w1_dense", "w3_dense", "w2_dense", "w_router", "b_router",
        "w1_moe", "w3_moe", "w2_moe", "g_final"]
_OUTS = [("y_prompt", (1, SEQ, D)), ("y_sample", (NS, 1, D)),
         ("a_p", (DEPTH, 1, 2, W)), ("c_p", (DEPTH, 1, 30, W)), ("d_p", (DEPTH, 1, 15, W)), ("v_p", (DEPTH, 1, P, W)),
         ("a_s", (DEPTH, NS, 2, W)), ("c_s", (DEPTH, NS, 30, W)), ("d_s", (DEPTH, NS, 15, W)), ("v_s", (DEPTH, NS, 1, W))]


def kernel(**inputs):
    import numpy as _np
    import concourse.bacc as _bacc
    from concourse.bass_utils import run_bass_kernel_spmd as _run

    nc = _bacc.Bacc("TRN2", target_bir_lowering=False, num_devices=1)
    arrays, A, O = {}, {}, {}
    for name in _INS:
        a = _np.ascontiguousarray(inputs[name])
        arrays[f"in_{name}"] = a
        A[name] = nc.dram_tensor(f"in_{name}", a.shape, F32, kind="ExternalInput").ap()
    for name, shape in _OUTS:
        O[name] = nc.dram_tensor(f"out_{name}", shape, F32, kind="ExternalOutput").ap()
    trunk_program(nc, A, O)
    r = _run(nc, [arrays], core_ids=[0])
    return tuple(r.results[0][f"out_{name}"] for name, _ in _OUTS)
```

```python
from contextlib import ExitStack

import concourse.bass as bass
from concourse import mybir

F32 = mybir.dt.float32
I32 = mybir.dt.int32
U32 = mybir.dt.uint32
ALU = mybir.AluOpType
ACT = mybir.ActivationFunctionType
AX = mybir.AxisListType

P = 128
D = 1024
KD = D // P
SEQ = 512
NS = 8
T = SEQ + NS
HT = T // 2
NQ = 1 + NS
DEPTH = 2
W = 256
TAPS_A, TAPS_C, POOL = 3, 31, 16
FF = 2816
FE = 1408
NE = 8
EPS = 1e-6
RING = 6
SLOT = KD * 384
NT = (T + P - 1) // P
AT = [0, 128, 256, 384, T - P]
PICKS = 2 * T
ROOM = PICKS + T
NW = 2 * P
WIDTHS = [128, 144, 160, 192, 224, NW]

A_B, A_C, A_H, B_U, B_V, C_A, C_G, D_P = range(8)
ORDER = [C_G, C_A, B_V, D_P, A_H, A_C, B_U, A_B]
HOME = {C_G: 0, B_V: 2, A_H: 4, B_U: 6, A_B: 8}

ROWS, _at = {}, 0
for _name, _n in [("g_mix", 8), ("ln_v_g", 2), ("ln_v_b", 2), ("conv_c_b", 2), ("ln_c_g", 2), ("ln_c_b", 2),
                  ("pool_scale", 2), ("g_out", 8), ("g_ffn", 8), ("conv_a_w", 2 * TAPS_A), ("conv_c_w", 2 * TAPS_C),
                  ("g_final", 8)]:
    ROWS[_name] = (_at, _n)
    _at += _n
NROWS = _at

TAIL = [TAPS_A - 1, TAPS_C - 1, POOL - 1, NS, NS, NS, NS]

SHIFT1, SCALE1, GATE1, SHIFT2, SCALE2, GATE2 = range(6)

ADA0 = 0
WIN0 = ADA0 + 24 * DEPTH
WOUT0 = WIN0 + 8
DENSE = WOUT0 + 4
DENSE2 = DENSE + 16
WIN1 = DENSE2 + 8
WOUT1 = WIN1 + 8
MOE = WOUT1 + 4
PER_E = 12
FT = FF // P
ET = FE // P


def trunk_program(nc, A, O):
    ctx = ExitStack()
    with ctx:
        def sb(name, shape, dt=F32):
            return ctx.enter_context(nc.sbuf_tensor(name, shape, dt))

        def sem(name):
            return ctx.enter_context(nc.semaphore(name))

        ring = sb("ring", [P, RING, SLOT])
        xT = sb("xT", [P, KD, T])
        hT = sb("hT", [P, KD, T])
        work = sb("work", [P, KD, T])
        big = sb("big", [P, 11440])
        stage = sb("stage", [P, 3, D])
        vec = sb("vec", [P, DEPTH, NROWS])
        bada = sb("bada", [P, DEPTH * 48])
        mod = sb("mod", [P, DEPTH, 48, NQ])
        cT = sb("cT", [P, KD, NQ])
        ident = sb("ident", [P, P])
        ones = sb("ones", [P, P])
        eps = sb("eps", [P, 1])
        wrt = sb("wrt", [P, KD, NE])
        brt = sb("brt", [NE, 1])
        win = sb("win", [P, 2])
        winv = sb("winv", [P, 2])
        cinv = sb("cinv", [P, 2, POOL])
        flat = stage[:, :, :].rearrange("p a n -> p (a n)")

        def cut(src, at, *shape):
            n = 1
            for s in shape:
                n *= s
            v = src[:, at:at + n]
            if len(shape) == 2:
                v = v.rearrange("p (a b) -> p a b", a=shape[0])
            if len(shape) == 3:
                v = v.rearrange("p (a b c) -> p a b c", a=shape[0], b=shape[1])
            return v

        ws_raw = cut(flat, 0, 4, P)
        bsb = cut(flat, 512, 2, P)
        bd = cut(flat, 768, 2, P)
        stA = cut(flat, 1024, W)
        stC = cut(flat, 1280, 2, W)
        stD = cut(flat, 1792, W)
        wsT = cut(flat, 2048, 4, P)
        ws00 = sb("ws00", [P, 2])
        hisA = sb("hisA", [P, 2, NS, TAPS_A])
        hisC = sb("hisC", [P, 2, NS, TAPS_C])
        hisD = sb("hisD", [P, 2, NS, POOL])
        head16 = sb("head16", [P, 2, POOL])
        tapC = sb("tapC", [P, NS, TAPS_C])
        small = sb("small", [P, 2, NS])
        stat = sb("stat", [P, T])
        stat2 = sb("stat2", [P, T])
        lg = sb("lg", [P, NT, NE])
        vmax = sb("vmax", [P, NT, 8])
        imax = sb("imax", [P, NT, 8], U32)
        imf = sb("imf", [P, NT, 8])
        pick = sb("pick", [P, 2, NT, NE])
        mask = sb("mask", [P, NT, NE])
        before = sb("before", [P, NT, NE])
        totals = sb("totals", [P, NT, NE])
        tri = sb("tri", [P, P])
        eidx = sb("eidx", [P, NE])
        ebase = sb("ebase", [P, NE])
        valid = sb("valid", [P, NT])
        placef = sb("placef", [P, 2, NT])
        place = sb("place", [P, 2, NT], U32)
        gate = sb("gate", [P, 2, NT])
        ss = sb("ss", [P, NT])
        countf = sb("countf", [P, NE])
        count = sb("count", [P, NE], I32)
        first = sb("first", [P, NE], I32)
        modrow = sb("modrow", [P, 2, 256])

        xin = cut(big, 0, NT, D)
        rows = cut(big, 5 * D, 4, P)
        crow = cut(big, 5 * D + 4 * P, D)
        proj = cut(big, 0, 10, T)
        zin = cut(big, 10 * T, 2, TAPS_A - 1 + T)
        gin = cut(big, 10 * T + 2 * (2 + T), 2, TAPS_C - 1 + T)
        pin = cut(big, 10 * T + 2 * (32 + 2 * T), 2, POOL - 1 + T)
        DAT = 10 * T + 2 * (47 + 3 * T)
        pa = cut(big, DAT, 2, POOL - 1 + T)
        pb = cut(big, DAT + 2 * (15 + T), 2, POOL - 1 + T)
        outrow = cut(big, DAT, 7, W)
        vtok = cut(big, HOME[A_H] * T, 4, W)
        G = cut(big, 0, 22, T)
        hexp = cut(big, 11 * T, KD, T)
        hact = cut(big, 19 * T, 2, T)
        Gn = cut(big, 0, ET, NW)
        hn = cut(big, 11 * T, KD, NW)
        hactn = cut(big, 19 * T, 2, NW)
        wflat = work[:, :, :].rearrange("p k n -> p (k n)")
        yn = cut(wflat, 0, KD, NW)
        yrow = cut(wflat, KD * NW, 2, D)
        yg = ring[:, 0:NT, 0:2 * D].rearrange("p t (r n) -> p t r n", r=2)
        hflat = hT[:, :, :].rearrange("p k n -> p (k n)")
        gate_p, gate_s, gf, diag = (cut(hflat, i * D, D) for i in range(4))
        outs = work
        lgT = stat2[0:NE]

        PP = [ctx.enter_context(nc.psum_tensor(f"PP{q}", [P, 2, 512], F32)) for q in range(4)]

        Hd = nc.dram_tensor("h_by_expert", (ROOM, D), F32).ap()
        Yd = nc.dram_tensor("y_by_expert", (ROOM, D), F32).ap()

        def v_(name, l, j):
            return vec[:, l, ROWS[name][0] + j:ROWS[name][0] + j + 1]

        def tail_bank(n):
            return PP[3 - n // 4][:, n % 4 // 2, (n % 2) * W:(n % 2) * W + W]

        def pp(q, n=HT):
            return PP[q][:, :, 0:n]

        def two(ap):
            return ap.rearrange("p (h n) -> p h n", h=2)

        full = [sem(f"slot_full{s}") for s in range(RING)]
        const_ready = sem("const_ready")
        const_dve = sem("const_dve")
        x_in = sem("x_in")
        vec_in = sem("vec_in")
        c_in = sem("c_in")
        b_in = sem("b_in")
        wr_in = sem("wr_in")
        silu_c = sem("silu_c")
        pro_tr = sem("pro_tr")
        pro_act = sem("pro_act")
        pro_dve = sem("pro_dve")
        ada_mm = sem("ada_mm")
        ada_row = sem("ada_row")
        ada_tr = sem("ada_tr")
        ada_out = sem("ada_out")
        mod_ready = sem("mod_ready")
        dchain = sem("dve_order")
        achain = sem("act_order")
        gchain = sem("pool_order")
        stored = sem("stored")
        STEPS = {"mx_in": 256, "ws_tr": 1, "ws_copy": 1, "ws_masked": 1, "st_tr": 1, "st_copy": 3, "hist_zero": 1,
                 "pj_done": 16, "pj_free0": 8, "pj_free1": 8, "conv_tap": 2 * TAPS_C, "lnc_in": 1, "vxc": 2, "lnc_xc": 2,
                 "lnb_sum": 1, "lnb_sq": 2, "lnb_var": 1, "lnb_root": 1, "lnc_sum": 1, "lnc_sq": 2, "lnc_var": 1,
                 "lnc_root": 1, "lnc_hat": 2, "pool_out": 1, "pooled": 1, "pool_mm": 2, "pool_free": 1, "vn_ready": 2,
                 "vt_tr": 1, "vt_copy": 1, "mix_done": 1, "mix_read": 1, "gA": 2, "gB": 2, "gC": 2, "gD": 2,
                 "g_sq": 8, "g_sum": 4, "g_root": 4, "merged": 8, "po_done": 8, "po_free": 8,
                 "tail_tr": 7, "tail_copy": 7, "tail_out": 128}
        s = {name: sem(name) for name in STEPS}

        def step(l, name, n):
            return s[name], STEPS[name] * l + n

        NORM_STEPS = {"up": KD, "sq": KD, "sum": 1, "root": 1, "xhat": KD, "h": KD, "hs": 1}
        ns = {k: sem(f"norm_{k}") for k in NORM_STEPS}

        def norm_step(tag, k, n):
            return ns[k], NORM_STEPS[k] * tag + n

        ff_done, ff_act, ff_free = sem("ff_done"), sem("ff_act"), sem("ff_free")
        fy_done, fy_free = sem("fy_done"), sem("fy_free")
        R = {k: sem(f"moe_{k}") for k in ["lg", "lg_ev", "lg_tr", "idx", "mask", "pre", "route", "gate",
                                          "zero", "h_tr", "h_row", "h_in", "in_tr", "in_ev",
                                          "f_done", "f_act", "f_free", "y_done", "y_free", "yt_tr", "yt_ev",
                                          "y_out", "count", "exp_d", "diag", "g_mm", "g_ev", "x_tr", "x_ev",
                                          "ya", "ss", "ssr", "const"]}
        Rout = [sem(f"moe_rows_out{s}") for s in range(3)]
        Rwide = [sem(f"moe_wide_in{t}") for t in range(2, NT)]
        Rin = [sem(f"moe_in{s}") for s in range(2)]
        Rback = [[sem(f"moe_back{t}_{r}") for r in range(2)] for t in range(NT)]
        gf_in = sem("gf_in")
        fin_ev, fin_out = sem("fin_ev"), sem("fin_out")

        def slot(n, k, cols):
            return ring[:, n % RING, 0:k * cols].rearrange("p (k n) -> p k n", k=k)

        def tokens_of(eng, e):
            return eng.value_load(count[0:1, bass.ds(e, 1)], min_val=0, max_val=T)

        def first_of(eng, e):
            return eng.value_load(first[0:1, bass.ds(e, 1)], min_val=0, max_val=PICKS)

        w_in_v = [A["w_in"][l].rearrange("(k p) (b n) -> b p k n", p=P, n=256) for l in range(DEPTH)]
        w_out_v = [A["w_out"][l].rearrange("(k p) (b n) -> b p k n", p=P, n=256) for l in range(DEPTH)]
        w_ada_v = [A["w_ada"][l].rearrange("(k p) (b n) -> b p k n", p=P, n=256) for l in range(DEPTH)]
        w1_v = A["w1_dense"][0].rearrange("(k p) n -> p k n", p=P)
        w3_v = A["w3_dense"][0].rearrange("(k p) n -> p k n", p=P)
        w2_v = A["w2_dense"][0].rearrange("(g k p) (b n) -> b g p k n", g=2, p=P, n=256)

        def expert_chunk(e, j):
            if j < 8:
                w = A["w1_moe" if j % 2 == 0 else "w3_moe"][0]
                n = P * min(3, ET - 3 * (j // 2))
                return w[e].rearrange("(k p) n -> p k n", p=P)[:, :, (j // 2) * 384:(j // 2) * 384 + n], KD, n
            return A["w2_moe"][0][e].rearrange("(k p) n -> p k n", p=P)[:, :, (j - 8) * 256:(j - 7) * 256], ET, 256

        def chunk(n):
            if n < WIN0:
                return w_ada_v[n // 24][n % 24], KD, 256
            for base, v in ((WIN0, w_in_v[0]), (WIN1, w_in_v[1])):
                if base <= n < base + 8:
                    return v[ORDER[n - base]], KD, 256
            for base, v in ((WOUT0, w_out_v[0]), (WOUT1, w_out_v[1])):
                if base <= n < base + 4:
                    return v[n - base], KD, 256
            if n < DENSE2:
                c = (n - DENSE) // 2
                m = P * min(3, FT - 3 * c)
                return (w1_v, w3_v)[(n - DENSE) % 2][:, :, 384 * c:384 * c + m], KD, m
            return w2_v[(n - DENSE2) // 2][(n - DENSE2) % 2], 11, 256

        def released(n):
            if n < WIN0:
                return ada_mm, n + 1
            for l, base in ((0, WIN0), (1, WIN1)):
                if base <= n < base + 8:
                    return step(l, "pj_done", 2 * (n - base) + 2)
            for l, base in ((0, WOUT0), (1, WOUT1)):
                if base <= n < base + 4:
                    return step(l, "po_done", 2 * (n - base) + 2)
            if n < DENSE2:
                return ff_done, min(3 * ((n - DENSE) // 2) + 3, FT)
            return fy_done, 2 * ((n - DENSE2) // 2) + 2

        block = ctx.enter_context(nc.Block())

        @block.sync
        def _(sp):
            def load(n, src):
                ap, k, cols = src
                sp.dma_start(slot(n, k, cols), ap).then_inc(full[n % RING], 16)

            for n in range(RING):
                load(n, chunk(n))
            for l in range(DEPTH):
                with sp.Fori(0, 24 // RING - 1) as i:
                    for j in range(RING):
                        used = sp.snap(sp.to_reg(24 * l + RING * i + j + 1))
                        sp.wait_ge(const_ready, 1)
                        sp.wait_ge(ada_mm, used)
                        load(j, (w_ada_v[l][RING * i + RING + j], KD, 256))
                for j in range(RING):
                    sp.wait_ge(ada_mm, 24 * l + 24 - RING + j + 1)
                    load(j, chunk(24 * (l + 1) + j))
            for n in range(WIN0, MOE):
                sp.wait_ge(*released(n))
                load(n + RING, chunk(n + RING) if n + RING < MOE else expert_chunk(0, n + RING - MOE))

            def used(e, j):
                if j < 8:
                    return R["f_done"], ET * e + min(3 * (j // 2) + 3, ET)
                return R["y_done"], KD * e + 2 * (j - 8) + 2

            def first_rows(e):
                row = first_of(sp, e)
                for t in range(2):
                    sp.dma_start(stage[:, t, :], Hd[bass.ds(row + P * t, P), :]).then_inc(Rin[t], 16)

            def rest_of_rows(e):
                c, row = tokens_of(sp, e), first_of(sp, e)
                with sp.If(c <= NW):
                    for t in range(2, NT):
                        sp.sem_inc(Rwide[t - 2], 16)
                with sp.Else():
                    for t in range(2, NT):
                        free = sp.snap(sp.to_reg(NT * e + t - 1))
                        sp.wait_ge(const_ready, 1)
                        sp.wait_ge(R["in_tr"], free)
                        sp.dma_start(stage[:, t % 2, :], Hd[bass.ds(row + AT[t], P), :]).then_inc(Rwide[t - 2], 16)

            def rows_out(e):
                c, row = tokens_of(sp, e), first_of(sp, e)
                with sp.If(c <= NW):
                    sp.sem_inc(R["y_out"], 16 * (NT - 2))
                    for t in range(2):
                        there = sp.snap(sp.to_reg(NT * e + NT + t))
                        sp.wait_ge(const_ready, 1)
                        sp.wait_ge(R["yt_ev"], there)
                        sp.dma_start(Yd[bass.ds(row + P * t, P), :], yrow[:, t, :]).then_inc(R["y_out"], 16)
                with sp.Else():
                    for t in range(NT):
                        there = sp.snap(sp.to_reg(NT * e + t + 2))
                        sp.wait_ge(const_ready, 1)
                        sp.wait_ge(R["yt_ev"], there)
                        sp.dma_start(Yd[bass.ds(row + AT[t], P), :], stage[:, 2, :]).then_inc(R["y_out"], 16)

            for b in range(3):
                sp.wait_ge(Rout[b], 32 * len(range(b, NT, 3)))
            sp.wait_ge(R["count"], 2)
            first_rows(0)
            with sp.Fori(0, NE - 1) as e:
                rest_of_rows(e)
                free = sp.snap(sp.to_reg(NT * e + NT))
                sp.wait_ge(const_ready, 1)
                sp.wait_ge(R["in_tr"], free)
                first_rows(e + 1)
                for j in range(PER_E):
                    which, n = used(e, j)
                    n = sp.snap(sp.to_reg(n))
                    sp.wait_ge(const_ready, 1)
                    sp.wait_ge(which, n)
                    load(MOE + j + RING, expert_chunk(e, j + RING) if j < PER_E - RING else expert_chunk(e + 1, j + RING - PER_E))
                rows_out(e)
            last = sp.snap(sp.to_reg(NE - 1))
            rest_of_rows(last)
            for j in range(PER_E - RING):
                sp.wait_ge(*used(NE - 1, j))
                load(MOE + j + RING, expert_chunk(NE - 1, j + RING))
            rows_out(last)
            for t in range(NT):
                n = min(P, T - P * t)
                sp.wait_ge(fin_ev, t + 1)
                dst = O["y_prompt"][0, P * t:P * t + n, :] if t < 4 else O["y_sample"].rearrange("b s d -> (b s) d")
                sp.dma_start(dst, yg[0:n, t, 1, :]).then_inc(fin_out, 16)
            sp.wait_ge(fin_out, 16 * NT)
            sp.wait_ge(stored, 16 * 3 * DEPTH)
            for l in range(DEPTH):
                sp.wait_ge(*step(l, "tail_out", 16 * 8))

        @block.gpsimd
        def _(pool):
            order = [0]

            def link(ins):
                order[0] += 1
                ins.then_inc(gchain, 1)
                pool.wait_ge(gchain, order[0])

            link(pool.memset(modrow[:], 0.0))
            link(pool.memset(ident[:], 0.0))
            pool.affine_select(out=ident[:], in_=ident[:], compare_op=ALU.not_equal, fill=1.0, base=0,
                               pattern=[[-1, P]], channel_multiplier=1).then_inc(const_ready, 1)
            pool.iota(cinv[:], pattern=[[0, 2], [1, POOL]], base=1, channel_multiplier=0,
                      allow_small_or_imprecise_dtypes=True).then_inc(const_ready, 1)
            link(pool.memset(tri[:], 1.0))
            link(pool.memset(valid[:], 1.0))
            link(pool.memset(valid[:, NT - 1:NT], 0.0))
            pool.memset(valid[0:NS, NT - 1:NT], 1.0)
            pool.affine_select(out=tri[:], in_=tri[:], compare_op=ALU.is_gt, fill=0.0, base=0,
                               pattern=[[1, P]], channel_multiplier=-1).then_inc(R["const"], 1)
            pool.iota(eidx[:], pattern=[[1, NE]], base=0, channel_multiplier=0,
                      allow_small_or_imprecise_dtypes=True).then_inc(R["const"], 1)
            pool.memset(ebase[:], 0.0).then_inc(R["const"], 1)

            for l in range(DEPTH):
                for name, (at, n) in ROWS.items():
                    src = A[name] if name == "g_final" else A[name][l]
                    if name in ("g_out", "conv_a_w", "conv_c_w"):
                        src = src.rearrange("a (r p) -> (a r) p", p=P)
                    else:
                        src = src.rearrange("(r p) -> r p", p=P)
                    pool.dma_start(rows[at:at + n, l, :], src).then_inc(vec_in, 16)
            for t in range(4):
                pool.dma_start(xin[:, t, :], A["x_prompt"][0, P * t:P * t + P, :]).then_inc(x_in, 16)
            pool.dma_start(xin[0:NS, 4, :], A["x_sample"].rearrange("b s d -> (b s) d")).then_inc(x_in, 16)

            for l in range(DEPTH):
                if l:
                    pool.wait_ge(*norm_step(2 * l - 1, "up", KD))
                    link(pool.memset(stage[0:T // 5, 0, :], 0.0))
                    pool.dma_start(Hd[PICKS:ROOM].rearrange("(a p) n -> p a n", a=5),
                                   stage[0:T // 5, 0:1, :].to_broadcast([T // 5, 5, D])).then_inc(R["zero"], 16)
                    pool.wait_ge(R["zero"], 16)
                pool.dma_start(ws_raw, A["w_s"][l].rearrange("h t s -> t h s")).then_inc(s["mx_in"], 16)
                for h in range(4):
                    r = slice(64 * (h % 2), 64 * (h % 2) + 64)
                    pool.dma_start(bsb[r, h // 2, :], A["b_s"][l, h:h + 1, :].to_broadcast([64, P])).then_inc(s["mx_in"], 16)
                    pool.dma_start(ws00[r, h // 2:h // 2 + 1], A["w_s"][l, h, 0:1, 0:1].to_broadcast([64, 1])).then_inc(s["mx_in"], 16)
                link(pool.memset(bd, 0.0))
                for g in range(4):
                    r = slice(64 * (g % 2), 64 * (g % 2) + 64)
                    pool.dma_start(bd[r, g // 2, r], A["pool_w"][l, g]).then_inc(s["mx_in"], 16)
                pool.dma_start(stA[0:2 * NS], A["state_conv_a"][l].rearrange("b r c -> (b r) c")).then_inc(s["mx_in"], 16)
                pool.dma_start(stC[0:120], A["state_conv_c"][l].rearrange("(g b) r c -> (b r) g c", g=2)).then_inc(s["mx_in"], 16)
                pool.dma_start(stD[0:120], A["state_pool_d"][l].rearrange("b r c -> (b r) c")).then_inc(s["mx_in"], 16)
                pool.dma_start(O["a_s"][l, :, 0:1, :], A["state_conv_a"][l, :, 1:2, :]).then_inc(stored, 16)
                pool.dma_start(O["c_s"][l, :, 0:29, :], A["state_conv_c"][l, :, 1:30, :]).then_inc(stored, 16)
                pool.dma_start(O["d_s"][l, :, 0:14, :], A["state_pool_d"][l, :, 1:15, :]).then_inc(stored, 16)
                if l == 0:
                    pool.wait_ge(pro_tr, 12)
                else:
                    pool.wait_ge(fy_done, KD)
                pool.memset(zin[:, :, 0:TAPS_A - 1], 0.0)
                pool.memset(gin[:, :, 0:TAPS_C - 1], 0.0)
                pool.memset(pin[:, :, 0:POOL - 1], 0.0).then_inc(s["hist_zero"], 1)
                pool.wait_ge(*step(l, "ws_copy", 1))
                pool.affine_select(out=wsT, in_=wsT, compare_op=ALU.is_ge, fill=0.0, base=0,
                                   pattern=[[0, 4], [1, P]], channel_multiplier=-1).then_inc(s["ws_masked"], 1)
                pool.wait_ge(*step(l, "pj_free0", 4))
                pool.wait_ge(*step(l, "pj_free1", 4))
                lo, hi, n = slice(0, 64), slice(64, P), SEQ + 15

                def doubled(dst, src, back, a):
                    return pool.tensor_tensor(dst[..., a:n], src[..., a:n], src[..., a - back:n - back], ALU.add)

                def last(dst_rows, ct, src, back):
                    return pool.tensor_tensor(outs[dst_rows, 6 + ct, 0:SEQ], src[dst_rows, ct, 15:n],
                                              src[dst_rows, ct, 15 - back:n - back], ALU.add)
                link(doubled(pa, pin, 1, 1))
                link(last(lo, 0, pin, 1))
                link(last(hi, 0, pa, 2))
                link(doubled(pb[:, 1], pa[:, 1], 2, 3))
                link(last(lo, 1, pb, 4))
                link(doubled(pa[:, 1], pb[:, 1], 4, 7))
                last(hi, 1, pa, 8).then_inc(s["pool_out"], 1)
                pool.wait_ge(*step(l, "vt_copy", 1))
                pool.dma_start(O["v_p"][l, 0], vtok[:, 3, :]).then_inc(s["tail_out"], 16)
                for n, dst in enumerate([O["a_p"][l, 0], O["c_p"][l, 0], O["d_p"][l, 0], O["a_s"][l, :, 1, :],
                                         O["c_s"][l, :, 29, :], O["d_s"][l, :, 14, :], O["v_s"][l, :, 0, :]]):
                    pool.wait_ge(*step(l, "tail_copy", n + 1))
                    pool.dma_start(dst, outrow[0:TAIL[n], n, :]).then_inc(s["tail_out"], 16)
            pool.wait_ge(R["zero"], 16)
            for t in range(NT):
                n = min(P, T - P * t)
                pool.wait_ge(R["h_row"], t + 1)
                pool.wait_ge(R["route"], 1)
                for r in range(2):
                    pool.indirect_dma_start(Hd, bass.IndirectOffsetOnAxis(ap=place[0:n, r, t:t + 1], axis=0),
                                            stage[0:n, t % 3, :], None).then_inc(Rout[t % 3], 16)
            for b in range(3):
                pool.wait_ge(Rout[b], 32 * len(range(b, NT, 3)))
            pool.wait_ge(R["y_out"], 16 * NE * NT + 16)
            pool.wait_ge(R["y_done"], NE * KD)
            for t in range(NT):
                n = min(P, T - P * t)
                for r in range(2):
                    pool.indirect_dma_start(yg[0:n, t, r, :], None, Yd[0:PICKS],
                                            bass.IndirectOffsetOnAxis(ap=place[0:n, r, t:t + 1], axis=0)).then_inc(Rback[t][r], 16)

        NVEC = 12 * DEPTH
        XB = [2, 3, 0, 1, 2]
        YB = [0, 1, 3]
        GO = [0, 2, 3, 1]
        READY = {0: "gA", 1: "gB", 2: "gC", 3: "gD"}

        @block.tensor
        def _(pe):
            def gemm(q, lhs, rhs, kn):
                for k in range(kn):
                    for h in range(2):
                        mm = pe.matmul(PP[q][:, h, 0:HT], lhs(k), rhs(k)[:, HT * h:HT * h + HT],
                                       start=(k == 0), stop=(k == kn - 1))
                return mm

            def channel_sum(q, tiles):
                return gemm(q, lambda k: ones[:], lambda k: tiles[k], len(tiles))

            def norm_sum(tag, j):
                pe.wait_ge(*norm_step(tag, "sq", j + 1))
                for h in range(2):
                    mm = pe.matmul(PP[2][:, h, 0:HT], ones[:], work[:, j, HT * h:HT * h + HT],
                                   start=(j == 0), stop=(j == KD - 1))
                if j == KD - 1:
                    mm.then_inc(ns["sum"], 1)

            def gemm_h(q, lhs, tag):
                pe.wait_ge(*norm_step(tag, "hs", 1))
                for k in range(KD):
                    pe.wait_ge(*norm_step(tag, "h", k + 1))
                    for h in range(2):
                        mm = pe.matmul(PP[q][:, h, 0:HT], lhs(k), hT[:, k, HT * h:HT * h + HT],
                                       start=(k == 0), stop=(k == KD - 1))
                return mm

            def arrived(n):
                pe.wait_ge(full[n % RING], 16 * (n // RING + 1))

            pe.wait_ge(const_ready, 1)
            pe.wait_ge(silu_c, 1)
            for j in range(KD):
                tr = pe.transpose(PP[3][:, 0, j * NQ:(j + 1) * NQ], crow[0:NQ, j * P:(j + 1) * P], ident[0:NQ, 0:NQ])
            tr.then_inc(pro_tr, 1)
            pe.wait_ge(b_in, 16)
            pe.transpose(PP[2][:, 1, 0:96], rows[0:96, 2, :], ident[0:96, 0:96]).then_inc(pro_tr, 1)
            pe.wait_ge(pro_dve, 1)
            pe.sem_inc(ada_tr, 2)
            for l in range(DEPTH):
                with pe.Fori(0, 24 // RING) as i:
                    def turned(g):
                        n = 8 * l + 2 * i + g
                        pe.wait_ge(ada_row, 24 * l + RING * i + 3 * g + 5)
                        pe.wait_ge(ada_out, n + 1)
                        for m in range(2):
                            tr = pe.transpose(PP[1][:, g, m * P:(m + 1) * P], modrow[:, g, m * P:(m + 1) * P], ident[:])
                        tr.then_inc(ada_tr, 1)
                    for j in range(RING):
                        pe.wait_ge(full[j], 16 * (24 // RING * l + i + 1))
                        pe.wait_ge(ada_row, 24 * l + RING * i + j + 1)
                        for k in range(KD):
                            mm = pe.matmul(PP[0][0:NQ, j % 2, 0:256], cT[:, k, :], slot(j, KD, 256)[:, k, :],
                                           start=(k == 0), stop=(k == KD - 1))
                        mm.then_inc(ada_mm, 1)
                        if j == 3:
                            turned(0)
                    turned(1)
                if l == 0:
                    pe.wait_ge(vec_in, 16 * NVEC)
                    pe.wait_ge(pro_dve, 2)
                    for v in range(DEPTH):
                        tr = pe.transpose(PP[3][:, 0, v * NROWS:(v + 1) * NROWS], rows[0:NROWS, v, :], ident[0:NROWS, 0:NROWS])
                    tr.then_inc(pro_tr, 1)
                    pe.wait_ge(x_in, 16 * NT)
                    for j in range(KD):
                        if j >= 2:
                            pe.wait_ge(*((pro_dve, 3 + j // 2) if j % 2 == 0 else (pro_act, j // 2)))
                        for v in range(4):
                            tr = pe.transpose(PP[2][:, j % 2, v * P:(v + 1) * P], xin[:, v, j * P:(j + 1) * P], ident[:])
                        tr.then_inc(pro_tr, 1)
                    for j in range(KD):
                        tr = pe.transpose(PP[3][:, 1, j * NS:(j + 1) * NS], xin[0:NS, 4, j * P:(j + 1) * P], ident[0:NS, 0:NS])
                    tr.then_inc(pro_tr, 1)

            for l in range(DEPTH):
                pe.wait_ge(*step(l, "mx_in", 16 * 16))
                if l:
                    pe.wait_ge(fy_free, KD - 1)
                else:
                    pe.wait_ge(pro_dve, 8)
                    pe.wait_ge(pro_act, 4)
                for h in range(4):
                    tr = pe.transpose(PP[3][:, 0, h * P:(h + 1) * P], ws_raw[:, h, :], ident[:])
                tr.then_inc(s["ws_tr"], 1)
                for ct in range(2):
                    c = slice(ct * P, ct * P + P)
                    pe.transpose(PP[3][:, 1, 16 * ct:16 * ct + 16], stA[0:16, c], ident[0:16, 0:16])
                    for g in range(2):
                        at = 32 + 240 * ct + 120 * g
                        pe.transpose(PP[3][:, 1, at:at + 120], stC[0:120, g, c], ident[0:120, 0:120])
                    tr = pe.transpose(PP[0][:, 0, 120 * ct:120 * ct + 120], stD[0:120, c], ident[0:120, 0:120])
                tr.then_inc(s["st_tr"], 1)
                for j in range(KD) if l == 0 else (KD - 1,):
                    norm_sum(2 * l, j)
                for q in range(16):
                    n = (WIN0, WIN1)[l] + q // 2
                    if q % 2 == 0:
                        arrived(n)
                    if q >= 2:
                        pe.wait_ge(*step(l, f"pj_free{q % 2}", q // 2))
                    lhs = lambda k: slot(n, KD, 256)[:, k, P * (q % 2):P * (q % 2) + P]
                    if q == 0:
                        pe.wait_ge(*step(l, "st_copy", 3))
                    mm = gemm_h(q % 2, lhs, 2 * l) if q == 0 else gemm(q % 2, lhs, lambda k: hT[:, k, :], KD)
                    mm.then_inc(s["pj_done"], 1)
                    if q == 11:
                        pe.wait_ge(*step(l, "pj_free0", 3))
                        pe.wait_ge(*step(l, "pj_free1", 3))
                        channel_sum(2, [proj[:, HOME[B_V] + ct, :] for ct in range(2)]).then_inc(s["lnb_sum"], 1)
                        pe.wait_ge(*step(l, "lnc_in", 1))
                        channel_sum(3, [outs[:, 4 + ct, :] for ct in range(2)]).then_inc(s["lnc_sum"], 1)
                    if q == 13:
                        pe.wait_ge(*step(l, "lnb_sq", 2))
                        channel_sum(2, [proj[:, HOME[C_G] + ct, :] for ct in range(2)]).then_inc(s["lnb_var"], 1)
                        pe.wait_ge(*step(l, "lnc_sq", 2))
                        channel_sum(3, [proj[:, HOME[A_H] + ct, :] for ct in range(2)]).then_inc(s["lnc_var"], 1)
                pe.wait_ge(*step(l, "vn_ready", 2))
                pe.wait_ge(*step(l, "lnc_root", 1))
                for n in range(4):
                    for ct in range(2):
                        tr = pe.transpose(PP[3][:, n // 2, (n % 2) * W + ct * P:(n % 2) * W + ct * P + P],
                                          proj[:, HOME[B_V] + ct, n * P:(n + 1) * P], ident[:])
                tr.then_inc(s["vt_tr"], 1)
                pe.wait_ge(*step(l, "vt_copy", 1))
                pe.wait_ge(*step(l, "ws_masked", 1))
                pe.wait_ge(*step(l, "pj_free0", 8))
                pe.wait_ge(*step(l, "pj_free1", 8))
                for n in range(4):
                    for ct in range(2):
                        mm = pe.matmul(PP[n // 2][:, n % 2, ct * 256:ct * 256 + 256], vtok[:, n, ct * P:(ct + 1) * P],
                                       wsT[:, 2 * ct:2 * ct + 2, :].rearrange("p h t -> p (h t)"), start=True, stop=True)
                mm.then_inc(s["mix_done"], 1)
                pe.wait_ge(*step(l, "pooled", 1))
                for ct in range(2):
                    gemm(2 + ct, lambda k: bd[:, ct, :], lambda k: outs[:, 6 + ct, :], 1).then_inc(s["pool_mm"], 1)
                pe.wait_ge(*step(l, "gD", 2))
                for i, g in enumerate(GO):
                    pe.wait_ge(*step(l, "g_sq", 2 * i + 2))
                    if i == 2:
                        pe.wait_ge(*step(l, "mix_read", 1))
                    channel_sum((i + 2) % 4, [hT[:, 2 * g + ct, :] for ct in range(2)]).then_inc(s["g_sum"], 1)
                pe.wait_ge(*step(l, "g_root", 2))
                src = [zin[:, :, SEQ:SEQ + 2], gin[:, :, SEQ:SEQ + 30], pin[:, :, SEQ:SEQ + 15], zin[:, :, SEQ + 2:SEQ + 10],
                       gin[:, :, SEQ + 30:SEQ + 38], pin[:, :, SEQ + 15:SEQ + 23],
                       proj[:, HOME[B_V]:HOME[B_V] + 2, SEQ:T]]
                for n, (a, m) in enumerate(zip(src, TAIL)):
                    for ct in range(2):
                        tr = pe.transpose(tail_bank(n)[0:m, ct * P:(ct + 1) * P], a[:, ct, :], ident[:])
                    tr.then_inc(s["tail_tr"], 1)
                pe.wait_ge(*step(l, "g_root", 4))
                for q in range(KD):
                    n = (WOUT0, WOUT1)[l] + q // 2
                    if q % 2 == 0:
                        arrived(n)
                    if q >= 2:
                        pe.wait_ge(*step(l, "po_free", q - 1))
                    for i, k in enumerate(2 * g + ct for g in GO for ct in range(2)):
                        if q == 0:
                            pe.wait_ge(*step(l, "merged", i + 1))
                        for h in range(2):
                            mm = pe.matmul(PP[q % 2][:, h, 0:HT], slot(n, KD, 256)[:, k, P * (q % 2):P * (q % 2) + P],
                                           hT[:, k, HT * h:HT * h + HT], start=(i == 0), stop=(i == KD - 1))
                    mm.then_inc(s["po_done"], 1)
                    if q == 1:
                        pe.wait_ge(*step(l, "tail_copy", 7))
                    if q >= 2:
                        norm_sum(2 * l + 1, q - 2)
                norm_sum(2 * l + 1, KD - 2)
                norm_sum(2 * l + 1, KD - 1)
                if l == 0:
                    for f in range(FT):
                        n = DENSE + 2 * (f // 3)
                        if f % 3 == 0:
                            arrived(n)
                            arrived(n + 1)
                        if f >= 2:
                            pe.wait_ge(ff_free, f - 1)
                        m = P * min(3, FT - 3 * (f // 3))
                        for w in range(2):
                            lhs = lambda k: slot(n + w, KD, m)[:, k, P * (f % 3):P * (f % 3) + P]
                            if f == w == 0:
                                mm = gemm_h(0, lhs, 2 * l + 1)
                            else:
                                mm = gemm(2 * (f % 2) + w, lhs, lambda k: hT[:, k, :], KD)
                        mm.then_inc(ff_done, 1)
                    pe.wait_ge(ff_free, FT)
                    for q in range(KD):
                        n = DENSE2 + 2 * (q // 2)
                        if q % 2 == 0:
                            arrived(n)
                            arrived(n + 1)
                        if q >= 3:
                            pe.wait_ge(fy_free, q - 2)
                        gemm(YB[q % 3], lambda k: slot(n + k // 11, 11, 256)[:, k % 11, P * (q % 2):P * (q % 2) + P],
                             lambda k: G[:, k, :], FT).then_inc(fy_done, 1)
                        if q:
                            norm_sum(2, q - 1)

            pe.wait_ge(wr_in, 32)
            pe.wait_ge(*norm_step(3, "hs", 1))
            for k in range(KD):
                pe.wait_ge(*norm_step(3, "h", k + 1))
                for h in range(2):
                    gemm_r = pe.matmul(PP[0][0:NE, h, 0:HT], wrt[:, k, :], hT[:, k, HT * h:HT * h + HT],
                                       start=(k == 0), stop=(k == KD - 1))
            gemm_r.then_inc(R["lg"], 1)
            pe.wait_ge(R["lg_ev"], 1)
            for t in range(NT):
                n = min(P, T - P * t)
                tr = pe.transpose(PP[1][0:n, 0, t * NE:(t + 1) * NE], lgT[0:NE, P * t:P * t + n], ident[0:NE, 0:NE])
            tr.then_inc(R["lg_tr"], 1)
            def h_rows(t):
                n = min(P, T - P * t)
                if t:
                    pe.wait_ge(R["h_row"], t)
                for j in range(KD):
                    tr = pe.transpose(PP[2][0:n, j // 4, (j % 4) * P:(j % 4) * P + P], hT[:, j, P * t:P * t + n], ident[:])
                tr.then_inc(R["h_tr"], 1)
            h_rows(0)
            pe.wait_ge(R["mask"], 1)
            mflat = mask[:].rearrange("p t e -> p (t e)")
            pe.matmul(PP[0][:, 0, 0:NT * NE], tri[:], mflat, start=True, stop=True)
            pe.matmul(PP[0][:, 1, 0:NT * NE], ones[:], mflat, start=True, stop=True).then_inc(R["pre"], 1)
            for t in range(1, NT):
                h_rows(t)
            pe.wait_ge(R["route"], 1)


            def chunk_here(e, n):
                pe.wait_ge(full[n % RING], 16 * (n // RING + 1) + 32 * e)

            def narrow_rows(e):
                pe.sem_inc(R["in_tr"], 1)
                pe.sem_inc(R["yt_tr"], 3)
                for t in range(2):
                    pe.wait_ge(Rin[t], 16 * e + 16)
                    for h in range(2):
                        if t:
                            pe.wait_ge(R["in_ev"], NT * e + h + 2)
                        for j in range(4 * h, 4 * h + 4):
                            tr = pe.transpose(PP[3][:, h, (j % 4) * P:(j % 4) * P + P], stage[:, t, j * P:(j + 1) * P], ident[:])
                        tr.then_inc(R["in_tr"], 1)
                pe.wait_ge(R["in_ev"], NT * e + NT)

            def narrow_products(e, n):
                for f in range(ET):
                    c = f // 3
                    if f % 3 == 0:
                        chunk_here(e, MOE + 2 * c)
                        chunk_here(e, MOE + 2 * c + 1)
                    pe.wait_ge(R["f_free"], ET * e + f + 1)
                    m = P * min(3, ET - 3 * c)
                    for w in range(2):
                        for k in range(KD):
                            mm = pe.matmul(PP[w][:, f % 2, 0:n], slot(MOE + 2 * c + w, KD, m)[:, k, P * (f % 3):P * (f % 3) + P],
                                           hn[:, k, 0:n], start=(k == 0), stop=(k == KD - 1))
                    mm.then_inc(R["f_done"], 1)
                pe.wait_ge(R["f_free"], ET * e + ET + 2)
                for q in range(KD + 1):
                    if q < KD:
                        if q % 2 == 0:
                            chunk_here(e, MOE + 8 + q // 2)
                        pe.wait_ge(R["y_free"], KD * e + q + 1)
                        for k in range(ET):
                            mm = pe.matmul(PP[2][:, q % 2, 0:n], slot(MOE + 8 + q // 2, ET, 256)[:, k, P * (q % 2):P * (q % 2) + P],
                                           Gn[:, k, 0:n], start=(k == 0), stop=(k == ET - 1))
                        mm.then_inc(R["y_done"], 1)
                    if q:
                        j = q - 1
                        pe.wait_ge(R["y_free"], KD * e + j + 3)
                        if j == 4:
                            pe.wait_ge(R["yt_ev"], NT * e + 4)
                        for t in range(2):
                            tr = pe.transpose(PP[3][:, t, (j % 4) * P:(j % 4) * P + P], yn[:, j, P * t:P * t + P], ident[:])
                        if j % 4 == 3:
                            tr.then_inc(R["yt_tr"], 1)

            def wide(e):
                for t in range(NT):
                    if t < 2:
                        pe.wait_ge(Rin[t], 16 * e + 16)
                    else:
                        pe.wait_ge(Rwide[t - 2], 16 * e + 16)
                    if t:
                        pe.wait_ge(R["in_ev"], NT * e + t)
                    for j in range(KD):
                        tr = pe.transpose(PP[3][:, j // 4, (j % 4) * P:(j % 4) * P + P], stage[:, t % 2, j * P:(j + 1) * P], ident[:])
                    tr.then_inc(R["in_tr"], 1)
                pe.wait_ge(R["in_ev"], NT * e + NT)
                for f in range(ET):
                    c = f // 3
                    if f % 3 == 0:
                        chunk_here(e, MOE + 2 * c)
                        chunk_here(e, MOE + 2 * c + 1)
                    pe.wait_ge(R["f_free"], ET * e + f + 2)
                    m = P * min(3, ET - 3 * c)
                    for w in range(2):
                        mm = gemm(w, lambda k: slot(MOE + 2 * c + w, KD, m)[:, k, P * (f % 3):P * (f % 3) + P],
                                  lambda k: hexp[:, k, :], KD)
                    mm.then_inc(R["f_done"], 1)
                pe.wait_ge(R["f_free"], ET * e + ET + 2)
                for q in range(KD):
                    if q % 2 == 0:
                        chunk_here(e, MOE + 8 + q // 2)
                    pe.wait_ge(R["y_free"], KD * e + q + 2)
                    gemm(2, lambda k: slot(MOE + 8 + q // 2, ET, 256)[:, k, P * (q % 2):P * (q % 2) + P],
                         lambda k: G[:, k, :], ET).then_inc(R["y_done"], 1)
                pe.wait_ge(R["y_free"], KD * e + KD + 2)
                for t in range(NT):
                    if t:
                        pe.wait_ge(R["yt_ev"], NT * e + t + 1)
                    for j in range(KD):
                        tr = pe.transpose(PP[3][:, j // 4, (j % 4) * P:(j % 4) * P + P], work[:, j, AT[t]:AT[t] + P], ident[:])
                    tr.then_inc(R["yt_tr"], 1)

            def narrow_by_width(e, c, widths):
                if len(widths) == 1:
                    narrow_products(e, widths[0])
                    return
                with pe.If(c <= widths[0]):
                    narrow_products(e, widths[0])
                with pe.Else():
                    narrow_by_width(e, c, widths[1:])

            pe.wait_ge(R["count"], 2)
            with pe.Fori(0, NE) as e:
                c = tokens_of(pe, e)
                pe.wait_ge(R["yt_ev"], NT * e + 1)
                with pe.If(c <= NW):
                    narrow_rows(e)
                    narrow_by_width(e, c, WIDTHS)
                with pe.Else():
                    wide(e)
            pe.wait_ge(R["f_free"], ET * NE + 2)
            pe.wait_ge(R["diag"], 1)
            for j in range(KD):
                mm = pe.matmul(PP[0][:, j // 4, (j % 4) * P:(j % 4) * P + P], ones[:], diag[:, j * P:(j + 1) * P],
                               start=True, stop=True)
            mm.then_inc(R["g_mm"], 1)
            for j in range(KD):
                tr = pe.transpose(PP[1][0:NS, j // 4, (j % 4) * P:(j % 4) * P + P], mod[:, 1, 8 * GATE2 + j, 1:NQ], ident[:])
            tr.then_inc(R["g_mm"], 1)
            pe.wait_ge(R["y_free"], KD * NE + 2)
            pe.wait_ge(R["yt_ev"], NT * NE + 1)
            for t in range(NT):
                n = min(P, T - P * t)
                if t in (2, 3):
                    pe.wait_ge(R["g_ev"], t - 1)
                if t == 4:
                    pe.wait_ge(R["x_ev"], 1)
                for j in range(KD):
                    tr = pe.transpose(PP[XB[t]][0:n, j // 4, (j % 4) * P:(j % 4) * P + P], xT[:, j, P * t:P * t + n], ident[:])
                tr.then_inc(R["x_tr"], 1)

        @block.scalar
        def _(act):
            act.dma_start(crow[0:1], A["c_prompt"]).then_inc(c_in, 16)
            act.dma_start(crow[1:NQ], A["c_sample"]).then_inc(c_in, 16)
            act.dma_start(rows[0:96, 2, :], A["b_ada"].rearrange("l (r p) -> (l r) p", p=P)).then_inc(b_in, 16)
            act.wait_ge(c_in, 32)
            act.activation(crow[0:NQ], crow[0:NQ], ACT.Silu).then_inc(silu_c, 1)
            act.dma_start(wrt[:], A["w_router"][0].rearrange("(k p) e -> p k e", p=P)).then_inc(wr_in, 16)
            act.dma_start(brt[:], A["b_router"][0].rearrange("(e a) -> e a", a=1)).then_inc(wr_in, 16)

            act.wait_ge(const_ready, 1)
            act.sem_inc(ada_row, 2)
            for l in range(DEPTH):
                with act.Fori(0, 24 // RING) as i:
                    for j in range(RING):
                        n = 24 * l + RING * i + j
                        act.wait_ge(ada_mm, n + 1)
                        act.wait_ge(ada_tr, 8 * l + 2 * i + j // 3 + 1)
                        act.activation(modrow[32 * (j % 3):32 * (j % 3) + NQ, j // 3, :], PP[0][0:NQ, j % 2, 0:256],
                                       ACT.Copy).then_inc(ada_row, 1)
                if l == 0:
                    for j in range(1, KD, 2):
                        act.wait_ge(pro_tr, 4 + j)
                        act.activation(xT[:, j, 0:SEQ], PP[2][:, 1, :], ACT.Copy).then_inc(pro_act, 1)

            def root(q, dst, n, done):
                act.activation(two(dst), pp(q), ACT.Sqrt, bias=eps[:], scale=1.0 / n).then_inc(done, 1)

            def norm_act(tag, l, shift):
                for j in range(KD):
                    act.wait_ge(*norm_step(tag, "up", j + 1))
                    act.activation(work[:, j, :], xT[:, j, :], ACT.Square).then_inc(ns["sq"], 1)
                act.wait_ge(*norm_step(tag, "sum", 1))
                root(2, stat[:], D, ns["root"])
                for j in range(KD):
                    act.wait_ge(*norm_step(tag, "xhat", j + 1))
                    act.activation(hT[:, j, 0:SEQ], hT[:, j, 0:SEQ], ACT.Identity,
                                   bias=mod[:, l, 8 * shift + j, 0:1]).then_inc(ns["h"], 1)

            for l in range(DEPTH):
                if l == 0:
                    act.wait_ge(pro_act, 4)
                    act.wait_ge(const_dve, 1)
                norm_act(2 * l, l, SHIFT1)

                def evac(q, dst, func=ACT.Copy):
                    act.wait_ge(*step(l, "pj_done", q + 1))
                    act.activation(two(dst), pp(q % 2), func).then_inc(s[f"pj_free{q % 2}"], 1)

                for q in (0, 1):
                    evac(q, proj[:, HOME[C_G] + q, :], ACT.Sigmoid)
                for q in (4, 5):
                    evac(q, proj[:, HOME[B_V] + q - 4, :])
                act.wait_ge(*step(l, "hist_zero", 1))
                for q in (6, 7):
                    evac(q, pin[:, q - 6, 15:15 + T])
                for q in (8, 9):
                    evac(q, proj[:, HOME[A_H] + q - 8, :])
                for ct in range(2):
                    act.wait_ge(*step(l, "vxc", ct + 1))
                    act.activation(proj[:, HOME[C_G] + ct, :], proj[:, HOME[B_V] + ct, :], ACT.Square).then_inc(s["lnb_sq"], 1)
                for ct in range(2):
                    act.wait_ge(*step(l, "lnc_xc", ct + 1))
                    act.activation(proj[:, HOME[A_H] + ct, :], outs[:, 4 + ct, :], ACT.Square).then_inc(s["lnc_sq"], 1)
                for q in (12, 13):
                    evac(q, proj[:, HOME[B_U] + q - 12, :])
                act.wait_ge(*step(l, "lnb_var", 1))
                root(2, stat[:], W, s["lnb_root"])
                act.wait_ge(*step(l, "lnc_var", 1))
                root(3, stat2[:], W, s["lnc_root"])
                for q in (14, 15):
                    evac(q, proj[:, HOME[A_B] + q - 14, :])
                for ct in range(2):
                    act.wait_ge(*step(l, "lnc_hat", ct + 1))
                    act.activation(outs[:, 4 + ct, :], outs[:, 4 + ct, :], ACT.Silu, bias=v_("ln_c_b", l, ct),
                                   scale=v_("ln_c_g", l, ct)).then_inc(s["gC"], 1)
                act.wait_ge(*step(l, "pj_done", 16))
                for i in range(5):
                    if i < 4:
                        g = GO[i]
                        for ct in range(2):
                            act.wait_ge(*step(l, READY[g], ct + 1))
                            act.activation(hT[:, 2 * g + ct, :], outs[:, 2 * g + ct, :], ACT.Square).then_inc(s["g_sq"], 1)
                    if i:
                        act.wait_ge(*step(l, "g_sum", i))
                        if i >= 3:
                            act.wait_ge(*step(l, "merged", 2 * (i - 2)))
                        root((i + 1) % 4, (stat, stat2)[(i - 1) % 2][:], W, s["g_root"])
                act.wait_ge(*step(l, "pool_free", 1))
                for n in range(7):
                    act.wait_ge(*step(l, "tail_tr", min(n // 2 * 2 + 2, 7)))
                    act.activation(outrow[0:TAIL[n], n, :], tail_bank(n)[0:TAIL[n]], ACT.Copy).then_inc(s["tail_copy"], 1)
                norm_act(2 * l + 1, l, SHIFT2)
                if l == 0:
                    act.wait_ge(*step(l, "tail_out", 16 * 8))
                    for f in range(FT):
                        act.wait_ge(ff_done, f + 1)
                        if f >= 2:
                            act.wait_ge(ff_free, f - 1)
                        act.activation(two(work[:, f % 2, :]), pp(2 * (f % 2)), ACT.Silu).then_inc(ff_act, 1)

            act.wait_ge(R["lg"], 1)
            act.wait_ge(wr_in, 32)
            act.activation(two(lgT), PP[0][0:NE, :, 0:HT], ACT.Identity, bias=brt[:]).then_inc(R["lg_ev"], 1)
            act.wait_ge(R["exp_d"], 1)
            act.activation(gate[:, 1, :], gate[:, 0, :], ACT.Exp).then_inc(R["gate"], 1)
            act.wait_ge(R["h_tr"], NT)
            act.dma_start(gf, A["g_final"].rearrange("(a n) -> a n", a=1).to_broadcast([P, D])).then_inc(gf_in, 16)
            act.sem_inc(R["y_free"], 2)
            act.wait_ge(R["count"], 2)
            with act.Fori(0, NE) as e:
                c = tokens_of(act, e)
                with act.If(c <= NW):
                    for f in range(ET):
                        act.wait_ge(R["f_done"], ET * e + f + 1)
                        act.wait_ge(R["f_free"], ET * e + f + 1)
                        act.activation(hactn[:, f % 2, :], PP[0][:, f % 2, 0:NW], ACT.Silu).then_inc(R["f_act"], 1)
                    for q in range(KD):
                        act.wait_ge(R["y_done"], KD * e + q + 1)
                        act.activation(yn[:, q, :], PP[2][:, q % 2, 0:NW], ACT.Copy).then_inc(R["y_free"], 1)
                with act.Else():
                    for f in range(ET):
                        act.wait_ge(R["f_done"], ET * e + f + 1)
                        act.wait_ge(R["f_free"], ET * e + f + 1)
                        act.activation(two(hact[:, f % 2, :]), pp(0), ACT.Silu).then_inc(R["f_act"], 1)
                    act.wait_ge(R["y_out"], 16 * NT * e + 16)
                    for q in range(KD):
                        act.wait_ge(R["y_done"], KD * e + q + 1)
                        act.activation(two(work[:, q, :]), pp(2), ACT.Copy).then_inc(R["y_free"], 1)
            for t in range(NT + 1):
                if t < NT:
                    n = min(P, T - P * t)
                    act.wait_ge(Rback[t][0], 16)
                    act.activation(yg[0:n, t, 0, :], yg[0:n, t, 0, :], ACT.Copy, scale=gate[0:n, 0, t:t + 1]).then_inc(R["ya"], 1)
                if t:
                    n = min(P, T - P * (t - 1))
                    act.wait_ge(R["x_ev"], t)
                    act.activation(yg[0:n, t - 1, 0, :], yg[0:n, t - 1, 1, :], ACT.Square,
                                   accum_out=ss[0:n, t - 1:t]).then_inc(R["ss"], 1)
                    act.wait_ge(R["ss"], t)
                    act.activation(ss[0:n, t - 1:t], ss[0:n, t - 1:t], ACT.Sqrt, bias=eps[0:n], scale=1.0 / D).then_inc(R["ssr"], 1)

        @block.vector
        def _(dve):
            order = [0]

            def done(ins):
                order[0] += 1
                ins.then_inc(dchain, 1)
                return order[0]

            def link(ins):
                dve.wait_ge(dchain, done(ins))

            dve.memset(eps[:], EPS)
            dve.memset(ones[:], 1.0).then_inc(const_dve, 1)
            for ct in range(2):
                dve.memset(win[0:64, ct:ct + 1], float((2, 8)[ct]))
                last = dve.memset(win[64:P, ct:ct + 1], float((4, 16)[ct]))
            link(last)
            dve.wait_ge(const_ready, 2)
            dve.reciprocal(winv[:], win[:])
            for ct in range(2):
                last = dve.tensor_scalar(cinv[:, ct, :], cinv[:, ct, :], win[:, ct:ct + 1], None, ALU.min)
            link(last)
            link(dve.reciprocal(cinv[:], cinv[:]))
            dve.wait_ge(pro_tr, 1)
            dve.tensor_copy(cT[:], PP[3][:, 0, 0:KD * NQ].rearrange("p (k q) -> p k q", k=KD)).then_inc(pro_dve, 1)
            dve.wait_ge(pro_tr, 2)
            dve.tensor_copy(bada[:], PP[2][:, 1, 0:96]).then_inc(pro_dve, 1)
            dve.wait_ge(pro_dve, 2)
            dve.sem_inc(ada_out, 2)
            for l in range(DEPTH):
                bad = bada[:, 48 * l:48 * l + 48].rearrange("p (b m) -> p b m", m=2)
                mv = mod[:, l].rearrange("p (b m) q -> p b m q", m=2)
                with dve.Fori(0, 24 // RING) as i:
                    for g in range(2):
                        dve.wait_ge(ada_tr, 8 * l + 2 * i + g + 3)
                        for m in range(2):
                            last = dve.tensor_tensor(mv[:, bass.ds(RING * i + 3 * g, 3), m],
                                                     PP[1][:, g, m * P:m * P + 96].rearrange("p (b q) -> p b q", b=3)[:, :, 0:NQ],
                                                     bad[:, bass.ds(RING * i + 3 * g, 3), m].unsqueeze(2).to_broadcast([P, 3, NQ]),
                                                     ALU.add)
                        last.then_inc(ada_out, 1)
                if l == 0:
                    dve.wait_ge(pro_tr, 3)
                    dve.tensor_copy(vec[:], PP[3][:, 0, 0:DEPTH * NROWS].rearrange("p (l n) -> p l n", l=DEPTH)).then_inc(pro_dve, 1)
                    for j in range(0, KD, 2):
                        dve.wait_ge(pro_tr, 4 + j)
                        dve.tensor_copy(xT[:, j, 0:SEQ], PP[2][:, 0, :]).then_inc(pro_dve, 1)
                    dve.wait_ge(pro_tr, 12)
                    dve.tensor_copy(xT[:, :, SEQ:T], PP[3][:, 1, 0:KD * NS].rearrange("p (k q) -> p k q", k=KD)).then_inc(pro_dve, 1)
            dve.wait_ge(pro_dve, 3)
            dve.wait_ge(ada_out, 2 + 8 * DEPTH)
            dve.wait_ge(pro_dve, 8)
            dve.sem_inc(ns["up"], KD)
            for l in range(DEPTH):
                for sec, g in ((SCALE1, "g_mix"), (SCALE2, "g_ffn")):
                    a = mod[:, l, 8 * sec:8 * sec + 8, :]
                    gv = vec[:, l, ROWS[g][0]:ROWS[g][0] + 8]
                    last = dve.scalar_tensor_tensor(a, a, 1.0, gv.unsqueeze(2).to_broadcast([P, 8, NQ]), ALU.add, ALU.mult)
            link(last)

            def norm_dve(tag, l, scale, shift):
                dve.wait_ge(*norm_step(tag, "root", 1))
                link(dve.reciprocal(stat[:], stat[:]))
                hs = hT[:, :, SEQ:T]
                sample = [lambda: dve.tensor_tensor(hs, xT[:, :, SEQ:T], stat[:, SEQ:T].unsqueeze(1).to_broadcast([P, KD, NS]), ALU.mult),
                          lambda: dve.tensor_tensor(hs, hs, mod[:, l, 8 * scale:8 * scale + 8, 1:NQ], ALU.mult),
                          lambda: dve.tensor_tensor(hs, hs, mod[:, l, 8 * shift:8 * shift + 8, 1:NQ], ALU.add)]
                for j in range(KD):
                    if j in (0, 1):
                        c = done(sample[j]())
                    if j == 2:
                        sample[2]().then_inc(ns["hs"], 1)
                    dve.scalar_tensor_tensor(hT[:, j, 0:SEQ], xT[:, j, 0:SEQ], mod[:, l, 8 * scale + j, 0:1], stat[:, 0:SEQ],
                                             ALU.mult, ALU.mult).then_inc(ns["xhat"], 1)
                    if j in (0, 1):
                        dve.wait_ge(dchain, c)

            def add_gated(l, sec, q, pair, free):
                g = mod[:, l, 8 * sec + q, :]
                c = done(dve.tensor_tensor(small[:, q % 2, :], PP[pair][:, 1, HT - NS:HT], g[:, 1:NQ], ALU.mult))
                dve.scalar_tensor_tensor(xT[:, q, 0:HT], PP[pair][:, 0, 0:HT], g[:, 0:1], xT[:, q, 0:HT], ALU.mult, ALU.add)
                dve.scalar_tensor_tensor(xT[:, q, HT:SEQ], PP[pair][:, 1, 0:HT - NS], g[:, 0:1], xT[:, q, HT:SEQ],
                                         ALU.mult, ALU.add).then_inc(free, 1)
                dve.wait_ge(dchain, c)
                dve.tensor_tensor(xT[:, q, SEQ:T], xT[:, q, SEQ:T], small[:, q % 2, :], ALU.add).then_inc(ns["up"], 1)

            for l in range(DEPTH):
                dve.wait_ge(*step(l, "ws_tr", 1))
                dve.tensor_copy(wsT, PP[3][:, 0, :].rearrange("p (h t) -> p h t", h=4)).then_inc(s["ws_copy"], 1)
                dve.wait_ge(*step(l, "st_tr", 1))
                for dst, src, r in ((hisA, PP[3][:, 1, 0:32], 2), (hisC, PP[3][:, 1, 32:512], 30),
                                    (hisD, PP[0][:, 0, 0:240], 15)):
                    for ct in range(2):
                        m = NS * r
                        last = dve.tensor_copy(dst[:, ct, :, 0:r], src[:, ct * m:ct * m + m].rearrange("p (b r) -> p b r", r=r))
                    last.then_inc(s["st_copy"], 1)
                norm_dve(2 * l, l, SCALE1, SHIFT1)
                dve.wait_ge(*step(l, "hist_zero", 1))
                for q in (2, 3):
                    dve.wait_ge(*step(l, "pj_done", q + 1))
                    dve.wait_ge(*step(l, f"pj_free{q % 2}", 1))
                    dve.tensor_tensor(two(gin[:, q - 2, 30:30 + T]), pp(q % 2), two(proj[:, HOME[C_G] + q - 2, :]),
                                      ALU.mult).then_inc(s[f"pj_free{q % 2}"], 1)
                dve.wait_ge(*step(l, "pj_free0", 2))
                dve.wait_ge(*step(l, "pj_free1", 2))
                for ct in range(2):
                    last = dve.tensor_copy(hisC[:, ct, :, 30], gin[:, ct, SEQ + 30:SEQ + 38])
                link(last)

                def tap(name, k, ct):
                    return v_(name, l, 2 * k + ct)

                def taps(name, n, ct):
                    r0 = ROWS[name][0]
                    w = vec[:, l, r0:r0 + 2 * n].rearrange("p (k c) -> p c k", c=2)[:, ct]
                    return w.unsqueeze(1).to_broadcast([P, NS, n])

                for k in range(TAPS_C):
                    for ct in range(2):
                        acc = outs[:, 4 + ct, 0:SEQ]
                        if k == 0:
                            dve.tensor_scalar(acc, gin[:, ct, 0:SEQ], tap("conv_c_w", 0, ct), v_("conv_c_b", l, ct),
                                              ALU.mult, ALU.add).then_inc(s["conv_tap"], 1)
                        else:
                            dve.wait_ge(*step(l, "conv_tap", 2 * k + ct - 1))
                            dve.scalar_tensor_tensor(acc, gin[:, ct, k:k + SEQ], tap("conv_c_w", k, ct), acc,
                                                     ALU.mult, ALU.add).then_inc(s["conv_tap"], 1)
                for ct in range(2):
                    o = outs[:, 4 + ct, SEQ:T]
                    link(dve.tensor_tensor(tapC[:], hisC[:, ct], taps("conv_c_w", TAPS_C, ct), ALU.mult))
                    link(dve.tensor_reduce(o, tapC[:], AX.X, ALU.add))
                    last = dve.tensor_scalar(o, o, v_("conv_c_b", l, ct), None, ALU.add)
                last.then_inc(s["lnc_in"], 1)
                for q in (10, 11):
                    dve.wait_ge(*step(l, "pj_done", q + 1))
                    dve.wait_ge(*step(l, f"pj_free{q % 2}", 5))
                    dve.tensor_tensor(two(zin[:, q - 10, 2:2 + T]), pp(q % 2), two(proj[:, HOME[A_H] + q - 10, :]),
                                      ALU.mult).then_inc(s[f"pj_free{q % 2}"], 1)
                for q, tiles, sums, xc in ((2, [proj[:, HOME[B_V] + ct, :] for ct in range(2)], "lnb_sum", "vxc"),
                                           (3, [outs[:, 4 + ct, :] for ct in range(2)], "lnc_sum", "lnc_xc")):
                    dve.wait_ge(*step(l, sums, 1))
                    for ct in range(2):
                        dve.scalar_tensor_tensor(two(tiles[ct]), pp(q), -1.0 / W, two(tiles[ct]), ALU.mult,
                                                 ALU.add).then_inc(s[xc], 1)
                dve.wait_ge(*step(l, "pj_free0", 6))
                dve.wait_ge(*step(l, "pj_free1", 6))
                for ct in range(2):
                    last = dve.tensor_copy(hisA[:, ct, :, 2], zin[:, ct, SEQ + 2:SEQ + 10])
                link(last)
                for ct in range(2):
                    acc = outs[:, ct, 0:SEQ]
                    link(dve.tensor_scalar(acc, zin[:, ct, 0:SEQ], tap("conv_a_w", 0, ct), None, ALU.mult))
                    for k in (1, 2):
                        link(dve.scalar_tensor_tensor(acc, zin[:, ct, k:k + SEQ], tap("conv_a_w", k, ct), acc, ALU.mult, ALU.add))
                    link(dve.tensor_tensor(tapC[:, :, 0:TAPS_A], hisA[:, ct], taps("conv_a_w", TAPS_A, ct), ALU.mult))
                    link(dve.tensor_reduce(outs[:, ct, SEQ:T], tapC[:, :, 0:TAPS_A], AX.X, ALU.add))
                for ct in range(2):
                    last = dve.tensor_copy(hisD[:, ct, :, 15], pin[:, ct, SEQ + 15:SEQ + 23])
                link(last)
                for ct in range(2):
                    for r, w in ((slice(0, 64), (2, 8)[ct]), (slice(64, P), (4, 16)[ct])):
                        last = dve.tensor_reduce(outs[r, 6 + ct, SEQ:T], hisD[r, ct, :, POOL - w:POOL], AX.X, ALU.add)
                dve.wait_ge(*step(l, "pool_out", 1))
                link(last)
                link(dve.tensor_tensor(head16[:], outs[:, 6:8, 0:POOL], cinv[:], ALU.mult))
                for ct in range(2):
                    last = dve.scalar_tensor_tensor(outs[:, 6 + ct, :], outs[:, 6 + ct, :], winv[:, ct:ct + 1],
                                                    pin[:, ct, 15:15 + T], ALU.mult, ALU.subtract)
                link(last)
                dve.tensor_tensor(outs[:, 6:8, 0:POOL], head16[:], pin[:, :, 15:15 + POOL], ALU.subtract).then_inc(s["pooled"], 1)
                dve.wait_ge(*step(l, "lnb_root", 1))
                link(dve.reciprocal(stat[:], stat[:]))
                for ct in range(2):
                    v = proj[:, HOME[B_V] + ct, :]
                    link(dve.tensor_tensor(v, v, stat[:], ALU.mult))
                    dve.tensor_scalar(v, v, v_("ln_v_g", l, ct), v_("ln_v_b", l, ct), ALU.mult, ALU.add).then_inc(s["vn_ready"], 1)
                dve.wait_ge(*step(l, "lnc_root", 1))
                link(dve.reciprocal(stat2[:], stat2[:]))
                for ct in range(2):
                    o = outs[:, 4 + ct, :]
                    dve.tensor_tensor(o, o, stat2[:], ALU.mult).then_inc(s["lnc_hat"], 1)
                dve.wait_ge(*step(l, "pj_free0", 8))
                dve.wait_ge(*step(l, "pj_free1", 8))
                for ct in range(2):
                    dve.tensor_tensor(outs[:, ct, :], outs[:, ct, :], proj[:, HOME[A_B] + ct, :], ALU.mult).then_inc(s["gA"], 1)
                dve.wait_ge(*step(l, "vt_tr", 1))
                dve.wait_ge(*step(l, "lnc_sq", 2))
                dve.tensor_copy(vtok.rearrange("p (h a) w -> p h (a w)", h=2), PP[3][:]).then_inc(s["vt_copy"], 1)
                dve.wait_ge(*step(l, "vn_ready", 2))
                for ct in range(2):
                    last = dve.tensor_scalar(outs[:, 2 + ct, SEQ:T], proj[:, HOME[B_V] + ct, SEQ:T], ws00[:, ct:ct + 1],
                                             bsb[:, ct, 0:1], ALU.mult, ALU.add)
                dve.wait_ge(*step(l, "mix_done", 1))
                for r in range(2):
                    rr = slice(64 * r, 64 * r + 64)
                    for ct in range(2):
                        for h in range(2):
                            last = dve.tensor_tensor(outs[rr, 2 + ct, 256 * h:256 * h + 256].rearrange("p (n t) -> p n t", n=2),
                                                     PP[h][rr, :, ct * 256 + r * P:ct * 256 + r * P + P],
                                                     bsb[rr, ct:ct + 1, :].to_broadcast([64, 2, P]), ALU.add)
                last.then_inc(s["mix_read"], 1)
                dve.wait_ge(*step(l, "mix_read", 1))
                for ct in range(2):
                    dve.tensor_tensor(outs[:, 2 + ct, :], outs[:, 2 + ct, :], proj[:, HOME[B_U] + ct, :], ALU.mult).then_inc(s["gB"], 1)
                for ct in range(2):
                    dve.wait_ge(*step(l, "pool_mm", ct + 1))
                    dve.tensor_scalar(two(outs[:, 6 + ct, :]), pp(2 + ct), v_("pool_scale", l, ct), None, ALU.mult).then_inc(s["gD"], 1)
                dve.sem_inc(s["pool_free"], 1)
                for i, g in enumerate(GO):
                    st = (stat, stat2)[i % 2]
                    dve.wait_ge(*step(l, "g_root", i + 1))
                    link(dve.reciprocal(st[:], st[:]))
                    for ct in range(2):
                        j = 2 * g + ct
                        dve.scalar_tensor_tensor(hT[:, j, :], outs[:, j, :], v_("g_out", l, j), st[:], ALU.mult,
                                                 ALU.mult).then_inc(s["merged"], 1)
                for q in range(KD):
                    dve.wait_ge(*step(l, "po_done", q + 1))
                    add_gated(l, GATE1, q, q % 2, s["po_free"])
                norm_dve(2 * l + 1, l, SCALE2, SHIFT2)
                if l == 0:
                    dve.wait_ge(*step(l, "tail_out", 16 * 8))
                    for f in range(FT):
                        dve.wait_ge(ff_act, f + 1)
                        dve.tensor_tensor(two(G[:, f, :]), pp(2 * (f % 2) + 1), two(work[:, f % 2, :]), ALU.mult).then_inc(ff_free, 1)
                    for q in range(KD):
                        dve.wait_ge(fy_done, q + 1)
                        add_gated(l, GATE2, q, YB[q % 3], fy_free)

            link(dve.memset(lg[:], 0.0))
            dve.wait_ge(R["lg_tr"], 1)
            dve.tensor_copy(lg[:, 0:4, :], PP[1][:, 0, 0:4 * NE].rearrange("p (t e) -> p t e", t=4))
            link(dve.tensor_copy(lg[0:NS, 4, :], PP[1][0:NS, 0, 4 * NE:5 * NE]))
            for t in range(NT):
                last = dve.max(vmax[:, t, :], lg[:, t, :])
            link(last)
            for t in range(NT):
                last = dve.max_index(imax[:, t, :], vmax[:, t, :], lg[:, t, :])
            dve.tensor_tensor(gate[:, 0, :], vmax[:, :, 1], vmax[:, :, 0], ALU.subtract).then_inc(R["exp_d"], 1)
            link(last)
            link(dve.tensor_copy(imf[:], imax[:]))
            dve.wait_ge(R["const"], 3)
            for r in range(2):
                for t in range(NT):
                    last = dve.tensor_scalar(pick[:, r, t, :], eidx[:], imf[:, t, r:r + 1], valid[:, t:t + 1],
                                             ALU.is_equal, ALU.mult)
            link(last)
            dve.tensor_tensor(mask[:], pick[:, 0], pick[:, 1], ALU.add).then_inc(R["mask"], 1)
            dve.wait_ge(R["h_tr"], 1)
            dve.tensor_copy(stage[:, 0, :].rearrange("p (h n) -> p h n", h=2), PP[2][:]).then_inc(R["h_row"], 1)
            dve.wait_ge(R["pre"], 1)
            dve.tensor_copy(before[:], PP[0][:, 0, 0:NT * NE].rearrange("p (t e) -> p t e", t=NT))
            dve.tensor_copy(totals[:, 1:NT, :], PP[0][:, 1, 0:(NT - 1) * NE].rearrange("p (t e) -> p t e", t=NT - 1))
            link(dve.tensor_reduce(countf[:], PP[0][:, 1, 0:NT * NE].rearrange("p (t e) -> p e t", t=NT), AX.X, ALU.add))
            dve.tensor_copy(count[:], countf[:]).then_inc(R["count"], 1)
            for e in range(1, NE):
                link(dve.tensor_tensor(ebase[:, e:e + 1], ebase[:, e - 1:e], countf[:, e - 1:e], ALU.add))
            dve.tensor_copy(first[:], ebase[:]).then_inc(R["count"], 1)
            link(dve.tensor_copy(totals[:, 0, :], ebase[:]))
            for t in range(1, NT):
                link(dve.tensor_tensor(totals[:, t, :], totals[:, t, :], totals[:, t - 1, :], ALU.add))
            link(dve.tensor_tensor(before[:], before[:], totals[:], ALU.add))
            for r in range(2):
                last = dve.tensor_tensor(pick[:, r], pick[:, r], before[:], ALU.mult)
            link(last)
            link(dve.tensor_reduce(placef[:], pick[:], AX.X, ALU.add))
            dve.tensor_copy(place[:], placef[:]).then_inc(R["route"], 1)
            dve.wait_ge(R["gate"], 1)
            link(dve.tensor_scalar(gate[:, 0, :], gate[:, 1, :], 1.0, None, ALU.add))
            link(dve.reciprocal(gate[:, 0, :], gate[:, 0, :]))
            link(dve.tensor_tensor(gate[:, 1, :], gate[:, 1, :], gate[:, 0, :], ALU.mult))
            for t in range(1, NT):
                n = min(P, T - P * t)
                dve.wait_ge(R["h_tr"], t + 1)
                if t >= 3:
                    dve.wait_ge(Rout[t % 3], 32 * (t // 3))
                dve.tensor_copy(stage[0:n, t % 3, :].rearrange("p (h n) -> p h n", h=2), PP[2][0:n]).then_inc(R["h_row"], 1)

            dve.wait_ge(*step(1, "tail_out", 16 * 8))
            for b in range(3):
                dve.wait_ge(Rout[b], 32 * len(range(b, NT, 3)))
            dve.sem_inc(R["yt_ev"], 1)
            dve.sem_inc(R["f_free"], 2)
            dve.sem_inc(R["y_out"], 16)
            dve.wait_ge(R["count"], 2)
            with dve.Fori(0, NE) as e:
                c = tokens_of(dve, e)
                with dve.If(c <= NW):
                    dve.sem_inc(R["in_ev"], 1)
                    for t in range(2):
                        for h in range(2):
                            dve.wait_ge(R["in_tr"], NT * e + 2 * t + h + 2)
                            dve.tensor_copy(hn[:, 4 * h:4 * h + 4, P * t:P * t + P],
                                            PP[3][:, h, :].rearrange("p (a n) -> p a n", a=4)).then_inc(R["in_ev"], 1)
                    dve.sem_inc(R["yt_ev"], 1)
                    for f in range(ET):
                        dve.wait_ge(R["f_act"], ET * e + f + 1)
                        dve.tensor_tensor(Gn[:, f, :], PP[1][:, f % 2, 0:NW], hactn[:, f % 2, :], ALU.mult).then_inc(R["f_free"], 1)
                    dve.wait_ge(R["y_out"], 16 * NT * e + 16)
                    for h in range(2):
                        dve.wait_ge(R["yt_tr"], NT * e + h + 4)
                        for t in range(2):
                            dve.tensor_copy(yrow[:, t, 4 * P * h:4 * P * h + 4 * P], PP[3][:, t, :]).then_inc(R["yt_ev"], 1)
                with dve.Else():
                    for t in range(NT):
                        dve.wait_ge(R["in_tr"], NT * e + t + 1)
                        dve.tensor_copy(hexp[:, :, AT[t]:AT[t] + P].rearrange("p (h a) n -> p h a n", h=2),
                                        PP[3][:].rearrange("p h (a n) -> p h a n", a=4)).then_inc(R["in_ev"], 1)
                    for f in range(ET):
                        dve.wait_ge(R["f_act"], ET * e + f + 1)
                        dve.tensor_tensor(two(G[:, f, :]), pp(1), two(hact[:, f % 2, :]), ALU.mult).then_inc(R["f_free"], 1)
                    for t in range(NT):
                        dve.wait_ge(R["yt_tr"], NT * e + t + 1)
                        dve.wait_ge(R["y_out"], 16 * (NT * e + t) + 16)
                        dve.tensor_copy(stage[:, 2, :].rearrange("p (h n) -> p h n", h=2), PP[3][:]).then_inc(R["yt_ev"], 1)
            for j in range(KD):
                last = dve.tensor_scalar(diag[:, j * P:(j + 1) * P], ident[:], mod[:, 1, 8 * GATE2 + j, 0:1], None, ALU.mult)
            last.then_inc(R["diag"], 1)
            for i, (g, n) in enumerate(((gate_p, P), (gate_s, NS))):
                dve.wait_ge(R["g_mm"], i + 1)
                c = done(dve.tensor_copy(g[0:n].rearrange("p (h n) -> p h n", h=2), PP[i][0:n]))
                dve.wait_ge(dchain, c)
                dve.sem_inc(R["g_ev"], 1)
            dve.wait_ge(gf_in, 16)
            for t in range(NT + 1):
                if t < NT:
                    n = min(P, T - P * t)
                    a = yg[0:n, t, 1, :]
                    dve.wait_ge(R["ya"], t + 1)
                    dve.wait_ge(Rback[t][1], 16)
                    link(dve.scalar_tensor_tensor(a, a, gate[0:n, 1, t:t + 1], yg[0:n, t, 0, :], ALU.mult, ALU.add))
                    link(dve.tensor_tensor(a, a, (gate_p if t < 4 else gate_s)[0:n], ALU.mult))
                    dve.wait_ge(R["x_tr"], t + 1)
                    dve.tensor_tensor(a.rearrange("p (h n) -> p h n", h=2), a.rearrange("p (h n) -> p h n", h=2), PP[XB[t]][0:n],
                                      ALU.add).then_inc(R["x_ev"], 1)
                if t:
                    n = min(P, T - P * (t - 1))
                    a = yg[0:n, t - 1, 1, :]
                    dve.wait_ge(R["ssr"], t)
                    link(dve.reciprocal(ss[0:n, t - 1:t], ss[0:n, t - 1:t]))
                    dve.scalar_tensor_tensor(a, a, ss[0:n, t - 1:t], gf[0:n], ALU.mult, ALU.mult).then_inc(fin_ev, 1)


_INS = ["x_prompt", "x_sample", "state_conv_a", "state_conv_c", "state_pool_d", "c_prompt", "c_sample", "w_ada", "b_ada",
        "g_mix", "w_in", "conv_a_w", "ln_v_g", "ln_v_b", "w_s", "b_s", "conv_c_w", "conv_c_b", "ln_c_g", "ln_c_b",
        "pool_w", "pool_scale", "g_out", "w_out", "g_ffn", "w1_dense", "w3_dense", "w2_dense", "w_router", "b_router",
        "w1_moe", "w3_moe", "w2_moe", "g_final"]
_OUTS = [("y_prompt", (1, SEQ, D)), ("y_sample", (NS, 1, D)),
         ("a_p", (DEPTH, 1, 2, W)), ("c_p", (DEPTH, 1, 30, W)), ("d_p", (DEPTH, 1, 15, W)), ("v_p", (DEPTH, 1, P, W)),
         ("a_s", (DEPTH, NS, 2, W)), ("c_s", (DEPTH, NS, 30, W)), ("d_s", (DEPTH, NS, 15, W)), ("v_s", (DEPTH, NS, 1, W))]


def kernel(**inputs):
    import numpy as _np
    import concourse.bacc as _bacc
    from concourse.bass_utils import run_bass_kernel_spmd as _run

    nc = _bacc.Bacc("TRN2", target_bir_lowering=False, num_devices=1)
    arrays, A, O = {}, {}, {}
    for name in _INS:
        a = _np.ascontiguousarray(inputs[name])
        arrays[f"in_{name}"] = a
        A[name] = nc.dram_tensor(f"in_{name}", a.shape, F32, kind="ExternalInput").ap()
    for name, shape in _OUTS:
        O[name] = nc.dram_tensor(f"out_{name}", shape, F32, kind="ExternalOutput").ap()
    trunk_program(nc, A, O)
    r = _run(nc, [arrays], core_ids=[0])
    return tuple(r.results[0][f"out_{name}"] for name, _ in _OUTS)
```

```python
from contextlib import ExitStack

import concourse.bass as bass
from concourse import mybir

F32 = mybir.dt.float32
F32R = mybir.dt.float32r
I32 = mybir.dt.int32
U32 = mybir.dt.uint32
ALU = mybir.AluOpType
ACT = mybir.ActivationFunctionType
AX = mybir.AxisListType

P = 128
D = 1024
KD = D // P
SEQ = 512
NS = 8
T = SEQ + NS
HT = T // 2
NQ = 1 + NS
DEPTH = 2
W = 256
TAPS_A, TAPS_C, POOL = 3, 31, 16
FF = 2816
FE = 1408
NE = 8
EPS = 1e-6
RING = 4
SLOT = KD * 256
ADA_RING = 6
NA = 24 // ADA_RING
EXPERT_RING = 6
EXPERT_SLOT = KD * 384
FH = FF // P // 2
UNIT_SLOTS = 4
UNIT = FH * P
NT = (T + P - 1) // P
AT = [0, 128, 256, 384, T - P]
PICKS = 2 * T
ROOM = PICKS + T
NW = 2 * P
WIDTHS = [128, 136, 144, 152, 160, 176, 192, 208, 224, NW]

A_B, A_C, A_H, B_U, B_V, C_A, C_G, D_P = range(8)
ORDER = [C_G, C_A, B_V, D_P, A_H, A_C, B_U, A_B]
HOME = {C_G: 0, B_V: 2, A_H: 4, B_U: 6, A_B: 8}

ROWS, _at = {}, 0
for _name, _n in [("g_mix", 8), ("ln_v_g", 2), ("ln_v_b", 2), ("conv_c_b", 2), ("ln_c_g", 2), ("ln_c_b", 2),
                  ("pool_scale", 2), ("g_out", 8), ("g_ffn", 8), ("conv_a_w", 2 * TAPS_A), ("conv_c_w", 2 * TAPS_C)]:
    ROWS[_name] = (_at, _n)
    _at += _n
NROWS = _at

TAIL = [TAPS_A - 1, TAPS_C - 1, POOL - 1, NS, NS, NS, NS]

SHIFT1, SCALE1, GATE1, SHIFT2, SCALE2, GATE2 = range(6)

WIN0 = 0
WOUT0 = WIN0 + 8
DENSE = WOUT0 + 4
PER_H = 20
WIN1 = DENSE + 2 * PER_H
WOUT1 = WIN1 + 8
MOE = WOUT1 + 4
PER_E = 12
FT = FF // P
ET = FE // P

U_IN = [0, 24 + 2 * (2 * FH + KD)]
U_OUT = [16, U_IN[1] + 16]
UNITS = U_OUT[1] + 8


def U_FF(h, f, w):
    return 24 + (2 * FH + KD) * h + 2 * f + w


def U_FY(h, q):
    return 24 + (2 * FH + KD) * h + 2 * FH + q


def trunk_program(nc, A, O):
    ctx = ExitStack()
    with ctx:
        def sb(name, shape, dt=F32):
            return ctx.enter_context(nc.sbuf_tensor(name, shape, dt))

        rounded = {}

        def sb_two(name, shape):
            with nc.sbuf_tensor(name, shape, F32) as buf:
                pass
            rounded[name] = sb(name + "_r", shape, F32R)
            return buf

        def r_(ap):
            return bass.AP(rounded[ap.tensor.name], ap.offset, ap.ap)

        def read_(ap):
            return r_(ap).bitcast(F32)

        def sem(name):
            return ctx.enter_context(nc.semaphore(name))

        mem = sb_two("mem", [P, EXPERT_RING * EXPERT_SLOT])
        xT = sb("xT", [P, KD, T])
        hT = sb_two("hT", [P, KD, T])
        work = sb("work", [P, KD, T])
        big = sb_two("big", [P, 2 * FH * T])
        stage = sb("stage", [P, 3, D])
        vec = sb("vec", [P, DEPTH, NROWS])
        bada = sb("bada", [P, DEPTH * 48])
        mod = sb("mod", [P, DEPTH, 48, NQ])
        cs = sb_two("cs", [P, KD, 2 * NQ])
        ident = sb("ident", [P, P])
        ones = sb("ones", [P, P])
        eps = sb("eps", [P, 1])
        wrt = sb("wrt", [P, KD, NE])
        brt = sb("brt", [NE, 1])
        win = sb("win", [P, 2])
        winv = sb("winv", [P, 2])
        cinv = sb("cinv", [P, 2, POOL])
        flat = stage[:, :, :].rearrange("p a n -> p (a n)")

        def cut(src, at, *shape):
            n = 1
            for s in shape:
                n *= s
            v = src[:, at:at + n]
            if len(shape) == 2:
                v = v.rearrange("p (a b) -> p a b", a=shape[0])
            if len(shape) == 3:
                v = v.rearrange("p (a b c) -> p a b c", a=shape[0], b=shape[1])
            return v

        ahi = cut(mem, ADA_RING * SLOT, 3, KD, 256)
        hlo = cut(mem, RING * SLOT + UNIT_SLOTS * UNIT, KD, T)
        ws_raw = cut(flat, 0, 4, P)
        bsb = cut(flat, 512, 2, P)
        bd = cut(flat, 768, 2, P)
        stA = cut(flat, 1024, W)
        stC = cut(flat, 1280, 2, W)
        stD = cut(flat, 1792, W)
        wsT = cut(flat, 2048, 4, P)
        ws00 = sb("ws00", [P, 2])
        hisA = sb("hisA", [P, 2, NS, TAPS_A])
        hisC = sb("hisC", [P, 2, NS, TAPS_C])
        hisD = sb("hisD", [P, 2, NS, POOL])
        head16 = sb("head16", [P, 2, POOL])
        tapC = sb("tapC", [P, NS, TAPS_C])
        small = sb("small", [P, 2, NS])
        stat = sb("stat", [P, T])
        stat2 = sb("stat2", [P, T])
        lg = sb("lg", [P, NT, NE])
        vmax = sb("vmax", [P, NT, 8])
        imax = sb("imax", [P, NT, 8], U32)
        imf = sb("imf", [P, NT, 8])
        pick = sb("pick", [P, 2, NT, NE])
        mask = sb("mask", [P, NT, NE])
        before = sb("before", [P, NT, NE])
        totals = sb("totals", [P, NT, NE])
        tri = sb("tri", [P, P])
        eidx = sb("eidx", [P, NE])
        ebase = sb("ebase", [P, NE])
        valid = sb("valid", [P, NT])
        placef = sb("placef", [P, 2, NT])
        place = sb("place", [P, 2, NT], U32)
        gate = sb("gate", [P, 2, NT])
        ss = sb("ss", [P, NT])
        countf = sb("countf", [P, NE])
        count = sb("count", [P, NE], I32)
        first = sb("first", [P, NE], I32)
        modrow = sb("modrow", [P, 256])

        xin = cut(big, 0, NT, D)
        rows = cut(big, 5 * D, 4, P)
        crow = cut(big, 5 * D + 4 * P, D)
        proj = cut(big, 0, 10, T)
        zin = cut(big, 10 * T, 2, TAPS_A - 1 + T)
        gin = cut(big, 10 * T + 2 * (2 + T), 2, TAPS_C - 1 + T)
        pin = cut(big, 10 * T + 2 * (32 + 2 * T), 2, POOL - 1 + T)
        DAT = 10 * T + 2 * (47 + 3 * T)
        pa = cut(big, DAT, 2, POOL - 1 + T)
        pb = cut(big, DAT + 2 * (15 + T), 2, POOL - 1 + T)
        outrow = cut(big, DAT, 7, W)
        vtok = cut(big, HOME[A_H] * T, 4, W)
        G = cut(big, 0, FH, T)
        Glo = cut(big, FH * T, FH, T)
        mod_lo = cut(big, 7 * D, DEPTH, 48, NQ)
        turned = cut(big, 8 * D, 256)
        hexp = cut(big, 11 * T, KD, T)
        hact = cut(big, 19 * T, 2, T)
        Gn = cut(big, 0, ET, NW)
        hn = cut(big, 11 * T, KD, NW)
        hactn = cut(big, 19 * T, 2, NW)
        wflat = work[:, :, :].rearrange("p k n -> p (k n)")
        yn = cut(wflat, 0, KD, NW)
        yrow = cut(wflat, KD * NW, 2, D)
        hrow = [cut(wflat, t * D, D) for t in range(NT - 1)] + [stage[:, 2, :]]
        yg = cut(mem, 0, NT, 2, D)
        hflat = hT[:, :, :].rearrange("p k n -> p (k n)")
        gate_p, gate_s, gf, diag = (cut(hflat, i * D, D) for i in range(4))
        outs = work
        lgT = stat2[0:NE]

        PP = [ctx.enter_context(nc.psum_tensor(f"PP{q}", [P, 2, 512], F32)) for q in range(4)]

        Hd = nc.dram_tensor("h_by_expert", (ROOM, D), F32).ap()
        Yd = nc.dram_tensor("y_by_expert", (ROOM, D), F32).ap()

        def v_(name, l, j):
            return vec[:, l, ROWS[name][0] + j:ROWS[name][0] + j + 1]

        def tail_bank(n):
            return PP[3 - n // 4][:, n % 4 // 2, (n % 2) * W:(n % 2) * W + W]

        def pp(q, n=HT):
            return PP[q][:, :, 0:n]

        def two(ap):
            return ap.rearrange("p (h n) -> p h n", h=2)

        full = [sem(f"slot_full{s}") for s in range(RING)]
        efull = [sem(f"wide_slot_full{s}") for s in range(EXPERT_RING)]
        x_half = sem("x_half")
        w_hi, w_lo = sem("w_hi"), sem("w_lo")
        ada_hi, ada_lo = sem("ada_hi"), sem("ada_lo")
        g_hi, g_lo = sem("g_hi"), sem("g_lo")
        const_ready = sem("const_ready")
        const_dve = sem("const_dve")
        x_in = sem("x_in")
        vec_in = sem("vec_in")
        c_in = sem("c_in")
        b_in = sem("b_in")
        wr_in = sem("wr_in")
        silu_c = sem("silu_c")
        pro_tr = sem("pro_tr")
        pro_act = sem("pro_act")
        pro_dve = sem("pro_dve")
        ada_mm = sem("ada_mm")
        ada_row = sem("ada_row")
        ada_tr = sem("ada_tr")
        ada_out = sem("ada_out")
        ada_t = sem("ada_turned")
        dchain = sem("dve_order")
        gchain = sem("pool_order")
        stored = sem("stored")
        STEPS = {"mx_in": 256, "bd_zero": 1, "m_hi": 8, "m_lo": 8, "ws_tr": 1, "ws_copy": 1, "ws_masked": 1, "st_tr": 1, "st_copy": 3, "hist_zero": 1,
                 "pj_done": 16, "pj_free0": 8, "pj_free1": 8, "conv_tap": 2 * TAPS_C, "lnc_in": 1, "vxc": 2, "lnc_xc": 2,
                 "lnb_sum": 1, "lnb_sq": 2, "lnb_var": 1, "lnb_root": 1, "lnc_sum": 1, "lnc_sq": 2, "lnc_var": 1,
                 "lnc_root": 1, "lnc_hat": 2, "pool_out": 1, "pooled": 1, "pool_mm": 2, "pool_free": 1, "vn_ready": 2,
                 "vt_tr": 1, "vt_copy": 1, "mix_done": 1, "mix_read": 1, "gA": 2, "gB": 2, "gC": 2, "gD": 2,
                 "g_sq": 8, "g_sum": 4, "g_root": 4, "merged": 8, "po_done": 8, "po_free": 8,
                 "tail_tr": 7, "tail_copy": 7, "tail_out": 128}
        s = {name: sem(name) for name in STEPS}

        def step(l, name, n):
            return s[name], STEPS[name] * l + n

        NORM_STEPS = {"up": KD, "sq": KD, "sum": 1, "root": 1, "xhat": KD, "hi": KD, "h": KD, "hs": 1, "rec": 1}
        ns = {k: sem(f"norm_{k}") for k in NORM_STEPS}

        def norm_step(tag, k, n):
            return ns[k], NORM_STEPS[k] * tag + n

        ff_done, ff_act, ff_free = sem("ff_done"), sem("ff_act"), sem("ff_free")
        fy_done, fy_free = sem("fy_done"), sem("fy_free")
        R = {k: sem(f"moe_{k}") for k in ["lg", "lg_ev", "lg_tr", "mask", "pre", "route", "gate",
                                          "zero", "h_tr", "h_row", "in_tr", "in_ev", "in_ev1",
                                          "f_done", "f_act", "f_free", "y_done", "y_free", "yt_tr", "yt_ev",
                                          "y_out", "count", "exp_d", "diag", "g_mm", "g_ev", "x_tr", "x_ev",
                                          "ya", "ss", "ssr", "rr", "scaled", "mods", "const"]}
        Rout = [sem(f"moe_rows_out{t}") for t in range(NT)]
        Rwide = [sem(f"moe_wide_in{t}") for t in range(2, NT)]
        Rin = [sem(f"moe_in{s}") for s in range(2)]
        Rback = [[sem(f"moe_back{t}_{r}") for r in range(2)] for t in range(NT)]
        gf_in = sem("gf_in")
        fin_ev, fin_out = sem("fin_ev"), sem("fin_out")

        def slot(n, k, cols):
            return cut(mem, (n % RING) * SLOT, k, cols)

        def ada_slot(j):
            return cut(mem, (j % ADA_RING) * SLOT, KD, 256)

        def expert_slot(j, k, cols):
            return cut(mem, (j % EXPERT_RING) * EXPERT_SLOT, k, cols)

        def tokens_of(eng, e):
            return eng.value_load(count[0:1, bass.ds(e, 1)], min_val=0, max_val=T)

        def first_of(eng, e):
            return eng.value_load(first[0:1, bass.ds(e, 1)], min_val=0, max_val=PICKS)

        w_in_v = [A["w_in"][l].rearrange("(k p) (b n) -> b p k n", p=P, n=256) for l in range(DEPTH)]
        w_out_v = [A["w_out"][l].rearrange("(k p) (b n) -> b p k n", p=P, n=256) for l in range(DEPTH)]
        w_ada_v = [A["w_ada"][l].rearrange("(k p) (b n) -> b p k n", p=P, n=256) for l in range(DEPTH)]
        w1_v = A["w1_dense"][0].rearrange("(k p) n -> p k n", p=P)
        w3_v = A["w3_dense"][0].rearrange("(k p) n -> p k n", p=P)
        w2_v = A["w2_dense"][0].rearrange("(g k p) (b n) -> g b p k n", g=2, p=P, n=P)

        def expert_chunk(e, j):
            if j < 8:
                w = A["w1_moe" if j % 2 == 0 else "w3_moe"][0]
                n = P * min(3, ET - 3 * (j // 2))
                return w[e].rearrange("(k p) n -> p k n", p=P)[:, :, (j // 2) * 384:(j // 2) * 384 + n], KD, n
            return A["w2_moe"][0][e].rearrange("(k p) n -> p k n", p=P)[:, :, (j - 8) * 256:(j - 7) * 256], ET, 256

        def chunk(n):
            for base, v in ((WIN0, w_in_v[0]), (WIN1, w_in_v[1])):
                if base <= n < base + 8:
                    return v[ORDER[n - base]], KD, 256
            for base, v in ((WOUT0, w_out_v[0]), (WOUT1, w_out_v[1])):
                if base <= n < base + 4:
                    return v[n - base], KD, 256
            h, c = divmod(n - DENSE, PER_H)
            if c < 12:
                f, m = FH * h + 2 * (c // 2), P * min(2, FH - 2 * (c // 2))
                return (w1_v, w3_v)[c % 2][:, :, P * f:P * f + m], KD, m
            return w2_v[h][c - 12], FH, P

        def released(n):
            for l, base in ((0, WIN0), (1, WIN1)):
                if base <= n < base + 8:
                    return step(l, "pj_done", 2 * (n - base) + 2)
            for l, base in ((0, WOUT0), (1, WOUT1)):
                if base <= n < base + 4:
                    return step(l, "po_done", 2 * (n - base) + 2)
            h, c = divmod(n - DENSE, PER_H)
            if c < 12:
                return ff_done, FH * h + min(2 * (c // 2) + 2, FH)
            return fy_done, KD * h + c - 12 + 1

        unit = []
        for l in range(DEPTH):
            unit += [((WIN0, WIN1)[l] + q // 2, q % 2, KD, 256, step(l, "pj_done", q + 1)) for q in range(16)]
            unit += [((WOUT0, WOUT1)[l] + q // 2, q % 2, KD, 256, step(l, "po_done", q + 1)) for q in range(8)]
            for h in range(2) if l == 0 else ():
                unit += [(DENSE + PER_H * h + 2 * (f // 2) + w, f % 2, KD, P * min(2, FH - 2 * (f // 2)), (ff_done, FH * h + f + 1))
                         for f in range(FH) for w in range(2)]
                unit += [(DENSE + PER_H * h + 12 + q, 0, FH, P, (fy_done, KD * h + q + 1)) for q in range(KD)]

        def w_of(u):
            n, part, k, cols, _ = unit[u]
            return slot(n, k, cols)[:, :, P * part:P * part + P], cut(mem, RING * SLOT + (u % UNIT_SLOTS) * UNIT, k, P)

        block = ctx.enter_context(nc.Block())

        @block.sync
        def _(sp):
            def load(n, src):
                ap, k, cols = src
                sp.dma_start(slot(n, k, cols), ap).then_inc(full[n % RING], 16)

            def eload(j, src):
                ap, k, cols = src
                sp.dma_start(expert_slot(j, k, cols), ap).then_inc(efull[j % EXPERT_RING], 16)

            def mixer_loads(l):
                sp.wait_ge(*step(l, "bd_zero", 1))
                if l:
                    sp.wait_ge(R["zero"], 16)
                    sp.wait_ge(*norm_step(2 * l - 1, "up", KD))
                sp.dma_start(ws_raw, A["w_s"][l].rearrange("h t s -> t h s")).then_inc(s["mx_in"], 16)
                for h in range(4):
                    r = slice(64 * (h % 2), 64 * (h % 2) + 64)
                    sp.dma_start(bsb[r, h // 2, :], A["b_s"][l, h:h + 1, :].to_broadcast([64, P])).then_inc(s["mx_in"], 16)
                    sp.dma_start(ws00[r, h // 2:h // 2 + 1], A["w_s"][l, h, 0:1, 0:1].to_broadcast([64, 1])).then_inc(s["mx_in"], 16)
                for g in range(4):
                    r = slice(64 * (g % 2), 64 * (g % 2) + 64)
                    sp.dma_start(bd[r, g // 2, r], A["pool_w"][l, g]).then_inc(s["mx_in"], 16)
                sp.dma_start(stA[0:2 * NS], A["state_conv_a"][l].rearrange("b r c -> (b r) c")).then_inc(s["mx_in"], 16)
                sp.dma_start(stC[0:120], A["state_conv_c"][l].rearrange("(g b) r c -> (b r) g c", g=2)).then_inc(s["mx_in"], 16)
                sp.dma_start(stD[0:120], A["state_pool_d"][l].rearrange("b r c -> (b r) c")).then_inc(s["mx_in"], 16)
                sp.dma_start(O["a_s"][l, :, 0:1, :], A["state_conv_a"][l, :, 1:2, :]).then_inc(stored, 16)
                sp.dma_start(O["c_s"][l, :, 0:29, :], A["state_conv_c"][l, :, 1:30, :]).then_inc(stored, 16)
                sp.dma_start(O["d_s"][l, :, 0:14, :], A["state_pool_d"][l, :, 1:15, :]).then_inc(stored, 16)

            def ada_load(j, l, b):
                sp.dma_start(ada_slot(j), w_ada_v[l][b]).then_inc(efull[j], 16)

            sp.dma_start(crow[0:1], A["c_prompt"]).then_inc(c_in, 16)
            sp.dma_start(crow[1:NQ], A["c_sample"]).then_inc(c_in, 16)
            sp.dma_start(rows[0:96, 2, :], A["b_ada"].rearrange("l (r p) -> (l r) p", p=P)).then_inc(b_in, 16)
            for j in range(ADA_RING):
                ada_load(j, 0, j)
            for l in range(DEPTH):
                with sp.Fori(0, NA - 1) as i:
                    for j in range(ADA_RING):
                        used = sp.snap(sp.to_reg(24 * l + ADA_RING * i + j + 4))
                        sp.wait_ge(const_ready, 1)
                        sp.wait_ge(ada_mm, used)
                        ada_load(j, l, ADA_RING * i + ADA_RING + j)
                if l == 0:
                    for v in range(DEPTH):
                        for name, (at, n) in ROWS.items():
                            src = A[name][v]
                            if name in ("g_out", "conv_a_w", "conv_c_w"):
                                src = src.rearrange("a (r p) -> (a r) p", p=P)
                            else:
                                src = src.rearrange("(r p) -> r p", p=P)
                            sp.dma_start(rows[at:at + n, v, :], src).then_inc(vec_in, 16)
                    for t in range(4):
                        sp.dma_start(xin[:, t, :], A["x_prompt"][0, P * t:P * t + P, :]).then_inc(x_in, 16)
                    sp.dma_start(xin[0:NS, 4, :], A["x_sample"].rearrange("b s d -> (b s) d")).then_inc(x_in, 16)
                    mixer_loads(0)
                for j in range(ADA_RING if l == 0 else RING):
                    sp.wait_ge(ada_mm, 24 * l + 24 - ADA_RING + j + 4)
                    if l == 0:
                        ada_load(j, 1, j)
                    else:
                        load(WIN0 + j, chunk(WIN0 + j))
            for n in range(WIN0, MOE - RING):
                sp.wait_ge(*released(n))
                load(n + RING, chunk(n + RING))
                if n == DENSE:
                    mixer_loads(1)
            sp.wait_ge(*step(1, "po_done", KD))
            for j in range(EXPERT_RING):
                eload(j, expert_chunk(0, j))

            def used(e, j):
                if j < 8:
                    return R["f_done"], ET * e + min(3 * (j // 2) + 3, ET)
                return R["y_done"], KD * e + 2 * (j - 8) + 2

            def first_rows(row):
                for t in range(2):
                    sp.dma_start(stage[:, t, :], Hd[bass.ds(row + P * t, P), :]).then_inc(Rin[t], 16)

            def rest_of_rows(e):
                c, row = tokens_of(sp, e), first_of(sp, e)
                with sp.If(c <= NW):
                    for t in range(2, NT):
                        sp.sem_inc(Rwide[t - 2], 16)
                with sp.Else():
                    for t in range(2, NT):
                        free = sp.snap(sp.to_reg(NT * e + t - 1))
                        sp.wait_ge(const_ready, 1)
                        sp.wait_ge(R["in_tr"], free)
                        sp.dma_start(stage[:, t % 2, :], Hd[bass.ds(row + AT[t], P), :]).then_inc(Rwide[t - 2], 16)

            def rows_out(e):
                c, row = tokens_of(sp, e), first_of(sp, e)
                with sp.If(c <= NW):
                    sp.sem_inc(R["y_out"], 16 * (NT - 2))
                    for t in range(2):
                        there = sp.snap(sp.to_reg(NT * e + NT + t))
                        sp.wait_ge(const_ready, 1)
                        sp.wait_ge(R["yt_ev"], there)
                        sp.dma_start(Yd[bass.ds(row + P * t, P), :], yrow[:, t, :]).then_inc(R["y_out"], 16)
                with sp.Else():
                    for t in range(NT):
                        there = sp.snap(sp.to_reg(NT * e + t + 2))
                        sp.wait_ge(const_ready, 1)
                        sp.wait_ge(R["yt_ev"], there)
                        sp.dma_start(Yd[bass.ds(row + AT[t], P), :], stage[:, 2, :]).then_inc(R["y_out"], 16)

            sp.wait_ge(R["count"], 2)
            row0 = first_of(sp, 0)
            for t in range(NT):
                sp.wait_ge(Rout[t], 32)
            first_rows(row0)
            with sp.Fori(0, NE - 1) as e:
                rest_of_rows(e)
                row = first_of(sp, e + 1)
                free = sp.snap(sp.to_reg(NT * e + NT))
                sp.wait_ge(const_ready, 1)
                sp.wait_ge(R["in_tr"], free)
                first_rows(row)
                for j in range(PER_E):
                    which, n = used(e, j)
                    n = sp.snap(sp.to_reg(n))
                    sp.wait_ge(const_ready, 1)
                    sp.wait_ge(which, n)
                    j += EXPERT_RING
                    eload(j, expert_chunk(e, j) if j < PER_E else expert_chunk(e + 1, j - PER_E))
                rows_out(e)
            last = sp.snap(sp.to_reg(NE - 1))
            rest_of_rows(last)
            for j in range(PER_E - EXPERT_RING):
                sp.wait_ge(*used(NE - 1, j))
                eload(j + EXPERT_RING, expert_chunk(NE - 1, j + EXPERT_RING))
            rows_out(last)
            for t in range(NT):
                n = min(P, T - P * t)
                sp.wait_ge(fin_ev, t + 1)
                dst = O["y_prompt"][0, P * t:P * t + n, :] if t < 4 else O["y_sample"].rearrange("b s d -> (b s) d")
                sp.dma_start(dst, yg[0:n, t, 1, :]).then_inc(fin_out, 16)
            sp.wait_ge(fin_out, 16 * NT)
            sp.wait_ge(stored, 16 * 3 * DEPTH)
            for l in range(DEPTH):
                sp.wait_ge(*step(l, "tail_out", 16 * 8))

        XB = [2, 3, 0, 1, 2]
        YB = [0, 1, 3]
        GO = [0, 2, 3, 1]
        READY = {0: "gA", 1: "gB", 2: "gC", 3: "gD"}

        @block.gpsimd
        def _(pool):
            order = [0]

            def link(ins):
                order[0] += 1
                ins.then_inc(gchain, 1)
                pool.wait_ge(gchain, order[0])

            pool.sem_inc(ada_out, 1)
            link(pool.memset(modrow[:], 0.0))
            link(pool.memset(ident[:], 0.0))
            pool.affine_select(out=ident[:], in_=ident[:], compare_op=ALU.not_equal, fill=1.0, base=0,
                               pattern=[[-1, P]], channel_multiplier=1).then_inc(const_ready, 1)
            pool.iota(cinv[:], pattern=[[0, 2], [1, POOL]], base=1, channel_multiplier=0,
                      allow_small_or_imprecise_dtypes=True).then_inc(const_ready, 1)
            link(pool.memset(tri[:], 1.0))
            link(pool.memset(valid[:], 1.0))
            link(pool.memset(valid[:, NT - 1:NT], 0.0))
            pool.memset(valid[0:NS, NT - 1:NT], 1.0)
            pool.affine_select(out=tri[:], in_=tri[:], compare_op=ALU.is_gt, fill=0.0, base=0,
                               pattern=[[1, P]], channel_multiplier=-1).then_inc(R["const"], 1)
            pool.iota(eidx[:], pattern=[[1, NE]], base=0, channel_multiplier=0,
                      allow_small_or_imprecise_dtypes=True).then_inc(R["const"], 1)
            pool.memset(ebase[:], 0.0).then_inc(R["const"], 1)


            pool.memset(bd, 0.0).then_inc(s["bd_zero"], 1)

            pool.wait_ge(pro_dve, 2)
            for l in range(DEPTH):
                bad = bada[:, 48 * l:48 * l + 48].rearrange("p (b m) -> p b m", m=2)
                mv, ml = (x[:, l].rearrange("p (b m) q -> p b m q", m=2) for x in (mod, mod_lo))
                with pool.Fori(0, NA) as i:
                    for g in range(2):
                        there = pool.snap(pool.to_reg(2 * NA * l + 2 * i + g + 1))
                        pool.wait_ge(const_ready, 1)
                        pool.wait_ge(ada_t, there)
                        for m in range(2):
                            c = turned[:, m * P:m * P + 96].rearrange("p (b q) -> p b q", b=3)
                            at = bass.ds(ADA_RING * i + 3 * g, 3)
                            pool.tensor_tensor(mv[:, at, m], c[:, :, 0:NQ], bad[:, at, m].unsqueeze(2).to_broadcast([P, 3, NQ]), ALU.add)
                            last = pool.tensor_copy(ml[:, at, m], c[:, :, NQ:2 * NQ])
                        last.then_inc(ada_out, 1)

            def lower(*units):
                for u in units:
                    raw, hi = w_of(u)
                    pool.wait_ge(w_hi, u + 1)
                    pool.tensor_tensor(r_(raw), raw, read_(hi), ALU.subtract).then_inc(w_lo, 1)

            def norm_samples(tag, l, scale, shift):
                split = tag < 3
                xs, hi = xT[:, :, SEQ:T], hT[:, :, SEQ:T]
                hs = hlo[:, :, SEQ:T] if split else hi
                pool.wait_ge(*norm_step(tag, "rec", 1))
                link(pool.tensor_tensor(hs, xs, stat[:, SEQ:T].unsqueeze(1).to_broadcast([P, KD, NS]), ALU.mult))
                link(pool.tensor_tensor(hs, hs, mod[:, l, 8 * scale:8 * scale + 8, 1:NQ], ALU.mult))
                last = pool.tensor_tensor(hs, hs, mod[:, l, 8 * shift:8 * shift + 8, 1:NQ], ALU.add)
                if split:
                    link(last)
                    link(pool.tensor_copy(r_(hi), hs))
                    last = pool.tensor_tensor(r_(hs), hs, read_(hi), ALU.subtract)
                last.then_inc(ns["hs"], 1)

            for l in range(DEPTH):
                lower(U_IN[l], U_IN[l] + 1)
                norm_samples(2 * l, l, SCALE1, SHIFT1)
                lower(U_IN[l] + 2, U_IN[l] + 3)
                if l == 0:
                    pool.wait_ge(pro_tr, 12)
                    pool.wait_ge(R["mods"], 1)
                else:
                    pool.wait_ge(fy_done, 2 * KD)
                pool.memset(zin[:, :, 0:TAPS_A - 1], 0.0)
                pool.memset(gin[:, :, 0:TAPS_C - 1], 0.0)
                pool.memset(pin[:, :, 0:POOL - 1], 0.0).then_inc(s["hist_zero"], 1)
                pool.wait_ge(*step(l, "ws_copy", 1))
                pool.affine_select(out=wsT, in_=wsT, compare_op=ALU.is_ge, fill=0.0, base=0,
                                   pattern=[[0, 4], [1, P]], channel_multiplier=-1).then_inc(s["ws_masked"], 1)
                lower(*range(U_IN[l] + 4, U_IN[l] + 11))
                pool.wait_ge(*step(l, "pj_free0", 4))
                pool.wait_ge(*step(l, "pj_free1", 4))
                lo, hi, n = slice(0, 64), slice(64, P), SEQ + 15

                def doubled(dst, src, back, a):
                    return pool.tensor_tensor(dst[..., a:n], src[..., a:n], src[..., a - back:n - back], ALU.add)

                def last(dst_rows, ct, src, back):
                    return pool.tensor_tensor(outs[dst_rows, 6 + ct, 0:SEQ], src[dst_rows, ct, 15:n],
                                              src[dst_rows, ct, 15 - back:n - back], ALU.add)
                link(doubled(pa, pin, 1, 1))
                lower(U_IN[l] + 11)
                link(last(lo, 0, pin, 1))
                link(last(hi, 0, pa, 2))
                lower(U_IN[l] + 12)
                link(doubled(pb[:, 1], pa[:, 1], 2, 3))
                link(last(lo, 1, pb, 4))
                lower(U_IN[l] + 13)
                link(doubled(pa[:, 1], pb[:, 1], 4, 7))
                last(hi, 1, pa, 8).then_inc(s["pool_out"], 1)
                pool.wait_ge(*step(l, "pool_out", 1))
                lower(U_IN[l] + 14, U_IN[l] + 15)
                lower(*range(U_OUT[l], U_OUT[l] + 4))
                for i, j in enumerate(2 * g + ct for g in GO for ct in range(2)):
                    pool.wait_ge(*step(l, "m_hi", i + 1))
                    pool.tensor_tensor(r_(hlo[:, j, :]), hlo[:, j, :], read_(hT[:, j, :]), ALU.subtract).then_inc(s["m_lo"], 1)
                pool.wait_ge(*step(l, "vt_copy", 1))
                pool.dma_start(O["v_p"][l, 0], vtok[:, 3, :]).then_inc(s["tail_out"], 16)
                for n, dst in enumerate([O["a_p"][l, 0], O["c_p"][l, 0], O["d_p"][l, 0], O["a_s"][l, :, 1, :],
                                         O["c_s"][l, :, 29, :], O["d_s"][l, :, 14, :], O["v_s"][l, :, 0, :]]):
                    pool.wait_ge(*step(l, "tail_copy", n + 1))
                    pool.dma_start(dst, outrow[0:TAIL[n], n, :]).then_inc(s["tail_out"], 16)
                lower(*range(U_OUT[l] + 4, U_OUT[l] + 8))
                if l == 0:
                    lower(24, 25)
                    norm_samples(1, l, SCALE2, SHIFT2)
                    lower(26, 27)
                    pool.wait_ge(*norm_step(1, "up", KD))
                    link(pool.memset(stage[0:T // 5, 2, :], 0.0))
                    pool.dma_start(Hd[PICKS:ROOM].rearrange("(a p) n -> p a n", a=5),
                                   stage[0:T // 5, 2:3, :].to_broadcast([T // 5, 5, D])).then_inc(R["zero"], 16)
                    pool.memset(bd, 0.0).then_inc(s["bd_zero"], 1)
                    lower(*range(28, U_IN[1]))
                else:
                    norm_samples(3, l, SCALE2, SHIFT2)
            pool.wait_ge(R["zero"], 16)
            for t in range(NT):
                n = min(P, T - P * t)
                pool.wait_ge(R["h_row"], t + 1)
                pool.wait_ge(R["route"], 1)
                for r in range(2):
                    pool.indirect_dma_start(Hd, bass.IndirectOffsetOnAxis(ap=place[0:n, r, t:t + 1], axis=0),
                                            hrow[t][0:n], None).then_inc(Rout[t], 16)
            pool.wait_ge(R["y_out"], 16 * NE * NT + 16)
            pool.wait_ge(R["y_done"], NE * KD)
            for t in range(NT):
                n = min(P, T - P * t)
                for r in range(2):
                    pool.indirect_dma_start(yg[0:n, t, r, :], None, Yd[0:PICKS],
                                            bass.IndirectOffsetOnAxis(ap=place[0:n, r, t:t + 1], axis=0)).then_inc(Rback[t][r], 16)

            pool.wait_ge(gf_in, 16)
            for t in range(NT):
                a = yg[0:min(P, T - P * t), t, 1, :]
                pool.wait_ge(R["scaled"], t + 1)
                pool.tensor_tensor(a, a, gf[0:min(P, T - P * t)], ALU.mult).then_inc(fin_ev, 1)

        NVEC = len(ROWS) * DEPTH
        @block.tensor
        def _(pe):
            def gemm(q, lhs, rhs, kn):
                for k in range(kn):
                    for h in range(2):
                        mm = pe.matmul(PP[q][:, h, 0:HT], lhs(k), rhs(k)[:, HT * h:HT * h + HT],
                                       start=(k == 0), stop=(k == kn - 1))
                return mm

            def channel_sum(q, tiles):
                return gemm(q, lambda k: ones[:], lambda k: tiles[k], len(tiles))

            def norm_sum(tag, j):
                pe.wait_ge(*norm_step(tag, "sq", j + 1))
                for h in range(2):
                    mm = pe.matmul(PP[2][:, h, 0:HT], ones[:], work[:, j, HT * h:HT * h + HT],
                                   start=(j == 0), stop=(j == KD - 1))
                if j == KD - 1:
                    mm.then_inc(ns["sum"], 1)

            def product(q, u, hi, lo, order, before=None):
                pe.wait_ge(w_lo, u + 1)
                wl, wh = w_of(u)
                for i, k in enumerate(order):
                    if before is not None:
                        before(i)
                    for w, x in ((wh, hi), (wh, lo), (wl, hi)):
                        for h in range(2):
                            mm = pe.matmul(PP[q][:, h, 0:HT], r_(w[:, k, :]), r_(x[:, k, HT * h:HT * h + HT]),
                                           start=(i == 0 and w is wh and x is hi), stop=(i == len(order) - 1 and w is wl))
                return mm

            def two_products(q, u, hi, lo, order, before):
                pe.wait_ge(w_lo, u + 2)
                for i, k in enumerate(order):
                    before(i)
                    for c in range(2):
                        wl, wh = w_of(u + c)
                        for w, x in ((wh, hi), (wh, lo), (wl, hi)):
                            for h in range(2):
                                mm = pe.matmul(PP[q + c][:, h, 0:HT], r_(w[:, k, :]), r_(x[:, k, HT * h:HT * h + HT]),
                                               start=(i == 0 and w is wh and x is hi), stop=(i == len(order) - 1 and w is wl))
                return mm

            def h_tile(tag):
                def before(k):
                    if k == 0:
                        pe.wait_ge(*norm_step(tag, "hs", 1))
                    pe.wait_ge(*norm_step(tag, "h", k + 1))
                return before

            pe.wait_ge(const_ready, 1)
            pe.wait_ge(silu_c, 1)
            for j in range(KD):
                tr = pe.transpose(PP[3][:, 0, j * NQ:(j + 1) * NQ], crow[0:NQ, j * P:(j + 1) * P], ident[0:NQ, 0:NQ])
            tr.then_inc(pro_tr, 1)
            pe.wait_ge(b_in, 16)
            pe.transpose(PP[2][:, 1, 0:96], rows[0:96, 2, :], ident[0:96, 0:96]).then_inc(pro_tr, 1)
            pe.wait_ge(pro_dve, 1)
            pe.sem_inc(ada_mm, 3)
            for l in range(DEPTH):
                with pe.Fori(0, NA) as i:
                    for j in range(ADA_RING):
                        n = 24 * l + ADA_RING * i + j
                        pe.wait_ge(ada_lo, n + 1)
                        pe.wait_ge(ada_row, n + 1)
                        for k in range(KD):
                            for lower, w in enumerate((ahi[:, j % 3], ada_slot(j))):
                                mm = pe.matmul(PP[0][0:2 * NQ, j % 2, 0:256], r_(cs[:, k, :]), r_(w[:, k, :]),
                                               start=(k == 0 and not lower), stop=(k == KD - 1 and bool(lower)))
                        mm.then_inc(ada_mm, 1)
                        if j % 3 == 2:
                            pe.wait_ge(ada_row, n + 3)
                            for m in range(2):
                                tr = pe.transpose(PP[1][:, 0, m * P:(m + 1) * P], modrow[:, m * P:(m + 1) * P], ident[:])
                            tr.then_inc(ada_tr, 1)
                if l == 0:
                    pe.wait_ge(vec_in, 16 * NVEC)
                    pe.wait_ge(pro_dve, 2)
                    for v in range(DEPTH):
                        tr = pe.transpose(PP[3][:, 0, v * NROWS:(v + 1) * NROWS], rows[0:NROWS, v, :], ident[0:NROWS, 0:NROWS])
                    tr.then_inc(pro_tr, 1)
                    pe.wait_ge(x_in, 16 * NT)
                    for j in range(KD):
                        if j >= 2:
                            pe.wait_ge(*((pro_dve, 3 + j // 2) if j % 2 == 0 else (pro_act, j // 2)))
                        for t in range(4):
                            tr = pe.transpose(PP[2][:, j % 2, t * P:(t + 1) * P], xin[:, t, j * P:(j + 1) * P], ident[:])
                        tr.then_inc(pro_tr, 1)
                    for j in range(KD):
                        tr = pe.transpose(PP[3][:, 1, j * NS:(j + 1) * NS], xin[0:NS, 4, j * P:(j + 1) * P], ident[0:NS, 0:NS])
                    tr.then_inc(pro_tr, 1)
                    pe.wait_ge(pro_dve, 8)
                    pe.wait_ge(const_dve, 1)
                    for j in range(KD):
                        norm_sum(0, j)

            for l in range(DEPTH):
                pe.wait_ge(*step(l, "mx_in", 16 * 16))
                if l:
                    pe.wait_ge(fy_free, 2 * KD - 1)
                else:
                    pe.wait_ge(pro_dve, 8)
                    pe.wait_ge(pro_act, 4)
                for h in range(4):
                    tr = pe.transpose(PP[3][:, 0, h * P:(h + 1) * P], ws_raw[:, h, :], ident[:])
                tr.then_inc(s["ws_tr"], 1)
                for ct in range(2):
                    c = slice(ct * P, ct * P + P)
                    pe.transpose(PP[3][:, 1, 16 * ct:16 * ct + 16], stA[0:16, c], ident[0:16, 0:16])
                    for g in range(2):
                        at = 32 + 240 * ct + 120 * g
                        pe.transpose(PP[3][:, 1, at:at + 120], stC[0:120, g, c], ident[0:120, 0:120])
                    tr = pe.transpose(PP[0][:, 0, 120 * ct:120 * ct + 120], stD[0:120, c], ident[0:120, 0:120])
                tr.then_inc(s["st_tr"], 1)
                if l:
                    norm_sum(2 * l, KD - 1)
                for q in range(16):
                    if q >= 2:
                        pe.wait_ge(*step(l, f"pj_free{q % 2}", q // 2))
                    if q == 0:
                        pe.wait_ge(*step(l, "st_copy", 3))
                        two_products(0, U_IN[l], hT, hlo, range(KD), h_tile(2 * l)).then_inc(s["pj_done"], 1)
                        pe.wait_ge(*step(l, "pj_done", 1))
                        pe.sem_inc(s["pj_done"], 1)
                    if q >= 2:
                        product(q % 2, U_IN[l] + q, hT, hlo, range(KD)).then_inc(s["pj_done"], 1)
                    if q == 11:
                        pe.wait_ge(*step(l, "pj_free0", 3))
                        pe.wait_ge(*step(l, "pj_free1", 3))
                        channel_sum(2, [proj[:, HOME[B_V] + ct, :] for ct in range(2)]).then_inc(s["lnb_sum"], 1)
                        pe.wait_ge(*step(l, "lnc_in", 1))
                        channel_sum(3, [outs[:, 4 + ct, :] for ct in range(2)]).then_inc(s["lnc_sum"], 1)
                    if q == 13:
                        pe.wait_ge(*step(l, "lnb_sq", 2))
                        channel_sum(2, [proj[:, HOME[C_G] + ct, :] for ct in range(2)]).then_inc(s["lnb_var"], 1)
                        pe.wait_ge(*step(l, "lnc_sq", 2))
                        channel_sum(3, [proj[:, HOME[A_H] + ct, :] for ct in range(2)]).then_inc(s["lnc_var"], 1)
                pe.wait_ge(*step(l, "vn_ready", 2))
                pe.wait_ge(*step(l, "lnc_root", 1))
                for n in range(4):
                    for ct in range(2):
                        tr = pe.transpose(PP[3][:, n // 2, (n % 2) * W + ct * P:(n % 2) * W + ct * P + P],
                                          proj[:, HOME[B_V] + ct, n * P:(n + 1) * P], ident[:])
                tr.then_inc(s["vt_tr"], 1)
                pe.wait_ge(*step(l, "vt_copy", 1))
                pe.wait_ge(*step(l, "ws_masked", 1))
                pe.wait_ge(*step(l, "pj_free0", 8))
                pe.wait_ge(*step(l, "pj_free1", 8))
                for n in range(4):
                    for ct in range(2):
                        mm = pe.matmul(PP[n // 2][:, n % 2, ct * 256:ct * 256 + 256], vtok[:, n, ct * P:(ct + 1) * P],
                                       wsT[:, 2 * ct:2 * ct + 2, :].rearrange("p h t -> p (h t)"), start=True, stop=True)
                mm.then_inc(s["mix_done"], 1)
                pe.wait_ge(*step(l, "pooled", 1))
                for ct in range(2):
                    gemm(2 + ct, lambda k: bd[:, ct, :], lambda k: outs[:, 6 + ct, :], 1).then_inc(s["pool_mm"], 1)
                pe.wait_ge(*step(l, "gD", 2))
                for i, g in enumerate(GO):
                    pe.wait_ge(*step(l, "g_sq", 2 * i + 2))
                    if i == 2:
                        pe.wait_ge(*step(l, "mix_read", 1))
                    channel_sum((i + 2) % 4, [hT[:, 2 * g + ct, :] for ct in range(2)]).then_inc(s["g_sum"], 1)
                pe.wait_ge(*step(l, "g_root", 2))
                src = [zin[:, :, SEQ:SEQ + 2], gin[:, :, SEQ:SEQ + 30], pin[:, :, SEQ:SEQ + 15], zin[:, :, SEQ + 2:SEQ + 10],
                       gin[:, :, SEQ + 30:SEQ + 38], pin[:, :, SEQ + 15:SEQ + 23],
                       proj[:, HOME[B_V]:HOME[B_V] + 2, SEQ:T]]
                for n, (a, m) in enumerate(zip(src, TAIL)):
                    for ct in range(2):
                        tr = pe.transpose(tail_bank(n)[0:m, ct * P:(ct + 1) * P], a[:, ct, :], ident[:])
                    tr.then_inc(s["tail_tr"], 1)
                pe.wait_ge(*step(l, "g_root", 4))
                for q in range(KD):
                    if q >= 2:
                        pe.wait_ge(*step(l, "po_free", q - 1))
                        product(q % 2, U_OUT[l] + q, hT, hlo, range(KD)).then_inc(s["po_done"], 1)
                    if q == 0:
                        two_products(0, U_OUT[l], hT, hlo, [2 * g + ct for g in GO for ct in range(2)],
                                     lambda i: pe.wait_ge(*step(l, "m_lo", i + 1))).then_inc(s["po_done"], 1)
                        pe.wait_ge(*step(l, "po_done", 1))
                        pe.sem_inc(s["po_done"], 1)
                    if q == 1:
                        pe.wait_ge(*step(l, "tail_copy", 7))
                    if q >= 2:
                        norm_sum(2 * l + 1, q - 2)
                norm_sum(2 * l + 1, KD - 2)
                norm_sum(2 * l + 1, KD - 1)
                if l == 0:
                    for h in range(2):
                        if h:
                            pe.wait_ge(fy_free, KD)
                        for f in range(FH):
                            if f >= 2:
                                pe.wait_ge(ff_free, FH * h + f - 1)
                            if h == f == 0:
                                mm = two_products(0, U_FF(0, 0, 0), hT, hlo, range(KD), h_tile(1))
                            else:
                                for w in range(2):
                                    mm = product(2 * (f % 2) + w, U_FF(h, f, w), hT, hlo, range(KD))
                            mm.then_inc(ff_done, 1)
                        pe.wait_ge(ff_free, FH * (h + 1))
                        for q in range(KD):
                            if q >= 3:
                                pe.wait_ge(fy_free, KD * h + q - 2)
                            product(YB[q % 3], U_FY(h, q), G, Glo, range(FH),
                                    (lambda k: pe.wait_ge(g_lo, FH * h + k + 1)) if q == 0 else None).then_inc(fy_done, 1)
                            if h and q:
                                norm_sum(2, q - 1)

            pe.wait_ge(wr_in, 32)
            pe.wait_ge(*norm_step(3, "hs", 1))
            for k in range(KD):
                pe.wait_ge(*norm_step(3, "h", k + 1))
                for h in range(2):
                    gemm_r = pe.matmul(PP[0][0:NE, h, 0:HT], wrt[:, k, :], hT[:, k, HT * h:HT * h + HT],
                                       start=(k == 0), stop=(k == KD - 1))
            gemm_r.then_inc(R["lg"], 1)
            pe.wait_ge(R["lg_ev"], 1)
            for t in range(NT):
                n = min(P, T - P * t)
                tr = pe.transpose(PP[1][0:n, 0, t * NE:(t + 1) * NE], lgT[0:NE, P * t:P * t + n], ident[0:NE, 0:NE])
            tr.then_inc(R["lg_tr"], 1)
            def h_rows(t):
                n = min(P, T - P * t)
                if t >= 2:
                    pe.wait_ge(R["h_row"], t - 1)
                for j in range(KD):
                    tr = pe.transpose(PP[2 + t % 2][0:n, j // 4, (j % 4) * P:(j % 4) * P + P], hT[:, j, P * t:P * t + n], ident[:])
                tr.then_inc(R["h_tr"], 1)
            for t in range(3):
                h_rows(t)
            pe.wait_ge(R["mask"], 1)
            mflat = mask[:].rearrange("p t e -> p (t e)")
            pe.matmul(PP[0][:, 0, 0:NT * NE], tri[:], mflat, start=True, stop=True)
            pe.matmul(PP[0][:, 1, 0:NT * NE], ones[:], mflat, start=True, stop=True).then_inc(R["pre"], 1)
            for t in range(3, NT):
                h_rows(t)
            pe.wait_ge(R["route"], 1)


            def chunk_here(e, j):
                pe.wait_ge(efull[j % EXPERT_RING], 16 * (DEPTH * NA + j // EXPERT_RING + 1) + 32 * e)

            def narrow_rows(e):
                pe.sem_inc(R["in_tr"], 1)
                for t in range(2):
                    pe.wait_ge(Rin[t], 16 * e + 16)
                    for h in range(2):
                        for j in range(4 * h, 4 * h + 4):
                            tr = pe.transpose(PP[t][:, h, (j % 4) * P:(j % 4) * P + P], stage[:, t, j * P:(j + 1) * P], ident[:])
                        tr.then_inc(R["in_tr"], 1)

            def narrow_products(e, n):
                for f in range(ET):
                    c = f // 3
                    if f % 3 == 0:
                        chunk_here(e, 2 * c)
                        chunk_here(e, 2 * c + 1)
                    pe.wait_ge(R["f_free"], ET * e + f + 1)
                    m = P * min(3, ET - 3 * c)
                    for w in range(2):
                        for k in range(KD):
                            if f == w == 0 and k == 0:
                                pe.wait_ge(R["in_ev"], NT * e + NT)
                            if f == w == 0 and k == 4:
                                pe.wait_ge(R["in_ev1"], 2 * e + 2)
                            mm = pe.matmul(PP[w][:, f % 2, 0:n], expert_slot(2 * c + w, KD, m)[:, k, P * (f % 3):P * (f % 3) + P],
                                           hn[:, k, 0:n], start=(k == 0), stop=(k == KD - 1))
                    mm.then_inc(R["f_done"], 1)
                pe.wait_ge(R["yt_ev"], NT * e + 1)
                pe.sem_inc(R["yt_tr"], 3)
                for q in range(KD + 1):
                    if q < KD:
                        if q % 2 == 0:
                            chunk_here(e, 8 + q // 2)
                        pe.wait_ge(R["y_free"], KD * e + q + 1)
                        for k in range(ET):
                            if q == 0 and k in (0, ET - 1):
                                pe.wait_ge(R["f_free"], ET * e + (ET + 1 if k == 0 else ET + 2))
                            mm = pe.matmul(PP[2][:, q % 2, 0:n], expert_slot(8 + q // 2, ET, 256)[:, k, P * (q % 2):P * (q % 2) + P],
                                           Gn[:, k, 0:n], start=(k == 0), stop=(k == ET - 1))
                        mm.then_inc(R["y_done"], 1)
                    if q:
                        j = q - 1
                        pe.wait_ge(R["y_free"], KD * e + j + 3)
                        if j == 4:
                            pe.wait_ge(R["yt_ev"], NT * e + 4)
                        for t in range(2):
                            tr = pe.transpose(PP[3][:, t, (j % 4) * P:(j % 4) * P + P], yn[:, j, P * t:P * t + P], ident[:])
                        if j % 4 == 3:
                            tr.then_inc(R["yt_tr"], 1)

            def wide(e):
                pe.wait_ge(R["yt_ev"], NT * e + 1)
                for t in range(NT):
                    if t < 2:
                        pe.wait_ge(Rin[t], 16 * e + 16)
                    else:
                        pe.wait_ge(Rwide[t - 2], 16 * e + 16)
                    if t:
                        pe.wait_ge(R["in_ev"], NT * e + t)
                    for j in range(KD):
                        tr = pe.transpose(PP[3][:, j // 4, (j % 4) * P:(j % 4) * P + P], stage[:, t % 2, j * P:(j + 1) * P], ident[:])
                    tr.then_inc(R["in_tr"], 1)
                pe.wait_ge(R["in_ev"], NT * e + NT)
                for f in range(ET):
                    c = f // 3
                    if f % 3 == 0:
                        chunk_here(e, 2 * c)
                        chunk_here(e, 2 * c + 1)
                    pe.wait_ge(R["f_free"], ET * e + f + 2)
                    m = P * min(3, ET - 3 * c)
                    for w in range(2):
                        mm = gemm(w, lambda k: expert_slot(2 * c + w, KD, m)[:, k, P * (f % 3):P * (f % 3) + P],
                                  lambda k: hexp[:, k, :], KD)
                    mm.then_inc(R["f_done"], 1)
                pe.wait_ge(R["f_free"], ET * e + ET + 2)
                for q in range(KD):
                    if q % 2 == 0:
                        chunk_here(e, 8 + q // 2)
                    pe.wait_ge(R["y_free"], KD * e + q + 2)
                    gemm(2, lambda k: expert_slot(8 + q // 2, ET, 256)[:, k, P * (q % 2):P * (q % 2) + P],
                         lambda k: G[:, k, :], ET).then_inc(R["y_done"], 1)
                pe.wait_ge(R["y_free"], KD * e + KD + 2)
                for t in range(NT):
                    if t:
                        pe.wait_ge(R["yt_ev"], NT * e + t + 1)
                    for j in range(KD):
                        tr = pe.transpose(PP[3][:, j // 4, (j % 4) * P:(j % 4) * P + P], work[:, j, AT[t]:AT[t] + P], ident[:])
                    tr.then_inc(R["yt_tr"], 1)

            def narrow_by_width(e, c, widths):
                if len(widths) == 1:
                    narrow_products(e, widths[0])
                    return
                with pe.If(c <= widths[0]):
                    narrow_products(e, widths[0])
                with pe.Else():
                    narrow_by_width(e, c, widths[1:])

            pe.wait_ge(R["count"], 2)
            with pe.Fori(0, NE) as e:
                c = tokens_of(pe, e)
                with pe.If(c <= NW):
                    narrow_rows(e)
                    narrow_by_width(e, c, WIDTHS)
                with pe.Else():
                    wide(e)
            pe.wait_ge(R["f_free"], ET * NE + 2)
            pe.wait_ge(R["diag"], 1)
            for j in range(KD):
                mm = pe.matmul(PP[0][:, j // 4, (j % 4) * P:(j % 4) * P + P], ones[:], diag[:, j * P:(j + 1) * P],
                               start=True, stop=True)
            mm.then_inc(R["g_mm"], 1)
            for j in range(KD):
                tr = pe.transpose(PP[1][0:NS, j // 4, (j % 4) * P:(j % 4) * P + P], mod[:, 1, 8 * GATE2 + j, 1:NQ], ident[:])
            tr.then_inc(R["g_mm"], 1)
            pe.wait_ge(R["y_free"], KD * NE + 2)
            pe.wait_ge(R["yt_ev"], NT * NE + 1)
            for t in range(NT):
                n = min(P, T - P * t)
                if t in (2, 3):
                    pe.wait_ge(R["g_ev"], t - 1)
                if t == 4:
                    pe.wait_ge(R["x_ev"], 1)
                for j in range(KD):
                    tr = pe.transpose(PP[XB[t]][0:n, j // 4, (j % 4) * P:(j % 4) * P + P], xT[:, j, P * t:P * t + n], ident[:])
                tr.then_inc(R["x_tr"], 1)

        @block.scalar
        def _(act):
            act.wait_ge(c_in, 32)
            act.activation(crow[0:NQ], crow[0:NQ], ACT.Silu).then_inc(silu_c, 1)
            act.dma_start(wrt[:], A["w_router"][0].rearrange("(k p) e -> p k e", p=P)).then_inc(wr_in, 16)
            act.dma_start(brt[:], A["b_router"][0].rearrange("(e a) -> e a", a=1)).then_inc(wr_in, 16)

            act.wait_ge(const_ready, 1)
            def root(q, dst, n, done):
                act.activation(two(dst), pp(q), ACT.Sqrt, bias=eps[:], scale=1.0 / n).then_inc(done, 1)

            def upper(u):
                if u < UNITS:
                    raw, hi = w_of(u)
                    n = unit[u][0]
                    act.wait_ge(full[n % RING], 16 * ((n - WIN0) // RING + 1))
                    if u >= UNIT_SLOTS:
                        act.wait_ge(*unit[u - UNIT_SLOTS][4])
                    act.activation(r_(hi), raw, ACT.Copy).then_inc(w_hi, 1)

            def squares(tag, u):
                for j in range(KD):
                    act.wait_ge(*norm_step(tag, "up", j + 1))
                    act.activation(work[:, j, :], xT[:, j, :], ACT.Square).then_inc(ns["sq"], 1)
                    if tag and j < KD - 2:
                        upper(u + j)

            act.sem_inc(ada_row, 2)
            for l in range(DEPTH):
                def upper_ada(i, j):
                    act.wait_ge(efull[j % ADA_RING], 16 * (NA * l + i + 1 + j // ADA_RING))
                    act.wait_ge(ada_mm, 24 * l + ADA_RING * i + j + 1)
                    act.activation(r_(ahi[:, j % 3]), ada_slot(j), ACT.Copy).then_inc(ada_hi, 1)

                def row_out(i, j):
                    act.wait_ge(ada_mm, 24 * l + ADA_RING * i + j + 4)
                    act.activation(modrow[32 * (j % 3):32 * (j % 3) + 2 * NQ, :], PP[0][0:2 * NQ, j % 2, 0:256],
                                   ACT.Copy).then_inc(ada_row, 1)
                    if j % 3 == 2:
                        act.wait_ge(ada_tr, 2 * (NA * l + i) + j // 3 + 1)
                        act.wait_ge(ada_out, 2 * (NA * l + i) + j // 3 + 1)
                        act.activation(turned, PP[1][:, 0, 0:256], ACT.Copy).then_inc(ada_t, 1)

                upper_ada(0, 0)
                upper_ada(0, 1)
                with act.Fori(0, NA - 1) as i:
                    for j in range(ADA_RING):
                        upper_ada(i, j + 2)
                        row_out(i, j)
                for j in range(ADA_RING):
                    if j + 2 < ADA_RING:
                        upper_ada(NA - 1, j + 2)
                    row_out(NA - 1, j)
                if l == 0:
                    for j in range(1, KD, 2):
                        act.wait_ge(pro_tr, 4 + j)
                        act.activation(xT[:, j, 0:SEQ], PP[2][:, 1, :], ACT.Copy).then_inc(pro_act, 1)
                    act.wait_ge(pro_act, 4)
                    squares(0, None)

            def norm_act(tag, l, shift, u):
                if tag:
                    squares(tag, u)
                act.wait_ge(*norm_step(tag, "sum", 1))
                root(2, stat[:], D, ns["root"])
                for j in (KD - 2, KD - 1) if tag else range(UNIT_SLOTS):
                    upper(u + j)
                for j in range(KD):
                    act.wait_ge(*norm_step(tag, "xhat", j + 1))
                    if tag == 3:
                        act.activation(hT[:, j, 0:SEQ], hT[:, j, 0:SEQ], ACT.Identity,
                                       bias=mod[:, l, 8 * shift + j, 0:1]).then_inc(ns["h"], 1)
                    else:
                        act.activation(r_(hT[:, j, 0:SEQ]), hlo[:, j, 0:SEQ], ACT.Identity,
                                       bias=mod[:, l, 8 * shift + j, 0:1]).then_inc(ns["hi"], 1)

            for l in range(DEPTH):
                if l == 0:
                    act.wait_ge(pro_act, 4)
                    act.wait_ge(const_dve, 1)
                norm_act(2 * l, l, SHIFT1, U_IN[0] if l == 0 else U_FY(1, 0) + UNIT_SLOTS)
                u4 = U_IN[l] + UNIT_SLOTS

                def evac(q, dst, func=ACT.Copy):
                    act.wait_ge(*step(l, "pj_done", q + 1))
                    act.activation(two(dst), pp(q % 2), func).then_inc(s[f"pj_free{q % 2}"], 1)

                for q in (0, 1):
                    evac(q, proj[:, HOME[C_G] + q, :], ACT.Sigmoid)
                    upper(u4 + q)
                for q in (2, 3):
                    upper(u4 + q)
                for q in (4, 5):
                    evac(q, proj[:, HOME[B_V] + q - 4, :])
                    upper(u4 + q)
                act.wait_ge(*step(l, "hist_zero", 1))
                for q in (6, 7):
                    evac(q, pin[:, q - 6, 15:15 + T])
                    upper(u4 + q)
                for q in (8, 9):
                    evac(q, proj[:, HOME[A_H] + q - 8, :])
                    upper(u4 + q)
                upper(u4 + 10)
                upper(u4 + 11)
                for ct in range(2):
                    act.wait_ge(*step(l, "vxc", ct + 1))
                    act.activation(proj[:, HOME[C_G] + ct, :], proj[:, HOME[B_V] + ct, :], ACT.Square).then_inc(s["lnb_sq"], 1)
                for ct in range(2):
                    act.wait_ge(*step(l, "lnc_xc", ct + 1))
                    act.activation(proj[:, HOME[A_H] + ct, :], outs[:, 4 + ct, :], ACT.Square).then_inc(s["lnc_sq"], 1)
                for q in (12, 13):
                    evac(q, proj[:, HOME[B_U] + q - 12, :])
                act.wait_ge(*step(l, "lnb_var", 1))
                root(2, stat[:], W, s["lnb_root"])
                act.wait_ge(*step(l, "lnc_var", 1))
                root(3, stat2[:], W, s["lnc_root"])
                for q in (14, 15):
                    evac(q, proj[:, HOME[A_B] + q - 14, :])
                for ct in range(2):
                    act.wait_ge(*step(l, "lnc_hat", ct + 1))
                    act.activation(outs[:, 4 + ct, :], outs[:, 4 + ct, :], ACT.Silu, bias=v_("ln_c_b", l, ct),
                                   scale=v_("ln_c_g", l, ct)).then_inc(s["gC"], 1)
                for q in range(12, 16):
                    upper(u4 + q)
                act.wait_ge(*step(l, "pj_done", 16))
                for i in range(6):
                    if i < 4:
                        g = GO[i]
                        for ct in range(2):
                            act.wait_ge(*step(l, READY[g], ct + 1))
                            act.activation(hT[:, 2 * g + ct, :], outs[:, 2 * g + ct, :], ACT.Square).then_inc(s["g_sq"], 1)
                    if 1 <= i <= 4:
                        act.wait_ge(*step(l, "g_sum", i))
                        if i >= 3:
                            act.wait_ge(*step(l, "merged", 2 * (i - 2)))
                        root((i + 1) % 4, (stat, stat2)[(i - 1) % 2][:], W, s["g_root"])
                    if i >= 2:
                        for ct in range(2):
                            act.wait_ge(*step(l, "merged", 2 * (i - 2) + ct + 1))
                            act.activation(r_(hT[:, 2 * GO[i - 2] + ct, :]), hlo[:, 2 * GO[i - 2] + ct, :], ACT.Copy).then_inc(s["m_hi"], 1)
                act.wait_ge(*step(l, "pool_free", 1))
                for n in range(7):
                    act.wait_ge(*step(l, "tail_tr", min(n // 2 * 2 + 2, 7)))
                    act.activation(outrow[0:TAIL[n], n, :], tail_bank(n)[0:TAIL[n]], ACT.Copy).then_inc(s["tail_copy"], 1)
                norm_act(2 * l + 1, l, SHIFT2, U_OUT[l] + UNIT_SLOTS)
                if l == 0:
                    act.wait_ge(*step(l, "tail_out", 16 * 8))
                    for h in range(2):
                        def upper_g(n):
                            act.wait_ge(ff_free, n + 1)
                            act.activation(r_(G[:, n % FH, :]), Glo[:, n % FH, :], ACT.Copy).then_inc(g_hi, 1)
                        for f in range(FH):
                            n = FH * h + f
                            act.wait_ge(ff_done, n + 1)
                            if n >= 2:
                                act.wait_ge(ff_free, n - 1)
                            act.activation(two(work[:, f % 2, :]), pp(2 * (f % 2)), ACT.Silu).then_inc(ff_act, 1)
                            if f:
                                upper_g(n - 1)
                            if f == FH - 1:
                                upper_g(n)
                            for w in range(2):
                                upper(U_FF(h, f, w) + UNIT_SLOTS)
                        if h == 0:
                            for q in range(KD):
                                upper(U_FY(h, q) + UNIT_SLOTS)

            act.wait_ge(R["lg"], 1)
            act.wait_ge(wr_in, 32)
            act.activation(two(lgT), PP[0][0:NE, :, 0:HT], ACT.Identity, bias=brt[:]).then_inc(R["lg_ev"], 1)
            for t in range(NT):
                n = min(P, T - P * t)
                act.wait_ge(R["h_tr"], t + 1)
                act.activation(hrow[t][0:n].rearrange("p (h n) -> p h n", h=2), PP[2 + t % 2][0:n], ACT.Copy).then_inc(R["h_row"], 1)
            act.wait_ge(R["exp_d"], 1)
            act.activation(gate[:, 1, :], gate[:, 0, :], ACT.Exp).then_inc(R["gate"], 1)
            act.dma_start(gf, A["g_final"].rearrange("(a n) -> a n", a=1).to_broadcast([P, D])).then_inc(gf_in, 16)
            for t in range(NT):
                act.wait_ge(Rout[t], 32)
            act.sem_inc(R["y_free"], 2)
            act.wait_ge(R["count"], 2)
            with act.Fori(0, NE) as e:
                c = tokens_of(act, e)
                with act.If(c <= NW):
                    for t in range(2):
                        act.wait_ge(R["in_tr"], NT * e + 2 * t + 3)
                        act.activation(hn[:, 4:8, P * t:P * t + P], PP[t][:, 1, :].rearrange("p (a n) -> p a n", a=4),
                                       ACT.Copy).then_inc(R["in_ev1"], 1)
                    for f in range(ET):
                        act.wait_ge(R["f_done"], ET * e + f + 1)
                        act.wait_ge(R["f_free"], ET * e + f + 1)
                        act.activation(hactn[:, f % 2, :], PP[0][:, f % 2, 0:NW], ACT.Silu).then_inc(R["f_act"], 1)
                    for q in range(KD):
                        act.wait_ge(R["y_done"], KD * e + q + 1)
                        act.activation(yn[:, q, :], PP[2][:, q % 2, 0:NW], ACT.Copy).then_inc(R["y_free"], 1)
                with act.Else():
                    act.sem_inc(R["in_ev1"], 2)
                    for f in range(ET):
                        act.wait_ge(R["f_done"], ET * e + f + 1)
                        act.wait_ge(R["f_free"], ET * e + f + 1)
                        act.activation(two(hact[:, f % 2, :]), pp(0), ACT.Silu).then_inc(R["f_act"], 1)
                    act.wait_ge(R["y_out"], 16 * NT * e + 16)
                    for q in range(KD):
                        act.wait_ge(R["y_done"], KD * e + q + 1)
                        act.activation(two(work[:, q, :]), pp(2), ACT.Copy).then_inc(R["y_free"], 1)
            for t in range(NT + 2):
                if t < NT:
                    n = min(P, T - P * t)
                    act.wait_ge(Rback[t][0], 16)
                    act.activation(yg[0:n, t, 0, :], yg[0:n, t, 0, :], ACT.Copy, scale=gate[0:n, 0, t:t + 1]).then_inc(R["ya"], 1)
                if 1 <= t <= NT:
                    n = min(P, T - P * (t - 1))
                    act.wait_ge(R["x_ev"], t)
                    act.activation(yg[0:n, t - 1, 0, :], yg[0:n, t - 1, 1, :], ACT.Square,
                                   accum_out=ss[0:n, t - 1:t]).then_inc(R["ss"], 1)
                    act.wait_ge(R["ss"], t)
                    act.activation(ss[0:n, t - 1:t], ss[0:n, t - 1:t], ACT.Sqrt, bias=eps[0:n], scale=1.0 / D).then_inc(R["ssr"], 1)
                if t >= 2:
                    n, a = min(P, T - P * (t - 2)), yg[0:min(P, T - P * (t - 2)), t - 2, 1, :]
                    act.wait_ge(R["rr"], t - 1)
                    act.activation(a, a, ACT.Copy, scale=ss[0:n, t - 2:t - 1]).then_inc(R["scaled"], 1)

        @block.vector
        def _(dve):
            order = [0]

            def done(ins):
                order[0] += 1
                ins.then_inc(dchain, 1)
                return order[0]

            def link(ins):
                dve.wait_ge(dchain, done(ins))

            dve.memset(eps[:], EPS)
            dve.memset(ones[:], 1.0).then_inc(const_dve, 1)
            for ct in range(2):
                dve.memset(win[0:64, ct:ct + 1], float((2, 8)[ct]))
                last = dve.memset(win[64:P, ct:ct + 1], float((4, 16)[ct]))
            link(last)
            dve.wait_ge(const_ready, 2)
            dve.reciprocal(winv[:], win[:])
            for ct in range(2):
                last = dve.tensor_scalar(cinv[:, ct, :], cinv[:, ct, :], win[:, ct:ct + 1], None, ALU.min)
            link(last)
            link(dve.reciprocal(cinv[:], cinv[:]))
            dve.wait_ge(pro_tr, 1)
            cps = PP[3][:, 0, 0:KD * NQ].rearrange("p (k q) -> p k q", k=KD)
            link(dve.tensor_copy(r_(cs[:, :, 0:NQ]), cps))
            dve.tensor_tensor(r_(cs[:, :, NQ:2 * NQ]), cps, read_(cs[:, :, 0:NQ]), ALU.subtract).then_inc(pro_dve, 1)
            dve.wait_ge(pro_tr, 2)
            dve.tensor_copy(bada[:], PP[2][:, 1, 0:96]).then_inc(pro_dve, 1)
            for l in range(DEPTH):
                with dve.Fori(0, NA) as i:
                    for j in range(ADA_RING):
                        dve.wait_ge(ada_hi, 24 * l + ADA_RING * i + j + 1)
                        dve.tensor_tensor(r_(ada_slot(j)), ada_slot(j), read_(ahi[:, j % 3]), ALU.subtract).then_inc(ada_lo, 1)
                if l == 0:
                    dve.wait_ge(pro_tr, 3)
                    dve.tensor_copy(vec[:], PP[3][:, 0, 0:DEPTH * NROWS].rearrange("p (l n) -> p l n", l=DEPTH)).then_inc(pro_dve, 1)
                    for j in range(0, KD, 2):
                        dve.wait_ge(pro_tr, 4 + j)
                        dve.tensor_copy(xT[:, j, 0:SEQ], PP[2][:, 0, :]).then_inc(pro_dve, 1)
                    dve.wait_ge(pro_tr, 12)
                    dve.tensor_copy(xT[:, :, SEQ:T], PP[3][:, 1, 0:KD * NS].rearrange("p (k q) -> p k q", k=KD)).then_inc(pro_dve, 1)
                    dve.wait_ge(pro_dve, 8)
                    dve.sem_inc(ns["up"], KD)
            dve.wait_ge(pro_dve, 3)
            dve.wait_ge(ada_out, 1 + 2 * NA * DEPTH)
            link(dve.tensor_tensor(mod[:], mod[:], mod_lo, ALU.add))
            dve.sem_inc(R["mods"], 1)
            for l in range(DEPTH):
                for sec, g in ((SCALE1, "g_mix"), (SCALE2, "g_ffn")):
                    a = mod[:, l, 8 * sec:8 * sec + 8, :]
                    gv = vec[:, l, ROWS[g][0]:ROWS[g][0] + 8]
                    last = dve.scalar_tensor_tensor(a, a, 1.0, gv.unsqueeze(2).to_broadcast([P, 8, NQ]), ALU.add, ALU.mult)
            link(last)

            def norm_dve(tag, l, scale, shift):
                dve.wait_ge(*norm_step(tag, "root", 1))
                dve.reciprocal(stat[:], stat[:]).then_inc(ns["rec"], 1)
                dve.wait_ge(*norm_step(tag, "rec", 1))
                split = tag < 3
                dst = hlo if split else hT

                def lower(j):
                    a = hlo[:, j, 0:SEQ]
                    dve.wait_ge(*norm_step(tag, "hi", j + 1))
                    dve.scalar_tensor_tensor(r_(a), a, mod[:, l, 8 * shift + j, 0:1], read_(hT[:, j, 0:SEQ]), ALU.add,
                                             ALU.subtract).then_inc(ns["h"], 1)

                for j in range(KD):
                    dve.scalar_tensor_tensor(dst[:, j, 0:SEQ], xT[:, j, 0:SEQ], mod[:, l, 8 * scale + j, 0:1], stat[:, 0:SEQ],
                                             ALU.mult, ALU.mult).then_inc(ns["xhat"], 1)
                    if j and split:
                        lower(j - 1)
                if split:
                    lower(KD - 1)

            def add_gated(l, sec, q, pair, free, up):
                g = mod[:, l, 8 * sec + q, :]
                c = done(dve.tensor_tensor(small[:, q % 2, :], PP[pair][:, 1, HT - NS:HT], g[:, 1:NQ], ALU.mult))
                dve.scalar_tensor_tensor(xT[:, q, 0:HT], PP[pair][:, 0, 0:HT], g[:, 0:1], xT[:, q, 0:HT], ALU.mult, ALU.add)
                dve.scalar_tensor_tensor(xT[:, q, HT:SEQ], PP[pair][:, 1, 0:HT - NS], g[:, 0:1], xT[:, q, HT:SEQ],
                                         ALU.mult, ALU.add).then_inc(free, 1)
                dve.wait_ge(dchain, c)
                dve.tensor_tensor(xT[:, q, SEQ:T], xT[:, q, SEQ:T], small[:, q % 2, :], ALU.add).then_inc(up, 1)

            for l in range(DEPTH):
                dve.wait_ge(*step(l, "ws_tr", 1))
                dve.tensor_copy(wsT, PP[3][:, 0, :].rearrange("p (h t) -> p h t", h=4)).then_inc(s["ws_copy"], 1)
                dve.wait_ge(*step(l, "st_tr", 1))
                for dst, src, r in ((hisA, PP[3][:, 1, 0:32], 2), (hisC, PP[3][:, 1, 32:512], 30),
                                    (hisD, PP[0][:, 0, 0:240], 15)):
                    for ct in range(2):
                        m = NS * r
                        last = dve.tensor_copy(dst[:, ct, :, 0:r], src[:, ct * m:ct * m + m].rearrange("p (b r) -> p b r", r=r))
                    last.then_inc(s["st_copy"], 1)
                norm_dve(2 * l, l, SCALE1, SHIFT1)
                dve.wait_ge(*step(l, "hist_zero", 1))
                for q in (2, 3):
                    dve.wait_ge(*step(l, "pj_done", q + 1))
                    dve.wait_ge(*step(l, f"pj_free{q % 2}", 1))
                    dve.tensor_tensor(two(gin[:, q - 2, 30:30 + T]), pp(q % 2), two(proj[:, HOME[C_G] + q - 2, :]),
                                      ALU.mult).then_inc(s[f"pj_free{q % 2}"], 1)
                dve.wait_ge(*step(l, "pj_free0", 2))
                dve.wait_ge(*step(l, "pj_free1", 2))
                for ct in range(2):
                    last = dve.tensor_copy(hisC[:, ct, :, 30], gin[:, ct, SEQ + 30:SEQ + 38])
                link(last)

                def tap(name, k, ct):
                    return v_(name, l, 2 * k + ct)

                def taps(name, n, ct):
                    r0 = ROWS[name][0]
                    w = vec[:, l, r0:r0 + 2 * n].rearrange("p (k c) -> p c k", c=2)[:, ct]
                    return w.unsqueeze(1).to_broadcast([P, NS, n])

                for k in range(TAPS_C):
                    for ct in range(2):
                        acc = outs[:, 4 + ct, 0:SEQ]
                        if k == 0:
                            dve.tensor_scalar(acc, gin[:, ct, 0:SEQ], tap("conv_c_w", 0, ct), v_("conv_c_b", l, ct),
                                              ALU.mult, ALU.add).then_inc(s["conv_tap"], 1)
                        else:
                            dve.wait_ge(*step(l, "conv_tap", 2 * k + ct - 1))
                            dve.scalar_tensor_tensor(acc, gin[:, ct, k:k + SEQ], tap("conv_c_w", k, ct), acc,
                                                     ALU.mult, ALU.add).then_inc(s["conv_tap"], 1)
                for ct in range(2):
                    o = outs[:, 4 + ct, SEQ:T]
                    link(dve.tensor_tensor(tapC[:], hisC[:, ct], taps("conv_c_w", TAPS_C, ct), ALU.mult))
                    link(dve.tensor_reduce(o, tapC[:], AX.X, ALU.add))
                    last = dve.tensor_scalar(o, o, v_("conv_c_b", l, ct), None, ALU.add)
                last.then_inc(s["lnc_in"], 1)
                for q in (10, 11):
                    dve.wait_ge(*step(l, "pj_done", q + 1))
                    dve.wait_ge(*step(l, f"pj_free{q % 2}", 5))
                    dve.tensor_tensor(two(zin[:, q - 10, 2:2 + T]), pp(q % 2), two(proj[:, HOME[A_H] + q - 10, :]),
                                      ALU.mult).then_inc(s[f"pj_free{q % 2}"], 1)
                for q, tiles, sums, xc in ((2, [proj[:, HOME[B_V] + ct, :] for ct in range(2)], "lnb_sum", "vxc"),
                                           (3, [outs[:, 4 + ct, :] for ct in range(2)], "lnc_sum", "lnc_xc")):
                    dve.wait_ge(*step(l, sums, 1))
                    for ct in range(2):
                        dve.scalar_tensor_tensor(two(tiles[ct]), pp(q), -1.0 / W, two(tiles[ct]), ALU.mult,
                                                 ALU.add).then_inc(s[xc], 1)
                dve.wait_ge(*step(l, "pj_free0", 6))
                dve.wait_ge(*step(l, "pj_free1", 6))
                for ct in range(2):
                    last = dve.tensor_copy(hisA[:, ct, :, 2], zin[:, ct, SEQ + 2:SEQ + 10])
                link(last)
                for ct in range(2):
                    acc = outs[:, ct, 0:SEQ]
                    link(dve.tensor_scalar(acc, zin[:, ct, 0:SEQ], tap("conv_a_w", 0, ct), None, ALU.mult))
                    for k in (1, 2):
                        link(dve.scalar_tensor_tensor(acc, zin[:, ct, k:k + SEQ], tap("conv_a_w", k, ct), acc, ALU.mult, ALU.add))
                    link(dve.tensor_tensor(tapC[:, :, 0:TAPS_A], hisA[:, ct], taps("conv_a_w", TAPS_A, ct), ALU.mult))
                    link(dve.tensor_reduce(outs[:, ct, SEQ:T], tapC[:, :, 0:TAPS_A], AX.X, ALU.add))
                for ct in range(2):
                    last = dve.tensor_copy(hisD[:, ct, :, 15], pin[:, ct, SEQ + 15:SEQ + 23])
                link(last)
                for ct in range(2):
                    for r, w in ((slice(0, 64), (2, 8)[ct]), (slice(64, P), (4, 16)[ct])):
                        last = dve.tensor_reduce(outs[r, 6 + ct, SEQ:T], hisD[r, ct, :, POOL - w:POOL], AX.X, ALU.add)
                dve.wait_ge(*step(l, "pool_out", 1))
                link(last)
                link(dve.tensor_tensor(head16[:], outs[:, 6:8, 0:POOL], cinv[:], ALU.mult))
                for ct in range(2):
                    last = dve.scalar_tensor_tensor(outs[:, 6 + ct, :], outs[:, 6 + ct, :], winv[:, ct:ct + 1],
                                                    pin[:, ct, 15:15 + T], ALU.mult, ALU.subtract)
                link(last)
                dve.tensor_tensor(outs[:, 6:8, 0:POOL], head16[:], pin[:, :, 15:15 + POOL], ALU.subtract).then_inc(s["pooled"], 1)
                dve.wait_ge(*step(l, "lnb_root", 1))
                link(dve.reciprocal(stat[:], stat[:]))
                for ct in range(2):
                    v = proj[:, HOME[B_V] + ct, :]
                    link(dve.tensor_tensor(v, v, stat[:], ALU.mult))
                    dve.tensor_scalar(v, v, v_("ln_v_g", l, ct), v_("ln_v_b", l, ct), ALU.mult, ALU.add).then_inc(s["vn_ready"], 1)
                dve.wait_ge(*step(l, "lnc_root", 1))
                link(dve.reciprocal(stat2[:], stat2[:]))
                for ct in range(2):
                    o = outs[:, 4 + ct, :]
                    dve.tensor_tensor(o, o, stat2[:], ALU.mult).then_inc(s["lnc_hat"], 1)
                dve.wait_ge(*step(l, "pj_free0", 8))
                dve.wait_ge(*step(l, "pj_free1", 8))
                for ct in range(2):
                    dve.tensor_tensor(outs[:, ct, :], outs[:, ct, :], proj[:, HOME[A_B] + ct, :], ALU.mult).then_inc(s["gA"], 1)
                dve.wait_ge(*step(l, "vt_tr", 1))
                dve.wait_ge(*step(l, "lnc_sq", 2))
                dve.tensor_copy(vtok.rearrange("p (h a) w -> p h (a w)", h=2), PP[3][:]).then_inc(s["vt_copy"], 1)
                dve.wait_ge(*step(l, "vn_ready", 2))
                for ct in range(2):
                    last = dve.tensor_scalar(outs[:, 2 + ct, SEQ:T], proj[:, HOME[B_V] + ct, SEQ:T], ws00[:, ct:ct + 1],
                                             bsb[:, ct, 0:1], ALU.mult, ALU.add)
                dve.wait_ge(*step(l, "mix_done", 1))
                for r in range(2):
                    rr = slice(64 * r, 64 * r + 64)
                    for ct in range(2):
                        for h in range(2):
                            last = dve.tensor_tensor(outs[rr, 2 + ct, 256 * h:256 * h + 256].rearrange("p (n t) -> p n t", n=2),
                                                     PP[h][rr, :, ct * 256 + r * P:ct * 256 + r * P + P],
                                                     bsb[rr, ct:ct + 1, :].to_broadcast([64, 2, P]), ALU.add)
                last.then_inc(s["mix_read"], 1)
                dve.wait_ge(*step(l, "mix_read", 1))
                for ct in range(2):
                    dve.tensor_tensor(outs[:, 2 + ct, :], outs[:, 2 + ct, :], proj[:, HOME[B_U] + ct, :], ALU.mult).then_inc(s["gB"], 1)
                for ct in range(2):
                    dve.wait_ge(*step(l, "pool_mm", ct + 1))
                    dve.tensor_scalar(two(outs[:, 6 + ct, :]), pp(2 + ct), v_("pool_scale", l, ct), None, ALU.mult).then_inc(s["gD"], 1)
                dve.sem_inc(s["pool_free"], 1)
                for i, g in enumerate(GO):
                    st = (stat, stat2)[i % 2]
                    dve.wait_ge(*step(l, "g_root", i + 1))
                    link(dve.reciprocal(st[:], st[:]))
                    for ct in range(2):
                        j = 2 * g + ct
                        dve.scalar_tensor_tensor(hlo[:, j, :], outs[:, j, :], v_("g_out", l, j), st[:], ALU.mult,
                                                 ALU.mult).then_inc(s["merged"], 1)
                for q in range(KD):
                    dve.wait_ge(*step(l, "po_done", q + 1))
                    add_gated(l, GATE1, q, q % 2, s["po_free"], ns["up"])
                norm_dve(2 * l + 1, l, SCALE2, SHIFT2)
                if l == 0:
                    dve.wait_ge(*step(l, "tail_out", 16 * 8))
                    def lower_g(n):
                        a = Glo[:, n % FH, :]
                        dve.wait_ge(g_hi, n + 1)
                        dve.tensor_tensor(r_(a), a, read_(G[:, n % FH, :]), ALU.subtract).then_inc(g_lo, 1)
                    for h in range(2):
                        for f in range(FH):
                            dve.wait_ge(ff_act, FH * h + f + 1)
                            dve.tensor_tensor(two(Glo[:, f, :]), pp(2 * (f % 2) + 1), two(work[:, f % 2, :]), ALU.mult).then_inc(ff_free, 1)
                            if f:
                                lower_g(FH * h + f - 1)
                        lower_g(FH * h + FH - 1)
                        for q in range(KD):
                            dve.wait_ge(fy_done, KD * h + q + 1)
                            if h:
                                dve.wait_ge(x_half, q + 1)
                            add_gated(l, GATE2, q, YB[q % 3], fy_free, ns["up"] if h else x_half)

            link(dve.memset(lg[:], 0.0))
            dve.wait_ge(R["lg_tr"], 1)
            dve.tensor_copy(lg[:, 0:4, :], PP[1][:, 0, 0:4 * NE].rearrange("p (t e) -> p t e", t=4))
            link(dve.tensor_copy(lg[0:NS, 4, :], PP[1][0:NS, 0, 4 * NE:5 * NE]))
            for t in range(NT):
                last = dve.max(vmax[:, t, :], lg[:, t, :])
            link(last)
            for t in range(NT):
                last = dve.max_index(imax[:, t, :], vmax[:, t, :], lg[:, t, :])
            dve.tensor_tensor(gate[:, 0, :], vmax[:, :, 1], vmax[:, :, 0], ALU.subtract).then_inc(R["exp_d"], 1)
            link(last)
            link(dve.tensor_copy(imf[:], imax[:]))
            dve.wait_ge(R["const"], 3)
            for r in range(2):
                for t in range(NT):
                    last = dve.tensor_scalar(pick[:, r, t, :], eidx[:], imf[:, t, r:r + 1], valid[:, t:t + 1],
                                             ALU.is_equal, ALU.mult)
            link(last)
            dve.tensor_tensor(mask[:], pick[:, 0], pick[:, 1], ALU.add).then_inc(R["mask"], 1)
            dve.wait_ge(R["pre"], 1)
            dve.tensor_copy(before[:], PP[0][:, 0, 0:NT * NE].rearrange("p (t e) -> p t e", t=NT))
            dve.tensor_copy(totals[:, 1:NT, :], PP[0][:, 1, 0:(NT - 1) * NE].rearrange("p (t e) -> p t e", t=NT - 1))
            link(dve.tensor_reduce(countf[:], PP[0][:, 1, 0:NT * NE].rearrange("p (t e) -> p e t", t=NT), AX.X, ALU.add))
            dve.tensor_copy(count[:], countf[:]).then_inc(R["count"], 1)
            for e in range(1, NE):
                link(dve.tensor_tensor(ebase[:, e:e + 1], ebase[:, e - 1:e], countf[:, e - 1:e], ALU.add))
            dve.tensor_copy(first[:], ebase[:]).then_inc(R["count"], 1)
            link(dve.tensor_copy(totals[:, 0, :], ebase[:]))
            for t in range(1, NT):
                link(dve.tensor_tensor(totals[:, t, :], totals[:, t, :], totals[:, t - 1, :], ALU.add))
            link(dve.tensor_tensor(before[:], before[:], totals[:], ALU.add))
            for r in range(2):
                last = dve.tensor_tensor(pick[:, r], pick[:, r], before[:], ALU.mult)
            link(last)
            link(dve.tensor_reduce(placef[:], pick[:], AX.X, ALU.add))
            dve.tensor_copy(place[:], placef[:]).then_inc(R["route"], 1)
            dve.wait_ge(R["gate"], 1)
            link(dve.tensor_scalar(gate[:, 0, :], gate[:, 1, :], 1.0, None, ALU.add))
            link(dve.reciprocal(gate[:, 0, :], gate[:, 0, :]))
            link(dve.tensor_tensor(gate[:, 1, :], gate[:, 1, :], gate[:, 0, :], ALU.mult))
            dve.wait_ge(*step(1, "tail_out", 16 * 8))
            for t in range(NT):
                dve.wait_ge(Rout[t], 32)
            dve.sem_inc(R["yt_ev"], 1)
            dve.sem_inc(R["f_free"], 2)
            dve.sem_inc(R["y_out"], 16)
            dve.wait_ge(R["count"], 2)
            with dve.Fori(0, NE) as e:
                c = tokens_of(dve, e)
                with dve.If(c <= NW):
                    dve.sem_inc(R["in_ev"], 3)
                    for t in range(2):
                        dve.wait_ge(R["in_tr"], NT * e + 2 * t + 2)
                        dve.tensor_copy(hn[:, 0:4, P * t:P * t + P],
                                        PP[t][:, 0, :].rearrange("p (a n) -> p a n", a=4)).then_inc(R["in_ev"], 1)
                    for f in range(ET):
                        dve.wait_ge(R["f_act"], ET * e + f + 1)
                        if f == 0:
                            dve.sem_inc(R["yt_ev"], 1)
                        dve.tensor_tensor(Gn[:, f, :], PP[1][:, f % 2, 0:NW], hactn[:, f % 2, :], ALU.mult).then_inc(R["f_free"], 1)
                    dve.wait_ge(R["y_out"], 16 * NT * e + 16)
                    for h in range(2):
                        dve.wait_ge(R["yt_tr"], NT * e + h + 4)
                        for t in range(2):
                            dve.tensor_copy(yrow[:, t, 4 * P * h:4 * P * h + 4 * P], PP[3][:, t, :]).then_inc(R["yt_ev"], 1)
                with dve.Else():
                    for t in range(NT):
                        dve.wait_ge(R["in_tr"], NT * e + t + 1)
                        dve.tensor_copy(hexp[:, :, AT[t]:AT[t] + P].rearrange("p (h a) n -> p h a n", h=2),
                                        PP[3][:].rearrange("p h (a n) -> p h a n", a=4)).then_inc(R["in_ev"], 1)
                    for f in range(ET):
                        dve.wait_ge(R["f_act"], ET * e + f + 1)
                        dve.tensor_tensor(two(G[:, f, :]), pp(1), two(hact[:, f % 2, :]), ALU.mult).then_inc(R["f_free"], 1)
                    for t in range(NT):
                        dve.wait_ge(R["yt_tr"], NT * e + t + 1)
                        dve.wait_ge(R["y_out"], 16 * (NT * e + t) + 16)
                        dve.tensor_copy(stage[:, 2, :].rearrange("p (h n) -> p h n", h=2), PP[3][:]).then_inc(R["yt_ev"], 1)
            for j in range(KD):
                last = dve.tensor_scalar(diag[:, j * P:(j + 1) * P], ident[:], mod[:, 1, 8 * GATE2 + j, 0:1], None, ALU.mult)
            last.then_inc(R["diag"], 1)
            for i, (g, n) in enumerate(((gate_p, P), (gate_s, NS))):
                dve.wait_ge(R["g_mm"], i + 1)
                c = done(dve.tensor_copy(g[0:n].rearrange("p (h n) -> p h n", h=2), PP[i][0:n]))
                dve.wait_ge(dchain, c)
                dve.sem_inc(R["g_ev"], 1)
            for t in range(NT + 1):
                if t < NT:
                    n = min(P, T - P * t)
                    a = yg[0:n, t, 1, :]
                    dve.wait_ge(R["ya"], t + 1)
                    dve.wait_ge(Rback[t][1], 16)
                    link(dve.scalar_tensor_tensor(a, a, gate[0:n, 1, t:t + 1], yg[0:n, t, 0, :], ALU.mult, ALU.add))
                    link(dve.tensor_tensor(a, a, (gate_p if t < 4 else gate_s)[0:n], ALU.mult))
                    dve.wait_ge(R["x_tr"], t + 1)
                    dve.tensor_tensor(a.rearrange("p (h n) -> p h n", h=2), a.rearrange("p (h n) -> p h n", h=2), PP[XB[t]][0:n],
                                      ALU.add).then_inc(R["x_ev"], 1)
                if t:
                    n = min(P, T - P * (t - 1))
                    dve.wait_ge(R["ssr"], t)
                    dve.reciprocal(ss[0:n, t - 1:t], ss[0:n, t - 1:t]).then_inc(R["rr"], 1)


_INS = ["x_prompt", "x_sample", "state_conv_a", "state_conv_c", "state_pool_d", "c_prompt", "c_sample", "w_ada", "b_ada",
        "g_mix", "w_in", "conv_a_w", "ln_v_g", "ln_v_b", "w_s", "b_s", "conv_c_w", "conv_c_b", "ln_c_g", "ln_c_b",
        "pool_w", "pool_scale", "g_out", "w_out", "g_ffn", "w1_dense", "w3_dense", "w2_dense", "w_router", "b_router",
        "w1_moe", "w3_moe", "w2_moe", "g_final"]
_OUTS = [("y_prompt", (1, SEQ, D)), ("y_sample", (NS, 1, D)),
         ("a_p", (DEPTH, 1, 2, W)), ("c_p", (DEPTH, 1, 30, W)), ("d_p", (DEPTH, 1, 15, W)), ("v_p", (DEPTH, 1, P, W)),
         ("a_s", (DEPTH, NS, 2, W)), ("c_s", (DEPTH, NS, 30, W)), ("d_s", (DEPTH, NS, 15, W)), ("v_s", (DEPTH, NS, 1, W))]


def kernel(**inputs):
    import numpy as _np
    import concourse.bacc as _bacc
    from concourse.bass_utils import run_bass_kernel_spmd as _run

    nc = _bacc.Bacc("TRN2", target_bir_lowering=False, num_devices=1)
    arrays, A, O = {}, {}, {}
    for name in _INS:
        a = _np.ascontiguousarray(inputs[name])
        arrays[f"in_{name}"] = a
        A[name] = nc.dram_tensor(f"in_{name}", a.shape, F32, kind="ExternalInput").ap()
    for name, shape in _OUTS:
        O[name] = nc.dram_tensor(f"out_{name}", shape, F32, kind="ExternalOutput").ap()
    trunk_program(nc, A, O)
    r = _run(nc, [arrays], core_ids=[0])
    return tuple(r.results[0][f"out_{name}"] for name, _ in _OUTS)
```
